# Optimizing a Trainium2 kernel written in Bass

```python
import jax
import jax.numpy as jnp
from jax import lax
import numpy as np
import math
import jax, jax.numpy as jnp

D_MODEL = 1024
BATCH = 1
SEQ = 256
DEPTH = 2

CHUNK = 64
D_PLE = 256
N_EVEN = (DEPTH + 1) // 2
N_ODD = DEPTH // 2
D_FF = 2816
A_HEADS = 8
A_KV_HEADS = 2
A_GROUP = A_HEADS // A_KV_HEADS
A_HEAD_DIM = 64
A_WIDTH = A_HEADS * A_HEAD_DIM
A_KV_WIDTH = A_KV_HEADS * A_HEAD_DIM
A_WINDOW = 128
A_PREV_CHUNKS = A_WINDOW // CHUNK
B_WIDTH = 512
B_BLOCKS = 8
B_BLOCK = B_WIDTH // B_BLOCKS
B_CONV = 4
RG_C = 8.0
AB_PROJ = A_WIDTH + 2 * A_KV_WIDTH + 2 * B_WIDTH
C_HEADS = 8
C_HEAD_DIM = 128
C_WIDTH = C_HEADS * C_HEAD_DIM
C_CONV = 4
C_PROJ = 4 * C_WIDTH + 2 * C_HEADS
DN_ALPHA = (2.0 * DEPTH) ** 0.25
DN_BETA = (8.0 * DEPTH) ** -0.25
LN_EPS = 1e-5
NORM_EPS = 1e-6
NEG = -1e30


def layer_norm(x, g, b):
    xf = x.astype(jnp.float32)
    mu = jnp.mean(xf, -1, keepdims=True)
    var = jnp.mean(jnp.square(xf - mu), -1, keepdims=True)
    return ((xf - mu) * lax.rsqrt(var + LN_EPS) * g + b).astype(x.dtype)

def swiglu(x, wg, wu, wd):
    return (jax.nn.silu(x @ wg) * (x @ wu)) @ wd

def causal_dwconv(x, w):
    k, s = w.shape[0], x.shape[1]
    xp = jnp.pad(x, ((0, 0), (k - 1, 0), (0, 0)))
    y = xp[:, 0:s] * w[0]
    for j in range(1, k):
        y = y + xp[:, j:j + s] * w[j]
    return y

def chunk_band(t, n_prev):
    b, s = t.shape[:2]
    nc = s // CHUNK
    pad = n_prev * CHUNK
    tp = jnp.pad(t, ((0, 0), (pad, 0), (0, 0), (0, 0)))
    return jnp.concatenate(
        [tp[:, j * CHUNK:j * CHUNK + s].reshape(b, nc, CHUNK, *t.shape[2:]) for j in range(n_prev + 1)],
        axis=2)

def alibi_slopes(n):
    return 2.0 ** (-8.0 * jnp.arange(1, n + 1, dtype=jnp.float32) / n)

def sliding_window_sink_attention(q, k, v, sinks):
    b, s = q.shape[:2]
    nc = s // CHUNK
    pad = A_PREV_CHUNKS * CHUNK
    nk = pad + CHUNK
    qb = q.reshape(b, nc, CHUNK, A_KV_HEADS, A_GROUP, A_HEAD_DIM)
    kb = chunk_band(k, A_PREV_CHUNKS)
    vb = chunk_band(v, A_PREV_CHUNKS)
    sc = jnp.einsum('bnckgd,bnskd->bnkgcs', qb, kb).astype(jnp.float32) * (A_HEAD_DIM ** -0.5)
    dist = jnp.abs(jnp.arange(CHUNK)[:, None] + pad - jnp.arange(nk)[None, :]).astype(jnp.float32)
    slopes = alibi_slopes(A_HEADS).reshape(A_KV_HEADS, A_GROUP)
    valid = (jnp.arange(nc)[:, None] * CHUNK + jnp.arange(nk)[None, :] - pad) >= 0
    sc = sc - slopes[:, :, None, None] * dist
    sc = jnp.where(valid[None, :, None, None, None, :], sc, NEG)
    sink = sinks.astype(jnp.float32).reshape(A_KV_HEADS, A_GROUP)[:, :, None]
    m = jnp.maximum(sc.max(-1), sink)
    pr = jnp.exp(sc - m[..., None])
    den = pr.sum(-1) + jnp.exp(sink - m)
    o = jnp.einsum('bnkgcs,bnskd->bnckgd', pr / den[..., None], vb.astype(jnp.float32))
    return o.reshape(b, s, A_WIDTH).astype(q.dtype)

def rg_lru(x, w_a, b_a, w_x, b_x, lam):
    xb = x.reshape(*x.shape[:2], B_BLOCKS, B_BLOCK)
    r = jax.nn.sigmoid(jnp.einsum('bshi,hij->bshj', xb, w_a).reshape(x.shape) + b_a)
    i = jax.nn.sigmoid(jnp.einsum('bshi,hij->bshj', xb, w_x).reshape(x.shape) + b_x)
    log_a = (-RG_C * r * jax.nn.softplus(-lam)).astype(jnp.float32)
    a = jnp.exp(log_a)
    u = jnp.sqrt(-jnp.expm1(2.0 * log_a)) * (i * x).astype(jnp.float32)

    def combine(c1, c2):
        a1, b1 = c1
        a2, b2 = c2
        return a1 * a2, a2 * b1 + b2

    _, h = lax.associative_scan(combine, (a, u), axis=1)
    return h.astype(x.dtype)

def mixer_ab(x, w_in, sinks, conv_w, conv_b, w_a, b_a, w_x, b_x, lam, w_out):
    b, s = x.shape[:2]
    proj = x @ w_in
    o1 = A_WIDTH
    o2 = o1 + A_KV_WIDTH
    o3 = o2 + A_KV_WIDTH
    o4 = o3 + B_WIDTH
    q = proj[..., :o1].reshape(b, s, A_HEADS, A_HEAD_DIM)
    k = proj[..., o1:o2].reshape(b, s, A_KV_HEADS, A_HEAD_DIM)
    v = proj[..., o2:o3].reshape(b, s, A_KV_HEADS, A_HEAD_DIM)
    bx = proj[..., o3:o4]
    bg = proj[..., o4:]
    ya = sliding_window_sink_attention(q, k, v, sinks)
    bx = causal_dwconv(bx, conv_w) + conv_b
    yb = rg_lru(bx, w_a, b_a, w_x, b_x, lam) * jax.nn.gelu(bg)
    return jnp.concatenate([ya, yb], axis=-1) @ w_out

def gated_delta_rule(q, k, v, g, beta):
    f32 = jnp.float32
    b, s, h, dk = q.shape
    dv = v.shape[-1]
    nc = s // CHUNK

    def to_chunks(t):
        return t.astype(f32).reshape(b, nc, CHUNK, h, -1).transpose(1, 0, 3, 2, 4)

    q = to_chunks(q) * (dk ** -0.5)
    k = to_chunks(k)
    v = to_chunks(v)
    g = g.astype(f32).reshape(b, nc, CHUNK, h).transpose(1, 0, 3, 2)
    beta = beta.astype(f32).reshape(b, nc, CHUNK, h).transpose(1, 0, 3, 2)
    gc = jnp.cumsum(g, axis=-1)
    tril = jnp.tril(jnp.ones((CHUNK, CHUNK), bool))
    strict = jnp.tril(jnp.ones((CHUNK, CHUNK), bool), -1)
    diff = gc[..., :, None] - gc[..., None, :]
    decay = jnp.where(tril, jnp.exp(jnp.where(tril, diff, 0.0)), 0.0)
    kb = k * beta[..., None]
    lmat = jnp.where(strict, jnp.einsum('nbhid,nbhjd->nbhij', kb, k) * decay, 0.0)
    amat = lmat + jnp.eye(CHUNK, dtype=f32)
    u = lax.linalg.triangular_solve(amat, v * beta[..., None], left_side=True, lower=True, unit_diagonal=True)
    w = lax.linalg.triangular_solve(amat, kb * jnp.exp(gc)[..., None], left_side=True, lower=True, unit_diagonal=True)
    attn = jnp.einsum('nbhid,nbhjd->nbhij', q, k) * decay
    qg = q * jnp.exp(gc)[..., None]
    kdec = k * jnp.exp(gc[..., -1:] - gc)[..., None]
    glast = jnp.exp(gc[..., -1])

    def step(state, xs):
        qg_n, kdec_n, w_n, u_n, attn_n, gl_n = xs
        v_new = u_n - jnp.einsum('bhcd,bhde->bhce', w_n, state)
        o = jnp.einsum('bhcd,bhde->bhce', qg_n, state) + jnp.einsum('bhij,bhje->bhie', attn_n, v_new)
        state = state * gl_n[..., None, None] + jnp.einsum('bhcd,bhce->bhde', kdec_n, v_new)
        return state, o

    s0 = jnp.zeros((b, h, dk, dv), f32)
    _, o = lax.scan(step, s0, (qg, kdec, w, u, attn, glast))
    return o.transpose(1, 0, 3, 2, 4).reshape(b, s, h, dv)

def mixer_c(x, w_in, conv_w, a_log, dt_bias, norm_g, w_out):
    b, s = x.shape[:2]
    proj = x @ w_in
    qkv = jax.nn.silu(causal_dwconv(proj[..., :3 * C_WIDTH], conv_w))
    z = proj[..., 3 * C_WIDTH:4 * C_WIDTH].reshape(b, s, C_HEADS, C_HEAD_DIM)
    b_logit = proj[..., 4 * C_WIDTH:4 * C_WIDTH + C_HEADS]
    a_in = proj[..., 4 * C_WIDTH + C_HEADS:]
    q = qkv[..., :C_WIDTH].reshape(b, s, C_HEADS, C_HEAD_DIM).astype(jnp.float32)
    k = qkv[..., C_WIDTH:2 * C_WIDTH].reshape(b, s, C_HEADS, C_HEAD_DIM).astype(jnp.float32)
    v = qkv[..., 2 * C_WIDTH:].reshape(b, s, C_HEADS, C_HEAD_DIM)
    q = q * lax.rsqrt(jnp.sum(q * q, -1, keepdims=True) + NORM_EPS)
    k = k * lax.rsqrt(jnp.sum(k * k, -1, keepdims=True) + NORM_EPS)
    beta = jax.nn.sigmoid(b_logit.astype(jnp.float32))
    g = -jnp.exp(a_log.astype(jnp.float32)) * jax.nn.softplus((a_in + dt_bias).astype(jnp.float32))
    o = gated_delta_rule(q, k, v, g, beta)
    o = o * lax.rsqrt(jnp.mean(o * o, -1, keepdims=True) + NORM_EPS) * norm_g
    o = (o * jax.nn.silu(z.astype(jnp.float32))).astype(x.dtype)
    return o.reshape(b, s, C_WIDTH) @ w_out

def first_inputs(seed: int = 0) -> dict:
    key = jax.random.key(seed)
    ks = iter(jax.random.split(key, 48))
    f32 = jnp.float32

    def nrm(shape, scale):
        return jax.random.normal(next(ks), shape, f32) * scale

    d = D_MODEL
    x = nrm((BATCH, SEQ, d), 1.0)
    p = nrm((DEPTH, BATCH, SEQ, D_PLE), 1.0)
    ffn1_wg = nrm((DEPTH, d, D_FF), d ** -0.5)
    ffn1_wu = nrm((DEPTH, d, D_FF), d ** -0.5)
    ffn1_wd = nrm((DEPTH, D_FF, d), DN_BETA * D_FF ** -0.5)
    ffn2_wg = nrm((DEPTH, d, D_FF), d ** -0.5)
    ffn2_wu = nrm((DEPTH, d, D_FF), d ** -0.5)
    ffn2_wd = nrm((DEPTH, D_FF, d), DN_BETA * D_FF ** -0.5)
    ln_g = 1.0 + nrm((DEPTH, 3, d), 0.02)
    ln_b = nrm((DEPTH, 3, d), 0.02)
    ple_wg = nrm((DEPTH, d, d), d ** -0.5)
    ple_bg = nrm((DEPTH, d), 0.02)
    ple_wp = nrm((DEPTH, D_PLE, d), D_PLE ** -0.5)
    ab_w_in = nrm((N_EVEN, d, AB_PROJ), d ** -0.5)
    a_sinks = nrm((N_EVEN, A_HEADS), 0.5)
    b_conv_w = nrm((N_EVEN, B_CONV, B_WIDTH), B_CONV ** -0.5)
    b_conv_b = nrm((N_EVEN, B_WIDTH), 0.02)
    b_wa = nrm((N_EVEN, B_BLOCKS, B_BLOCK, B_BLOCK), B_BLOCK ** -0.5)
    b_ba = nrm((N_EVEN, B_WIDTH), 0.02)
    b_wx = nrm((N_EVEN, B_BLOCKS, B_BLOCK, B_BLOCK), B_BLOCK ** -0.5)
    b_bx = nrm((N_EVEN, B_WIDTH), 0.02)
    a_c = jax.random.uniform(next(ks), (N_EVEN, B_WIDTH), f32, 0.9, 0.999)
    a0 = a_c ** (1.0 / RG_C)
    b_lam = jnp.log(a0) - jnp.log1p(-a0)
    ab_w_out = nrm((N_EVEN, A_WIDTH + B_WIDTH, d), DN_BETA * (A_WIDTH + B_WIDTH) ** -0.5)
    c_w_in = nrm((N_ODD, d, C_PROJ), d ** -0.5)
    c_conv_w = nrm((N_ODD, C_CONV, 3 * C_WIDTH), C_CONV ** -0.5)
    c_a_log = jnp.log(jax.random.uniform(next(ks), (N_ODD, C_HEADS), f32, 1.0, 16.0))
    dt = jnp.exp(jax.random.uniform(next(ks), (N_ODD, C_HEADS), f32, np.log(1e-3), np.log(1e-1)))
    c_dt_bias = dt + jnp.log(-jnp.expm1(-dt))
    c_norm_g = 1.0 + nrm((N_ODD, C_HEAD_DIM), 0.02)
    c_w_out = nrm((N_ODD, C_WIDTH, d), DN_BETA * C_WIDTH ** -0.5)
    return {'x': x, 'p': p,
            'ffn1_wg': ffn1_wg, 'ffn1_wu': ffn1_wu, 'ffn1_wd': ffn1_wd,
            'ffn2_wg': ffn2_wg, 'ffn2_wu': ffn2_wu, 'ffn2_wd': ffn2_wd,
            'ln_g': ln_g, 'ln_b': ln_b,
            'ple_wg': ple_wg, 'ple_bg': ple_bg, 'ple_wp': ple_wp,
            'ab_w_in': ab_w_in, 'a_sinks': a_sinks,
            'b_conv_w': b_conv_w, 'b_conv_b': b_conv_b,
            'b_wa': b_wa, 'b_ba': b_ba, 'b_wx': b_wx, 'b_bx': b_bx, 'b_lam': b_lam,
            'ab_w_out': ab_w_out,
            'c_w_in': c_w_in, 'c_conv_w': c_conv_w, 'c_a_log': c_a_log, 'c_dt_bias': c_dt_bias,
            'c_norm_g': c_norm_g, 'c_w_out': c_w_out}

def first_block(x, p, ffn1_wg, ffn1_wu, ffn1_wd, ffn2_wg, ffn2_wu, ffn2_wd, ln_g, ln_b,
              ple_wg, ple_bg, ple_wp, ab_w_in, a_sinks, b_conv_w, b_conv_b,
              b_wa, b_ba, b_wx, b_bx, b_lam, ab_w_out,
              c_w_in, c_conv_w, c_a_log, c_dt_bias, c_norm_g, c_w_out):
    for i in range(DEPTH):
        j = i // 2
        x = layer_norm(DN_ALPHA * x + 0.5 * swiglu(x, ffn1_wg[i], ffn1_wu[i], ffn1_wd[i]), ln_g[i, 0], ln_b[i, 0])
        if i % 2 == 0:
            y = mixer_ab(x, ab_w_in[j], a_sinks[j], b_conv_w[j], b_conv_b[j],
                         b_wa[j], b_ba[j], b_wx[j], b_bx[j], b_lam[j], ab_w_out[j])
        else:
            y = mixer_c(x, c_w_in[j], c_conv_w[j], c_a_log[j], c_dt_bias[j], c_norm_g[j], c_w_out[j])
        x = layer_norm(DN_ALPHA * x + y, ln_g[i, 1], ln_b[i, 1])
        x = layer_norm(DN_ALPHA * x + 0.5 * swiglu(x, ffn2_wg[i], ffn2_wu[i], ffn2_wd[i]), ln_g[i, 2], ln_b[i, 2])
        x = x + jax.nn.sigmoid(x @ ple_wg[i] + ple_bg[i]) * (p[i] @ ple_wp[i])
    return x


GRID_W = 64
CTX_LEN = 256
HEAD_DIM = 64
A_GROUP_2 = A_HEADS // A_KV_HEADS
B_HEADS = 8
NA_ROWS = 8
NA_COLS = 16
Q_BLOCK = 128
ROPE_THETA = 10000.0
MLA_HEADS = 16
MLA_Q_LORA = 768
MLA_KV_LORA = 256
MLA_NOPE_DIM = 64
MLA_ROPE_DIM = 32
MLA_V_DIM = 64
CONV_WIDTH = 3
N_MOD = 6
EPS = 1e-6
DEEPNORM_ALPHA = (2 * DEPTH) ** 0.25
DEEPNORM_BETA = (8 * DEPTH) ** -0.25
HEAD_SCALE = HEAD_DIM ** -0.5
MLA_SCALE = (MLA_NOPE_DIM + MLA_ROPE_DIM) ** -0.5
_A_Q = A_HEADS * HEAD_DIM
_A_KV = A_KV_HEADS * HEAD_DIM
_B_W = B_HEADS * HEAD_DIM
EVEN_IN_DIM = _A_Q + 2 * _A_KV + 3 * _B_W
EVEN_SPLITS = (_A_Q, _A_Q + _A_KV, _A_Q + 2 * _A_KV, _A_Q + 2 * _A_KV + _B_W, _A_Q + 2 * _A_KV + 2 * _B_W)
EVEN_OUT_DIM = (A_HEADS + B_HEADS) * HEAD_DIM
ODD_IN_DIM = MLA_Q_LORA + MLA_KV_LORA + MLA_ROPE_DIM
ODD_OUT_DIM = MLA_HEADS * MLA_V_DIM


def _layer_norm(x, g, b):
    xf = x.astype(jnp.float32)
    mu = jnp.mean(xf, axis=-1, keepdims=True)
    var = jnp.mean(jnp.square(xf - mu), axis=-1, keepdims=True)
    return ((xf - mu) * lax.rsqrt(var + EPS) * g + b).astype(x.dtype)

def _rms_norm(x, g):
    xf = x.astype(jnp.float32)
    return (xf * lax.rsqrt(jnp.mean(jnp.square(xf), axis=-1, keepdims=True) + EPS) * g).astype(x.dtype)

def _axial_rope(length, rot_dim, dtype):
    pos = jnp.arange(length, dtype=jnp.int32)
    rows = (pos // GRID_W).astype(jnp.float32)
    cols = (pos % GRID_W).astype(jnp.float32)
    axis_dim = rot_dim // 2
    inv = ROPE_THETA ** (-jnp.arange(0, axis_dim, 2, dtype=jnp.float32) / axis_dim)
    ang = jnp.concatenate([rows[:, None] * inv, cols[:, None] * inv], axis=-1)
    return jnp.cos(ang).astype(dtype), jnp.sin(ang).astype(dtype)

def _rope(x, cos, sin):
    xp = x.reshape(x.shape[:-1] + (x.shape[-1] // 2, 2))
    x1, x2 = xp[..., 0], xp[..., 1]
    return jnp.stack([x1 * cos - x2 * sin, x1 * sin + x2 * cos], axis=-1).reshape(x.shape)

def _heads(t, n, d):
    b, length, _ = t.shape
    return t.reshape(b, length, n, d).transpose(0, 2, 1, 3)

def _merge_heads(t):
    b, h, length, d = t.shape
    return t.transpose(0, 2, 1, 3).reshape(b, length, h * d)

def _dense_attention(q, k, v, kc, vc, scale):
    b, g, r, length, dk = q.shape
    nb = length // Q_BLOCK
    qb = jnp.moveaxis(q.reshape(b, g, r, nb, Q_BLOCK, dk), 3, 0)

    def one_block(qblk):
        s = jnp.concatenate([jnp.einsum('bgrqd,bgkd->bgrqk', qblk, k),
                             jnp.einsum('bgrqd,bgcd->bgrqc', qblk, kc)], axis=-1)
        p = jax.nn.softmax(s.astype(jnp.float32) * scale, axis=-1).astype(v.dtype)
        return (jnp.einsum('bgrqk,bgkd->bgrqd', p[..., :length], v)
                + jnp.einsum('bgrqc,bgcd->bgrqd', p[..., length:], vc))

    o = lax.map(one_block, qb)
    return jnp.moveaxis(o, 0, 3).reshape(b, g, r, length, -1)

def _context_attention(q, k, v, scale):
    s = jnp.einsum('bgrqd,bgkd->bgrqk', q, k).astype(jnp.float32) * scale
    p = jax.nn.softmax(s, axis=-1).astype(v.dtype)
    return jnp.einsum('bgrqk,bgkd->bgrqd', p, v)

def _neighbourhood_attention(q, k, v, kc, vc, rpb, scale):
    b, h, length, d = q.shape
    rows = length // GRID_W
    wr = min(NA_ROWS, rows)
    qg = q.reshape(b, h, rows, GRID_W, d)
    kg = k.reshape(b, h, rows, GRID_W, d)
    vg = v.reshape(b, h, rows, GRID_W, d)
    col = jnp.arange(GRID_W, dtype=jnp.int32)
    col_start = jnp.clip(col - NA_COLS // 2, 0, GRID_W - NA_COLS)
    col_idx = col_start[:, None] + jnp.arange(NA_COLS, dtype=jnp.int32)[None, :]
    col_bias = rpb[:, :, col_idx - col[:, None] + (NA_COLS - 1)].astype(jnp.float32)
    n_nb = wr * NA_COLS

    def one_row(args):
        r, q_row = args
        rs = jnp.clip(r - wr // 2, 0, rows - wr)
        k_win = lax.dynamic_slice_in_dim(kg, rs, wr, axis=2)[:, :, :, col_idx]
        v_win = lax.dynamic_slice_in_dim(vg, rs, wr, axis=2)[:, :, :, col_idx]
        row_off = rs + jnp.arange(wr, dtype=jnp.int32) - r + (NA_ROWS - 1)
        bias = col_bias[:, row_off].transpose(0, 2, 1, 3)
        s_nb = jnp.einsum('bhqd,bhrqkd->bhqrk', q_row, k_win).astype(jnp.float32) * scale + bias[None]
        s_ctx = jnp.einsum('bhqd,bhcd->bhqc', q_row, kc).astype(jnp.float32) * scale
        p = jax.nn.softmax(jnp.concatenate([s_nb.reshape(b, h, GRID_W, n_nb), s_ctx], axis=-1), axis=-1).astype(v.dtype)
        p_nb = p[..., :n_nb].reshape(b, h, GRID_W, wr, NA_COLS)
        return (jnp.einsum('bhqrk,bhrqkd->bhqd', p_nb, v_win)
                + jnp.einsum('bhqc,bhcd->bhqd', p[..., n_nb:], vc))

    out = lax.map(one_row, (jnp.arange(rows, dtype=jnp.int32), jnp.moveaxis(qg, 2, 0)))
    return jnp.moveaxis(out, 0, 2).reshape(b, h, length, d)

def _even_mixer(h, hc, w_in, q_gain, k_gain, rpb, w_out, need_ctx):
    b, length, _ = h.shape
    cos, sin = _axial_rope(length, HEAD_DIM, h.dtype)

    def project(t):
        qa, ka, va, qb, kb, vb = jnp.split(t @ w_in, EVEN_SPLITS, axis=-1)
        return (_rms_norm(_heads(qa, A_HEADS, HEAD_DIM), q_gain),
                _rms_norm(_heads(ka, A_KV_HEADS, HEAD_DIM), k_gain),
                _heads(va, A_KV_HEADS, HEAD_DIM),
                _heads(qb, B_HEADS, HEAD_DIM), _heads(kb, B_HEADS, HEAD_DIM), _heads(vb, B_HEADS, HEAD_DIM))

    qa, ka, va, qb, kb, vb = project(h)
    qac, kac, vac, qbc, kbc, vbc = project(hc)
    qa = _rope(qa, cos, sin)
    ka = _rope(ka, cos, sin)
    ya = _dense_attention(qa.reshape(b, A_KV_HEADS, A_GROUP_2, length, HEAD_DIM), ka, va, kac, vac,
                          HEAD_SCALE).reshape(b, A_HEADS, length, HEAD_DIM)
    yb = _neighbourhood_attention(qb, kb, vb, kbc, vbc, rpb, HEAD_SCALE)
    y = _merge_heads(jnp.concatenate([ya, yb], axis=1)) @ w_out
    yc = None
    if need_ctx:
        lc = hc.shape[1]
        yac = _context_attention(qac.reshape(b, A_KV_HEADS, A_GROUP_2, lc, HEAD_DIM), kac, vac,
                                 HEAD_SCALE).reshape(b, A_HEADS, lc, HEAD_DIM)
        ybc = _context_attention(qbc[:, :, None], kbc, vbc, HEAD_SCALE)[:, :, 0]
        yc = _merge_heads(jnp.concatenate([yac, ybc], axis=1)) @ w_out
    return y, yc

def _odd_mixer(h, hc, w_in, cq_gain, ckv_gain, w_uq, w_ukv, w_out, need_ctx):
    b, length, _ = h.shape
    cos, sin = _axial_rope(length, MLA_ROPE_DIM, h.dtype)

    def compress(t):
        c_q, c_kv, k_r = jnp.split(t @ w_in, (MLA_Q_LORA, MLA_Q_LORA + MLA_KV_LORA), axis=-1)
        return _rms_norm(c_q, cq_gain), _rms_norm(c_kv, ckv_gain), k_r

    def up_q(c_q):
        return jnp.split(_heads(c_q @ w_uq, MLA_HEADS, MLA_NOPE_DIM + MLA_ROPE_DIM), (MLA_NOPE_DIM,), axis=-1)

    def up_kv(c_kv, k_r):
        k_nope, v = jnp.split(_heads(c_kv @ w_ukv, MLA_HEADS, MLA_NOPE_DIM + MLA_V_DIM), (MLA_NOPE_DIM,), axis=-1)
        k_shared = jnp.broadcast_to(k_r[:, None], k_nope.shape[:-1] + (MLA_ROPE_DIM,))
        return jnp.concatenate([k_nope, k_shared], axis=-1), v

    c_q, c_kv, k_r = compress(h)
    cc_q, cc_kv, kc_r = compress(hc)
    q_nope, q_rope = up_q(c_q)
    q = jnp.concatenate([q_nope, _rope(q_rope, cos, sin)], axis=-1)
    k, v = up_kv(c_kv, _rope(k_r, cos, sin))
    kc, vc = up_kv(cc_kv, kc_r)
    y = _merge_heads(_dense_attention(q[:, :, None], k, v, kc, vc, MLA_SCALE)[:, :, 0]) @ w_out
    yc = None
    if need_ctx:
        qc = jnp.concatenate(up_q(cc_q), axis=-1)
        yc = _merge_heads(_context_attention(qc[:, :, None], kc, vc, MLA_SCALE)[:, :, 0]) @ w_out
    return y, yc

def _conv_ffn(h, w_up, conv_w, conv_b, w_down):
    gate, val = jnp.split(h @ w_up, 2, axis=-1)
    gate = lax.conv_general_dilated(gate, conv_w[:, None, :], (1,), ((CONV_WIDTH // 2, CONV_WIDTH // 2),),
                                    dimension_numbers=('NWC', 'WIO', 'NWC'), feature_group_count=D_FF) + conv_b
    return (jax.nn.silu(gate) * val) @ w_down

def _adaln(cond, w, b):
    return jnp.split(jax.nn.silu(cond) @ w + b, N_MOD, axis=-1)

def second_inputs(seed: int = 0) -> dict:
    key = jax.random.key(seed)
    ks = iter(jax.random.split(key, 40))

    def nrm(shape, scale):
        return jax.random.normal(next(ks), shape, jnp.float32) * scale

    def gain(n):
        return 1.0 + nrm((n,), 0.1)

    d = D_MODEL
    return {
        'x': nrm((BATCH, SEQ, d), 1.0),
        'c': nrm((BATCH, d), 1.0),
        'ctx': nrm((BATCH, CTX_LEN, d), 1.0),
        'c_ctx': nrm((d,), 1.0),
        'l0_w_ada': nrm((d, N_MOD * d), 0.5 * d ** -0.5),
        'l0_b_ada': nrm((N_MOD * d,), 0.1),
        'l0_w_in': nrm((d, EVEN_IN_DIM), d ** -0.5),
        'l0_q_gain': gain(HEAD_DIM),
        'l0_k_gain': gain(HEAD_DIM),
        'l0_rpb': nrm((B_HEADS, 2 * NA_ROWS - 1, 2 * NA_COLS - 1), 0.5),
        'l0_w_out': nrm((EVEN_OUT_DIM, d), DEEPNORM_BETA * EVEN_OUT_DIM ** -0.5),
        'l0_ln1_g': gain(d),
        'l0_ln1_b': nrm((d,), 0.02),
        'l0_w_up': nrm((d, 2 * D_FF), d ** -0.5),
        'l0_conv_w': nrm((CONV_WIDTH, D_FF), CONV_WIDTH ** -0.5),
        'l0_conv_b': nrm((D_FF,), 0.02),
        'l0_w_down': nrm((D_FF, d), DEEPNORM_BETA * D_FF ** -0.5),
        'l0_ln2_g': gain(d),
        'l0_ln2_b': nrm((d,), 0.02),
        'l1_w_ada': nrm((d, N_MOD * d), 0.5 * d ** -0.5),
        'l1_b_ada': nrm((N_MOD * d,), 0.1),
        'l1_w_in': nrm((d, ODD_IN_DIM), d ** -0.5),
        'l1_cq_gain': gain(MLA_Q_LORA),
        'l1_ckv_gain': gain(MLA_KV_LORA),
        'l1_w_uq': nrm((MLA_Q_LORA, MLA_HEADS * (MLA_NOPE_DIM + MLA_ROPE_DIM)), MLA_Q_LORA ** -0.5),
        'l1_w_ukv': nrm((MLA_KV_LORA, MLA_HEADS * (MLA_NOPE_DIM + MLA_V_DIM)), MLA_KV_LORA ** -0.5),
        'l1_w_out': nrm((ODD_OUT_DIM, d), DEEPNORM_BETA * ODD_OUT_DIM ** -0.5),
        'l1_ln1_g': gain(d),
        'l1_ln1_b': nrm((d,), 0.02),
        'l1_w_up': nrm((d, 2 * D_FF), d ** -0.5),
        'l1_conv_w': nrm((CONV_WIDTH, D_FF), CONV_WIDTH ** -0.5),
        'l1_conv_b': nrm((D_FF,), 0.02),
        'l1_w_down': nrm((D_FF, d), DEEPNORM_BETA * D_FF ** -0.5),
        'l1_ln2_g': gain(d),
        'l1_ln2_b': nrm((d,), 0.02),
    }

def second_block(x, c, ctx, c_ctx,
              l0_w_ada, l0_b_ada, l0_w_in, l0_q_gain, l0_k_gain, l0_rpb, l0_w_out, l0_ln1_g, l0_ln1_b,
              l0_w_up, l0_conv_w, l0_conv_b, l0_w_down, l0_ln2_g, l0_ln2_b,
              l1_w_ada, l1_b_ada, l1_w_in, l1_cq_gain, l1_ckv_gain, l1_w_uq, l1_w_ukv, l1_w_out, l1_ln1_g, l1_ln1_b,
              l1_w_up, l1_conv_w, l1_conv_b, l1_w_down, l1_ln2_g, l1_ln2_b):
    layers = (
        dict(w_ada=l0_w_ada, b_ada=l0_b_ada, w_in=l0_w_in, q_gain=l0_q_gain, k_gain=l0_k_gain, rpb=l0_rpb,
             w_out=l0_w_out, ln1_g=l0_ln1_g, ln1_b=l0_ln1_b, w_up=l0_w_up, conv_w=l0_conv_w, conv_b=l0_conv_b,
             w_down=l0_w_down, ln2_g=l0_ln2_g, ln2_b=l0_ln2_b),
        dict(w_ada=l1_w_ada, b_ada=l1_b_ada, w_in=l1_w_in, cq_gain=l1_cq_gain, ckv_gain=l1_ckv_gain,
             w_uq=l1_w_uq, w_ukv=l1_w_ukv, w_out=l1_w_out, ln1_g=l1_ln1_g, ln1_b=l1_ln1_b, w_up=l1_w_up,
             conv_w=l1_conv_w, conv_b=l1_conv_b, w_down=l1_w_down, ln2_g=l1_ln2_g, ln2_b=l1_ln2_b),
    )
    xc = ctx
    for i in range(DEPTH):
        p = layers[i]
        need_ctx = i < DEPTH - 1
        sh1, sc1, g1, sh2, sc2, g2 = [m[:, None, :] for m in _adaln(c, p['w_ada'], p['b_ada'])]
        csh1, csc1, cg1, csh2, csc2, cg2 = _adaln(c_ctx, p['w_ada'], p['b_ada'])
        h = x * (1.0 + sc1) + sh1
        hc = xc * (1.0 + csc1) + csh1
        if i % 2 == 0:
            y, yc = _even_mixer(h, hc, p['w_in'], p['q_gain'], p['k_gain'], p['rpb'], p['w_out'], need_ctx)
        else:
            y, yc = _odd_mixer(h, hc, p['w_in'], p['cq_gain'], p['ckv_gain'], p['w_uq'], p['w_ukv'],
                               p['w_out'], need_ctx)
        x = _layer_norm(DEEPNORM_ALPHA * x + g1 * y, p['ln1_g'], p['ln1_b'])
        h = x * (1.0 + sc2) + sh2
        x = _layer_norm(DEEPNORM_ALPHA * x + g2 * _conv_ffn(h, p['w_up'], p['conv_w'], p['conv_b'], p['w_down']),
                        p['ln2_g'], p['ln2_b'])
        if need_ctx:
            xc = _layer_norm(DEEPNORM_ALPHA * xc + cg1 * yc, p['ln1_g'], p['ln1_b'])
            hc = xc * (1.0 + csc2) + csh2
            xc = _layer_norm(DEEPNORM_ALPHA * xc + cg2 * _conv_ffn(hc, p['w_up'], p['conv_w'], p['conv_b'], p['w_down']),
                             p['ln2_g'], p['ln2_b'])
    return x


def setup_inputs(seed=0):
    out = dict(first_inputs(seed))
    for name, value in second_inputs(seed + 1).items():
        if name != "x":
            out[name + "_2"] = value
    return out


def reference(
    x, p, ffn1_wg, ffn1_wu, ffn1_wd, ffn2_wg, ffn2_wu, ffn2_wd, ln_g, ln_b, ple_wg, ple_bg,
    ple_wp, ab_w_in, a_sinks, b_conv_w, b_conv_b, b_wa, b_ba, b_wx, b_bx, b_lam, ab_w_out,
    c_w_in, c_conv_w, c_a_log, c_dt_bias, c_norm_g, c_w_out, c_2, ctx_2, c_ctx_2, l0_w_ada_2,
    l0_b_ada_2, l0_w_in_2, l0_q_gain_2, l0_k_gain_2, l0_rpb_2, l0_w_out_2, l0_ln1_g_2,
    l0_ln1_b_2, l0_w_up_2, l0_conv_w_2, l0_conv_b_2, l0_w_down_2, l0_ln2_g_2, l0_ln2_b_2,
    l1_w_ada_2, l1_b_ada_2, l1_w_in_2, l1_cq_gain_2, l1_ckv_gain_2, l1_w_uq_2, l1_w_ukv_2,
    l1_w_out_2, l1_ln1_g_2, l1_ln1_b_2, l1_w_up_2, l1_conv_w_2, l1_conv_b_2, l1_w_down_2,
    l1_ln2_g_2, l1_ln2_b_2,
):
    x = first_block(
        x, p, ffn1_wg, ffn1_wu, ffn1_wd, ffn2_wg, ffn2_wu, ffn2_wd, ln_g, ln_b, ple_wg, ple_bg,
        ple_wp, ab_w_in, a_sinks, b_conv_w, b_conv_b, b_wa, b_ba, b_wx, b_bx, b_lam, ab_w_out,
        c_w_in, c_conv_w, c_a_log, c_dt_bias, c_norm_g, c_w_out,
    )
    return second_block(
        x, c_2, ctx_2, c_ctx_2, l0_w_ada_2, l0_b_ada_2, l0_w_in_2, l0_q_gain_2, l0_k_gain_2,
        l0_rpb_2, l0_w_out_2, l0_ln1_g_2, l0_ln1_b_2, l0_w_up_2, l0_conv_w_2, l0_conv_b_2,
        l0_w_down_2, l0_ln2_g_2, l0_ln2_b_2, l1_w_ada_2, l1_b_ada_2, l1_w_in_2, l1_cq_gain_2,
        l1_ckv_gain_2, l1_w_uq_2, l1_w_ukv_2, l1_w_out_2, l1_ln1_g_2, l1_ln1_b_2, l1_w_up_2,
        l1_conv_w_2, l1_conv_b_2, l1_w_down_2, l1_ln2_g_2, l1_ln2_b_2,
    )


_drawn_inputs = setup_inputs


def setup_inputs(seed=0):
    import zlib

    import numpy as np

    out = dict(_drawn_inputs(seed))
    spreads = {}
    factors = {'ple_bg': 8.0,
     'a_sinks': 8.0,
     'b_conv_b': 5.25,
     'b_ba': 8.0,
     'b_bx': 8.0,
     'c_norm_g': 8.0,
     'ctx_2': 5.83,
     'l0_q_gain_2': 8.0,
     'l0_k_gain_2': 8.0,
     'l0_rpb_2': 27.446,
     'l0_ln1_b_2': 2.795,
     'l0_conv_b_2': 8.0,
     'l0_ln2_b_2': 2.795,
     'l1_cq_gain_2': 8.0,
     'l1_ckv_gain_2': 8.0,
     'l1_w_uq_2': 5.629,
     'l1_ln1_b_2': 2.929,
     'l1_conv_b_2': 36.611,
     'l1_ln2_b_2': 2.867}
    for name, (base, spread) in spreads.items():
        noise = np.random.default_rng([zlib.crc32(name.encode()), seed]).standard_normal(out[name].shape)
        drawn = base * np.exp(spread * noise) if base else spread * noise
        out[name] = jnp.asarray(drawn.astype(out[name].dtype))
    for name, factor in factors.items():
        out[name] = (out[name] * factor).astype(out[name].dtype)
    return out
```

```python
from contextlib import ExitStack

import numpy as np

import concourse.bass as bass
from concourse import mybir

F32 = mybir.dt.float32
F32R = mybir.dt.float32r
ACT = mybir.ActivationFunctionType
ALU = mybir.AluOpType
AX = mybir.AxisListType
ENG = mybir.EngineType

P = 128
D = 1024
KC = D // P
T = 256
F = 2816
NT = F // P
NPAIR = NT // 2
CH = 64
SLOT = 2048
RING = 6
ALPHA = 4.0 ** 0.25
NEG = -1e30
HEADS = 8
PAIRED = [h for t in range(4) for h in (t, t + 4)]
MLA_H, NOPE, ROPE = 16, 64, 32
CQ, CKV = 768, 256

STREAM = [
    ("ffn1_0", 3 * NPAIR), ("ab_in", 7), ("alibi", 2), ("ab_out", 4), ("ffn2_0", 3 * NPAIR),
    ("ple_p_0", 1), ("ple_g_0", 4),
    ("ffn1_1", 3 * NPAIR), ("c_in", 17), ("c_out", 4), ("ffn2_1", 3 * NPAIR),
    ("ple_p_1", 1), ("ple_g_1", 4),
    ("ada_0", 24), ("ada_1", 24), ("l0_in", 9), ("rpb", 2), ("l0_out", 4), ("l0_ffn", 3 * NPAIR),
    ("l1_in", 5), ("l1_uq", 6), ("l1_ukv", 2), ("l1_out", 4), ("l1_ffn", 3 * NPAIR),
]
ROW = {}
_n = 0
for _name, _count in STREAM:
    ROW[_name] = _n
    _n += _count
N_ROWS = _n

PARAMS = (
    [(f"ln_{v}{i}{k}", KC) for i in range(2) for k in range(3) for v in "gb"]
    + [(f"ple_b{i}", KC) for i in range(2)]
    + [("sink", HEADS), ("b_cw", 16), ("b_cb", 4), ("b_ba", 4), ("b_bx", 4), ("b_lam", 4)]
    + [("c_cw", 96), ("c_alog", 1), ("c_dt", 1), ("c_ng", 1), ("cond", 16), ("ada_b0", 48), ("ada_b1", 48)]
    + [("q_gain", 1), ("k_gain", 1), ("cq_gain", 6), ("ckv_gain", 2)]
    + [(f"l{i}_ln{k}{v}", KC) for i in range(2) for k in (1, 2) for v in "gb"]
    + [(f"l{i}_cw", 3 * NT) for i in range(2)] + [(f"l{i}_cb", NT) for i in range(2)]
)
PCOL = {}
_n = 0
for _name, _count in PARAMS:
    PCOL[_name] = _n
    _n += _count
N_PCOL = _n

CONSTS = [("ident", 128), ("mean", 128), ("ones", 128), ("mean64", 128), ("rot", 128),
          ("cosA", T), ("sinA", T), ("cosM", T), ("sinM", T),
          ("after", 128), ("upto", 128), ("before", 128), ("in16", 128), ("in32", 128), ("in64", 128)]
CCOL = {}
_n = 0
for _name, _count in CONSTS:
    CCOL[_name] = _n
    _n += _count
N_CCOL = _n


class Lane:

    def __init__(self, eng, new_sem, name):
        self.eng, self.new_sem, self.name, self.gen = eng, new_sem, name, 0
        self.seen = {}
        self.fresh()

    def fresh(self):
        self.sem, self.count, self.gen = self.new_sem(f"{self.name}_{self.gen}"), 0, self.gen + 1

    def after(self, *tokens):
        for tok in tokens:
            if tok is not None and self.seen.get(id(tok[0]), 0) < tok[1]:
                self.seen[id(tok[0])] = tok[1]
                self.eng.wait_ge(tok[0], tok[1])

    def mark(self, ins):
        self.count += 1
        ins.then_inc(self.sem, 1)
        return (self.sem, self.count)

    def last(self):
        return (self.sem, self.count) if self.count else None


def build_program(nc, wstream, params, consts, xin, cin, pin, wab, out):
    with ExitStack() as top:
        def new_sem(name):
            return top.enter_context(nc.semaphore(name))

        def alloc(stack, name, shape, dtype=F32):
            return stack.enter_context(nc.sbuf_tensor(name, [P] + list(shape), dtype))

        pe, act, dve = nc.tensor, nc.scalar, nc.vector
        PE, AC, VE = Lane(pe, new_sem, "s_pe"), Lane(act, new_sem, "s_act"), Lane(dve, new_sem, "s_dve")

        final = [None] * 3

        def join():
            ends = [lane.last() for lane in (PE, AC, VE)]
            for i, end in enumerate(ends):
                final[i] = end or final[i]
            for lane in (PE, AC, VE):
                lane.after(*ends)
            for lane in (PE, AC, VE):
                lane.fresh()

        ring = alloc(top, "ring", [RING, SLOT])
        block_1 = ExitStack()
        X = alloc(top, "X", [KC, T])
        PT_ = alloc(top, "PT_", [2, 2, T])
        PV = alloc(top, "PV", [N_PCOL])
        CN = alloc(top, "CN", [N_CCOL])
        MOD = alloc(top, "MOD", [2, 48, 2])
        rstd = alloc(top, "rstd", [2 * T])
        lnv = alloc(top, "lnv", [2 * T])
        hT = alloc(top, "hT", [4, T])
        sg = alloc(top, "sg", [4, T])
        cg = alloc(top, "cg", [4, T])
        ps = top.enter_context(nc.psum_tensor("ps", [P, 8, 512], F32))
        top.enter_context(block_1)
        Z = alloc(block_1, "Z", [KC, T])
        H = alloc(block_1, "H", [KC, T])

        def const(name):
            return CN[:, CCOL[name]:CCOL[name] + dict(CONSTS)[name]]

        def pcol(name, i=0, n=1):
            return PV[:, PCOL[name] + i:PCOL[name] + i + n]

        ident, mean, ones = const("ident"), const("mean"), const("ones")

        s_in = [new_sem(f"s_in{i}") for i in range(6)]
        first = [(PV[:, :], params), (CN[:, :], consts), (X[:, :, :], xin), (PT_[:, :, :, :], pin)]
        for s, (dst, src) in zip(s_in, first):
            act.dma_start(dst, src).then_inc(s, 16)
        for lane in (PE, AC, VE):
            lane.after(*[(s, 16) for s in s_in[:4]])

        s_load = [new_sem(f"s_load{i}") for i in range(RING)]
        s_gu, s_dn = new_sem("s_gu"), new_sem("s_dn")
        s_sg, s_h = new_sem("s_sg"), new_sem("s_h")
        s_hh, s_hl = new_sem("s_hh"), new_sem("s_hl")
        s_wh = [new_sem(f"s_wh{i}") for i in range(3)]
        s_lg, s_lu, s_ld = (new_sem(f"s_l{i}") for i in "gud")
        s_wl = (s_lg, s_lu, s_ld)
        s_id, s_cv = new_sem("s_id"), new_sem("s_cv")
        ring_log = []
        ffn_at = {}

        def loaded(n):
            return (s_load[n % RING], 16 * (n // RING + 1))

        def take(row):
            n = len(ring_log)
            ring_log.append([row, None])
            PE.after(loaded(n))
            return n, ring[:, n % RING, :]

        def release(n, tok):
            ring_log[n][1] = tok

        bank_free = [[] for _ in range(8)]
        bank_turn = [0]

        def bank(among=range(8)):
            among = list(among)
            b = among[bank_turn[0] % len(among)]
            bank_turn[0] += 1
            PE.after(*bank_free[b])
            bank_free[b] = []
            return b

        def feature_major(row, n_tiles, kc, rhs, N, evac, per_slot=2, M=P):
            for t in range(n_tiles):
                if t % per_slot == 0:
                    n, w = take(row + t // per_slot)
                    w = w[:, 0:kc * per_slot * M].rearrange("p (c m) -> p c m", c=kc)
                b = bank()
                at = (t % per_slot) * M
                for c in range(kc):
                    mm = pe.matmul(ps[0:M, b, 0:N], w[:, c, at:at + M], rhs(c), start=(c == 0), stop=(c == kc - 1))
                done = PE.mark(mm)
                if t % per_slot == per_slot - 1 or t == n_tiles - 1:
                    release(n, done)
                read = evac(t, ps[0:M, b, 0:N], done)
                bank_free[b] = read if isinstance(read, list) else [read]

        def token_major(w, kc, lhs, n_tt, cols, dst):
            for tt in range(n_tt):
                b = bank()
                for c in range(kc):
                    mm = pe.matmul(ps[:, b, 0:cols], lhs(c, tt), w[:, c, :], start=(c == 0), stop=(c == kc - 1))
                done = PE.mark(mm)
                AC.after(done)
                bank_free[b] = [AC.mark(act.activation(dst(tt), ps[:, b, 0:cols], ACT.Copy))]
            return done

        def layer_norm(z_ready, n0, N, eps, g, b):
            z = Z[:, :, n0:n0 + N]
            mb = bank()
            for c in range(KC):
                PE.after(z_ready[c])
                mm = pe.matmul(ps[:, mb, 0:N], mean, z[:, c, :], start=(c == 0), stop=(c == KC - 1))
            got_mean = PE.mark(mm)
            vb = bank()
            VE.after(got_mean)
            squares = []
            for q in range(4):
                zq = z[:, 2 * q:2 * q + 2, :]
                centred = VE.mark(dve.tensor_tensor(zq, zq, ps[:, mb, 0:N].unsqueeze(1).broadcast_to([P, 2, N]),
                                                    ALU.subtract))
                AC.after(centred)
                squares.append(AC.mark(act.activation(H[:, 2 * q:2 * q + 2, n0:n0 + N], zq, ACT.Square)))
            bank_free[mb] = [centred]
            for c in range(KC):
                PE.after(squares[c // 2])
                mm = pe.matmul(ps[:, vb, 0:N], mean, H[:, c, n0:n0 + N], start=(c == 0), stop=(c == KC - 1))
            got_var = PE.mark(mm)
            AC.after(got_var)
            VE.after(got_var)
            VE.after(AC.last())
            act.preload_act_table_set("natural_log_exp_and_others")
            t = VE.mark(dve.tensor_scalar(rstd[:, 0:N], ps[:, vb, 0:N], eps, None, ALU.add))
            bank_free[vb] = [t]
            AC.after(t)
            t = AC.mark(act.activation(lnv[:, 0:N], rstd[:, 0:N], ACT.Ln))
            AC.after(t)
            t = AC.mark(act.activation(rstd[:, 0:N], lnv[:, 0:N], ACT.Exp, scale=-0.5))
            VE.after(t)
            done = []
            for q in range(4):
                zq = z[:, 2 * q:2 * q + 2, :]
                t = VE.mark(dve.tensor_tensor(zq, zq, rstd[:, 0:N].unsqueeze(1).broadcast_to([P, 2, N]), ALU.mult))
                AC.after(t)
                for c in (2 * q, 2 * q + 1):
                    done.append(AC.mark(act.activation(X[:, c, n0:n0 + N], z[:, c, :], ACT.Identity,
                                                       scale=pcol(g, c), bias=pcol(b, c))))
            return done

        def scaled_residual(n0, N):
            return AC.mark(act.activation(Z[:, :, n0:n0 + N], X[:, :, n0:n0 + N], ACT.Copy, scale=ALPHA))

        ffn_count = [0]

        def ffn(name, src, conv=None):
            with ExitStack() as st:
                return ffn_split(name, src, conv, st)

        def ffn_split(name, src, conv, st):
            join()
            base = NT * ffn_count[0]
            ffn_count[0] += 1
            n0 = len(ring_log)
            ffn_at[n0] = (base, ROW[name])
            for p in range(NPAIR):
                for k in range(3):
                    ring_log.append([ROW[name] + 3 * p + k, (s_wl[k], base + 2 * p + 2)])

            tag = f"f{ffn_count[0]}"
            xh, xl = alloc(st, tag + "_xh", [KC, T], F32R), alloc(st, tag + "_xl", [KC, T], F32R)
            wh, wl = alloc(st, tag + "_wh", [2, 3, KC, P], F32R), alloc(st, tag + "_wl", [2, 3, KC, P], F32R)
            hh, hl = alloc(st, tag + "_hh", [2, T], F32R), alloc(st, tag + "_hl", [2, T], F32R)
            for c in range(0, KC, 2):
                t = AC.mark(act.activation(xh[:, c:c + 2, :], src(c, 2), ACT.Copy))
                VE.after(t)
                x_split = VE.mark(dve.tensor_tensor(xl[:, c:c + 2, :], src(c, 2), xh[:, c:c + 2, :].bitcast(F32),
                                                    ALU.subtract))
            PE.after(x_split)

            def slot(n, k, j):
                w = ring[:, (n + k) % RING, :]
                if k == 2:
                    return w.rearrange("p (j c m) -> p j c m", j=2, m=P)[:, j, :, :]
                return w.rearrange("p (c m) -> p c m", c=KC)[:, :, j * P:(j + 1) * P]

            def split_weights(ks, n, j, t, s, free=None, turns=0):
                for k in ks:
                    w = slot(n, k, j)
                    if j == 0:
                        for eng in (act, dve):
                            eng.wait_ge(s_load[(n + k) % RING], turns * 16 + 16 * ((n + k) // RING + 1))
                    if free is not None and k != 1:
                        act.wait_ge(*free)
                    act.activation(wh[:, s, k, :, :], w, ACT.Copy).then_inc(s_wh[k], 1)
                    dve.wait_ge(s_wh[k], t + 1)
                    dve.tensor_tensor(wl[:, s, k, :, :], w, wh[:, s, k, :, :].bitcast(F32),
                                      ALU.subtract).then_inc(s_wl[k], 1)

            def three(out, w_hi, w_lo, x_hi, x_lo, start):
                pe.matmul(out, w_hi, x_hi, start=start, stop=False, skip_group_check=True)
                pe.matmul(out, w_lo, x_hi, start=False, stop=False, skip_group_check=True)
                return pe.matmul(out, w_hi, x_lo, start=False, stop=True, skip_group_check=True)

            def gate_up(t, s, bk):
                pe.wait_ge(s_lg, t + 1)
                for k in range(2):
                    if k == 1:
                        pe.wait_ge(s_lu, t + 1)
                    for c in range(KC):
                        mm = three(ps[:, bk, k * T:(k + 1) * T], wh[:, s, k, c, :], wl[:, s, k, c, :],
                                   xh[:, c, :], xl[:, c, :], start=(c == 0))
                mm.then_inc(s_gu, 1)

            def down(t, s, first=False):
                pe.wait_ge(s_ld, t + 1)
                pe.wait_ge(s_hl, t + 1)
                for o in range(KC):
                    mm = three(ps[:, o // 2, (o % 2) * T:(o % 2 + 1) * T], wh[:, s, 2, o, :], wl[:, s, 2, o, :],
                               hh[:, s, :], hl[:, s, :], start=(first and o % 2 == 0))
                mm.then_inc(s_dn, 1)

            def hidden(t, k, bk, conv_at):
                gate, up = ps[:, bk, 0:T], ps[:, bk, T:2 * T]
                act.wait_ge(s_gu, t + 1)
                if conv is None:
                    act.activation(sg[:, k, :], gate, ACT.Silu).then_inc(s_sg, 1)
                else:
                    w = [PV[:, bass.ds(conv_at + PCOL[f"l{conv}_cw"] + NT * tap, 1)] for tap in range(3)]
                    bias = PV[:, bass.ds(conv_at + PCOL[f"l{conv}_cb"], 1)]
                    cb = conv_at + base_cv
                    act.activation(cg[:, k, :], gate, ACT.Identity, scale=w[1], bias=bias).then_inc(s_id, 1)
                    dve.wait_ge(s_id, cb + 1)
                    dve.scalar_tensor_tensor(cg[:, k, 1:T], gate[:, 0:T - 1], w[0], cg[:, k, 1:T],
                                             ALU.mult, ALU.add).then_inc(s_cv, 1)
                    dve.wait_ge(s_cv, cb * 2 + 1)
                    dve.scalar_tensor_tensor(cg[:, k, 0:T - 1], gate[:, 1:T], w[2], cg[:, k, 0:T - 1],
                                             ALU.mult, ALU.add).then_inc(s_cv, 1)
                    act.wait_ge(s_cv, cb * 2 + 2)
                    act.activation(sg[:, k, :], cg[:, k, :], ACT.Silu).then_inc(s_sg, 1)
                dve.wait_ge(s_sg, t + 1)
                dve.tensor_tensor(hT[:, k, :], sg[:, k, :], up, ALU.mult).then_inc(s_h, 1)
                act.wait_ge(s_h, t + 1)
                act.activation(hh[:, k % 2, :], hT[:, k, :], ACT.Copy).then_inc(s_hh, 1)
                dve.wait_ge(s_hh, t + 1)
                dve.tensor_tensor(hl[:, k % 2, :], hT[:, k, :], hh[:, k % 2, :].bitcast(F32),
                                  ALU.subtract).then_inc(s_hl, 1)

            base_cv = conv_count[0]
            if conv is not None:
                conv_count[0] += NT
            split_weights((0, 1, 2), n0, 0, base, 0)
            split_weights((0, 1), n0, 1, base + 1, 1)
            gate_up(base, 0, 4)
            hidden(base, 0, 4, 0)
            split_weights((2,), n0, 1, base + 1, 1)
            n1 = n0 + 3
            split_weights((0, 1), n1, 0, base + 2, 0, free=(s_gu, base + 1))
            gate_up(base + 1, 1, 5)
            hidden(base + 1, 1, 5, 1)
            down(base, 0, first=True)
            split_weights((2,), n1, 0, base + 2, 0, free=(s_dn, base + 1))

            def tile(t, i, n_next, j_next, conv_at, turns):
                if n_next is not None:
                    split_weights((0, 1), n_next, j_next, t + 1, (i + 1) % 2, free=(s_gu, t), turns=turns)
                gate_up(t, i % 2, 4 + (2 + i) % 4)
                hidden(t, (2 + i) % 4, 4 + (2 + i) % 4, conv_at)
                down(t - 1, (i + 1) % 2)
                if n_next is not None:
                    split_weights((2,), n_next, j_next, t + 1, (i + 1) % 2, free=(s_dn, t), turns=turns)

            turns_of_4 = (NT - 6) // 4
            with nc.Fori(0, turns_of_4, engines=(ENG.PE, ENG.Activation, ENG.DVE)) as it:
                for i in range(4):
                    t = it * 4 + (base + 2 + i)
                    tile(t, i, n1 + 3 * ((i + 1) // 2), (i + 1) % 2, it * 4 + (2 + i), it)
            for i in range(4):
                k = 4 * turns_of_4 + i
                nxt = n1 + 3 * ((k + 1) // 2) if i < 3 else None
                tile(base + 2 + k, i, nxt, (k + 1) % 2, 2 + k, 0)
            down(base + NT - 1, (NT - 1) % 2)
            PE.seen.clear()
            AC.seen.clear()
            VE.seen.clear()
            return (s_dn, base + NT)

        conv_count = [0]

        def ffn_residual(n0, done, coef):
            zin = AC.last()
            VE.after(done, zin)
            toks = []
            for c in range(KC):
                y = ps[:, c // 2, (c % 2) * T:(c % 2 + 1) * T]
                k = coef if isinstance(coef, float) else coef(c)
                z = Z[:, c, n0:n0 + T]
                toks.append(VE.mark(dve.scalar_tensor_tensor(z, y, k, z, ALU.mult, ALU.add)))
            for b in range(4):
                bank_free[b] = [toks[2 * b + 1]]
            return toks

        def add_branch(N, coef):
            toks = []

            def evac(t, tile, done):
                VE.after(done)
                for n0 in range(0, N, T):
                    k = coef if isinstance(coef, float) else coef(t, n0 // T)
                    z = Z[:, t, n0:n0 + T]
                    tok = VE.mark(dve.scalar_tensor_tensor(z, tile[:, n0:n0 + T], k, z, ALU.mult, ALU.add))
                toks.append(tok)
                return tok
            return evac, toks

        def attention(tag, units):
            st = ExitStack()
            n = len(units)
            parts = [buf[:, 2 * i:2 * i + 2, :].rearrange("p a n -> p (a n)") for buf in (hT, sg, cg) for i in range(2)]
            pb, pt = parts[0:3], parts[3:6]
            small = alloc(st, f"{tag}_s", [3, 8])
            G = units[0]["G"]
            K = 512 // G
            s_sets = [(0, 1), (2, 3)] if G == 2 else [(0,), (1,), (2,), (3,)]
            t_banks, o_banks = (4, 5), (6, 7)
            tok = [dict() for _ in units]
            o_turn = [0]

            def scores(i):
                banks = s_sets[i % len(s_sets)]
                PE.after(*bank_free[banks[0]])
                tok[i]["s"] = units[i]["scores"](banks)

            def row_max(i):
                u, banks = units[i], s_sets[i % len(s_sets)]
                s = ps[:, banks[0]:banks[0] + G, 0:K]
                nm = small[:, i % 3, 0:G]
                if i >= 3:
                    VE.after(tok[i - 3]["exp"])
                VE.after(tok[i]["s"])
                t = VE.mark(dve.tensor_reduce(nm, s, AX.X, ALU.max, negate=True))
                if u["sink"] is not None:
                    VE.after(t)
                    t = VE.mark(dve.tensor_tensor(nm, nm, u["nsink"], ALU.min))
                tok[i]["max"] = t

            def exponentials(i):
                u, banks = units[i], s_sets[i % len(s_sets)]
                nm, den, es = (small[:, i % 3, 2 * j:2 * j + G] for j in (0, 1, 3))
                AC.after(tok[i]["max"])
                if i >= 3:
                    AC.after(tok[i - 3]["tr"], tok[i - 3]["norm"])
                for g in range(G):
                    e = AC.mark(act.activation(pb[i % 3][:, g * K:(g + 1) * K], ps[:, banks[g], 0:K], ACT.Exp,
                                               bias=nm[:, g:g + 1], accum_out=den[:, g:g + 1]))
                bank_free[banks[0]] = [e]
                if u["sink"] is not None:
                    for g in range(G):
                        e = AC.mark(act.activation(es[:, g:g + 1], u["sink"][g], ACT.Exp, bias=nm[:, g:g + 1]))
                tok[i]["exp"] = e

            def normalise(i):
                u = units[i]
                den, rd, es = (small[:, i % 3, 2 * j:2 * j + G] for j in (1, 2, 3))
                VE.after(tok[i]["exp"])
                if u["sink"] is not None:
                    t = VE.mark(dve.tensor_tensor(den, den, es, ALU.add))
                    VE.after(t)
                t = VE.mark(dve.reciprocal(rd, den))
                VE.after(t)
                for g in range(G):
                    pg = pb[i % 3][:, g * K:(g + 1) * K]
                    t = VE.mark(dve.tensor_scalar(pg, pg, rd[:, g:g + 1], None, ALU.mult))
                tok[i]["norm"] = t

            def transposes(i):
                b = t_banks[i % 2]
                PE.after(*bank_free[b])
                PE.after(tok[i]["norm"])
                for k in range(4):
                    mm = pe.transpose(ps[:, b, k * P:(k + 1) * P], pb[i % 3][:, k * P:(k + 1) * P], ident)
                tok[i]["tr"] = PE.mark(mm)
                AC.after(tok[i]["tr"])
                if i >= 3:
                    AC.after(tok[i - 3]["pv"])
                tok[i]["pt"] = AC.mark(act.activation(pt[i % 3], ps[:, b, :], ACT.Copy))
                bank_free[b] = [tok[i]["pt"]]

            def values(i):
                u = units[i]
                b = o_banks[o_turn[0] % 2]
                if u["new_o"]:
                    PE.after(*bank_free[b])
                PE.after(tok[i]["pt"])
                for g in range(G):
                    half, blocks = u["halves"][g], 4 // G
                    for k in range(blocks):
                        blk = g * blocks + k
                        mm = pe.matmul(ps[64 * half:64 * half + 64, b, 0:P], u["v"](k, g),
                                       pt[i % 3][:, blk * P:(blk + 1) * P], start=(k == 0), stop=(k == blocks - 1),
                                       skip_group_check=True)
                tok[i]["pv"] = PE.mark(mm)
                if u["end_o"]:
                    VE.after(tok[i]["pv"])
                    bank_free[b] = [VE.mark(dve.tensor_copy(u["o"], ps[:, b, 0:P]))]
                    o_turn[0] += 1

            steps = ((scores, 0), (transposes, 2), (normalise, 1), (row_max, 0), (exponentials, 0), (values, 3))
            for i in range(n + 3):
                for step, lag in steps:
                    if 0 <= i - lag < n:
                        step(i - lag)
            join()
            st.close()

        def rms_rows(terms, matrix, N, eps, dst, extra=0.0):
            b = bank()
            for k, (tile, tk) in enumerate(terms):
                PE.after(tk)
                mm = pe.matmul(ps[:, b, 0:N], matrix, tile, start=(k == 0), stop=(k == len(terms) - 1))
            t = PE.mark(mm)
            VE.after(t)
            VE.after(AC.last())
            t = VE.mark(dve.tensor_scalar(dst, ps[:, b, 0:N], eps, None, ALU.add))
            bank_free[b] = [t]
            AC.after(t)
            t = AC.mark(act.activation(dst, dst, ACT.Ln))
            AC.after(t)
            return AC.mark(act.activation(dst, dst, ACT.Exp, scale=-0.5))

        def rope(q, cos, sin, tmp, ready):
            b = bank()
            PE.after(ready)
            t = PE.mark(pe.matmul(ps[:, b, 0:T], const("rot"), q, start=True, stop=True))
            VE.after(t)
            VE.after(VE.last())
            a = VE.mark(dve.tensor_tensor(tmp, ps[:, b, 0:T], sin, ALU.mult))
            bank_free[b] = [a]
            c = VE.mark(dve.tensor_tensor(q, q, cos, ALU.mult))
            VE.after(c)
            return VE.mark(dve.tensor_tensor(q, q, tmp, ALU.add))

        def mixer_ab():
            with ExitStack() as st:
                join()
                x = lambda c: X[:, c, 0:T]
                q = alloc(st, "ab_q", [4, T])
                k = alloc(st, "ab_k", [T])
                v = alloc(st, "ab_v", [2, P])
                y = alloc(st, "ab_y", [8, T])
                bx = alloc(st, "ab_bx", [4, T + 3])
                xb = alloc(st, "ab_xb", [4, T])
                bg = alloc(st, "ab_bg", [4, T])
                tr = alloc(st, "ab_tr", [4, T])
                ti = alloc(st, "ab_ti", [4, T])
                wab_sb = alloc(st, "ab_w", [8, P])
                cols = alloc(st, "ab_cols", [40])
                scaled_residual(0, T)
                act.dma_start(wab_sb[:, :, :], wab).then_inc(s_in[5], 16)
                pads = VE.mark(dve.memset(bx[:, :, 0:3], 0.0))

                def evac_q(t, tile, done):
                    AC.after(done)
                    return AC.mark(act.activation(q[:, t, :], tile, ACT.Copy, scale=0.125))

                feature_major(ROW["ab_in"], 4, KC, x, T, evac_q)
                n, w = take(ROW["ab_in"] + 2)
                w = w.rearrange("p (c m) -> p c m", c=KC)
                b = bank()
                for c in range(KC):
                    mm = pe.matmul(ps[:, b, 0:T], w[:, c, 0:P], x(c), start=(c == 0), stop=(c == KC - 1))
                t = PE.mark(mm)
                AC.after(t)
                bank_free[b] = [AC.mark(act.activation(k[:, :], ps[:, b, 0:T], ACT.Copy))]
                t = token_major(w[:, :, P:2 * P], KC, lambda c, tt: X[:, c, tt * P:(tt + 1) * P], 2, P,
                                lambda tt: v[:, tt, :])
                release(n, t)

                def evac_b(dst, off):
                    def evac(t, tile, done):
                        VE.after(done)
                        return VE.mark(dve.tensor_copy(dst[:, t, off:off + T], tile))
                    return evac
                feature_major(ROW["ab_in"] + 3, 4, KC, x, T, evac_b(bx, 3))
                feature_major(ROW["ab_in"] + 5, 4, KC, x, T, evac_b(bg, 0))

                nsink = cols[:, 0:8]
                t = VE.mark(dve.tensor_scalar(nsink, pcol("sink", 0, 8), -1.0, None, ALU.mult))
                VE.after(t)
                units, held = [], {}
                for qt in range(2):
                    for h in range(4):
                        def scores(banks, qt=qt, h=h):
                            if h == 0:
                                held["n"], held["w"] = take(ROW["alibi"] + qt)
                            for g in range(2):
                                r = slice(64 * g, 64 * g + 64)
                                o = ps[:, banks[g], 0:T]
                                pe.matmul(o, q[r, h, qt * P:(qt + 1) * P], k[r, :], start=True, stop=False)
                                mm = pe.matmul(o, ident, held["w"][:, (2 * h + g) * T:(2 * h + g + 1) * T],
                                               start=False, stop=True)
                            t = PE.mark(mm)
                            if h == 3:
                                release(held["n"], t)
                            return t
                        units.append(dict(
                            scores=scores, G=2, halves=(0, 1), new_o=True, end_o=True,
                            sink=[pcol("sink", 2 * h + g) for g in range(2)], nsink=nsink[:, 2 * h:2 * h + 2],
                            v=lambda kc, g: v[:, kc, 64 * g:64 * g + 64], o=y[:, h, qt * P:(qt + 1) * P]))
                join()
                attention("ab", units)

                for t_ in range(4):
                    s = None
                    for tap in range(4):
                        xs = bx[:, t_, tap:tap + T]
                        wt = pcol("b_cw", tap * 4 + t_)
                        if tap == 0:
                            s = VE.mark(dve.tensor_scalar(xb[:, t_, :], xs, wt, pcol("b_cb", t_), ALU.mult, ALU.add))
                        else:
                            VE.after(s)
                            s = VE.mark(dve.scalar_tensor_tensor(xb[:, t_, :], xs, wt, xb[:, t_, :],
                                                                 ALU.mult, ALU.add))
                hba, hbx, sp, e1, c4 = (cols[:, 8 + 4 * j:12 + 4 * j] for j in range(5))
                VE.mark(dve.tensor_scalar(hba, pcol("b_ba", 0, 4), 0.5, None, ALU.mult))
                t = VE.mark(dve.tensor_scalar(hbx, pcol("b_bx", 0, 4), 0.5, None, ALU.mult))
                c4t = softplus_cols(pcol("b_lam", 0, 4), -1.0, sp, e1, cols[:, 28:32], P)
                VE.after(c4t)
                t = VE.mark(dve.tensor_scalar(c4, sp, -4.0, None, ALU.mult))
                PE.after(t, (s_in[5], 16))
                AC.after(t)
                for w_i, (dst, hb) in enumerate(((tr, hba), (ti, hbx))):
                    for t_ in range(4):
                        b = bank()
                        m = PE.mark(pe.matmul(ps[:, b, 0:T], wab_sb[:, 4 * w_i + t_, :], xb[:, t_, :],
                                              start=True, stop=True))
                        AC.after(m)
                        bank_free[b] = [AC.mark(act.activation(dst[:, t_, :], ps[:, b, 0:T], ACT.Tanh,
                                                               bias=hb[:, t_:t_ + 1], scale=0.5))]
                la, a_, m1 = alloc(st, "ab_la", [4, T]), alloc(st, "ab_a", [4, T]), alloc(st, "ab_m1", [4, T])
                VE.after(AC.last())
                for t_ in range(4):
                    t = VE.mark(dve.tensor_scalar(la[:, t_, :], tr[:, t_, :], 1.0, c4[:, t_:t_ + 1], ALU.add, ALU.mult))
                AC.after(t)
                AC.mark(act.activation(a_[:, :, :], la[:, :, :], ACT.Exp))
                t = AC.mark(act.activation(tr[:, :, :], la[:, :, :], ACT.Tanh))
                VE.after(t)
                t = VE.mark(dve.tensor_scalar(m1[:, :, :], tr[:, :, :], -1.0, 1.0, ALU.mult, ALU.add))
                VE.after(t)
                t = VE.mark(dve.reciprocal(la[:, :, :], m1[:, :, :]))
                VE.after(t)
                t = VE.mark(dve.scalar_tensor_tensor(m1[:, :, :], tr[:, :, :], -2.0, la[:, :, :], ALU.mult, ALU.mult))
                AC.after(t)
                t = AC.mark(act.activation(la[:, :, :], m1[:, :, :], ACT.Sqrt))
                VE.after(t)
                t = VE.mark(dve.scalar_tensor_tensor(m1[:, :, :], ti[:, :, :], 1.0, xb[:, :, :], ALU.add, ALU.mult))
                VE.after(t)
                t = VE.mark(dve.scalar_tensor_tensor(m1[:, :, :], m1[:, :, :], 0.5, la[:, :, :], ALU.mult, ALU.mult))
                VE.after(t)
                for t_ in range(4):
                    t = VE.mark(dve.tensor_tensor_scan(tr[:, t_, :], a_[:, t_, :], m1[:, t_, :], 0.0,
                                                       ALU.mult, ALU.add))
                AC.after(t)
                s1 = AC.mark(act.activation(ti[:, :, :], bg[:, :, :], ACT.Square))
                VE.after(s1, t)
                g1 = VE.mark(dve.tensor_scalar(ti[:, :, :], ti[:, :, :], 0.044715, 1.0, ALU.mult, ALU.add))
                VE.after(g1)
                g1 = VE.mark(dve.tensor_tensor(ti[:, :, :], ti[:, :, :], bg[:, :, :], ALU.mult))
                AC.after(g1)
                g1 = AC.mark(act.activation(ti[:, :, :], ti[:, :, :], ACT.Tanh, scale=float(np.sqrt(2 / np.pi))))
                VE.after(g1)
                g1 = VE.mark(dve.scalar_tensor_tensor(bg[:, :, :], ti[:, :, :], 1.0, bg[:, :, :], ALU.add, ALU.mult))
                VE.after(g1)
                g1 = VE.mark(dve.scalar_tensor_tensor(y[:, 4:8, :], bg[:, :, :], 0.5, tr[:, :, :], ALU.mult, ALU.mult))
                PE.after(g1)
                evac, toks = add_branch(T, 1.0)
                feature_major(ROW["ab_out"], 8, KC, lambda c: y[:, c, :], T, evac)
                layer_norm(toks, 0, T, 1e-5, "ln_g01", "ln_b01")
                join()

        def softplus_cols(src, sign, dst, tmp, tmp2, rows):
            t = VE.mark(dve.tensor_scalar(dst, src, sign, None, ALU.mult))
            VE.after(t)
            t = VE.mark(dve.tensor_scalar(tmp, dst, -1.0, None, ALU.mult))
            VE.after(t)
            t = VE.mark(dve.tensor_tensor(tmp, tmp, dst, ALU.min))
            AC.after(t)
            t = AC.mark(act.activation(tmp2, tmp, ACT.Exp))
            VE.after(t)
            t = VE.mark(dve.tensor_scalar(tmp2, tmp2, 1.0, None, ALU.add))
            AC.after(t)
            t = AC.mark(act.activation(tmp, tmp2, ACT.Ln))
            VE.after(t)
            t = VE.mark(dve.tensor_scalar(dst, dst, 0.0, None, ALU.max))
            VE.after(t)
            return VE.mark(dve.tensor_tensor(dst, dst, tmp, ALU.add))

        def mixer_c():
            with ExitStack() as st:
                join()
                x = lambda c: X[:, c, 0:T]
                qkv = alloc(st, "c_qkv", [24, T])
                z = alloc(st, "c_z", [8, T])
                kbT = H
                o = qkv[:, 16:24, :]
                Kd = alloc(st, "c_kd", [8, 2, P])
                KB = alloc(st, "c_kb", [8, 2, P])
                VB = alloc(st, "c_vb", [8, 2, P])
                attnT = alloc(st, "c_at", [8, 2, P])
                Y = alloc(st, "c_Y", [8, 2, P])
                nWT = KB
                qg = alloc(st, "c_qg", [8, T])
                tcol = alloc(st, "c_tcol", [8, 8])
                glast = alloc(st, "c_gl", [8, 4])
                small = alloc(st, "c_small", [8])
                s1 = ExitStack()
                raw = alloc(s1, "c_raw", [4, T + 3])
                scaled_residual(0, T)
                pad = VE.mark(dve.memset(raw[:, :, 0:3], 0.0))
                AC.after(pad)
                raw_free = [None] * 4

                def evac_qkv(base):
                    def evac(t, tile, done):
                        g = base + t
                        AC.after(done, raw_free[g % 4])
                        r = raw[:, g % 4, :]
                        c = AC.mark(act.activation(r[:, 3:T + 3], tile, ACT.Copy))
                        VE.after(c)
                        dst = qkv[:, g, :]
                        s = VE.mark(dve.tensor_scalar(dst, r[:, 0:T], pcol("c_cw", g), None, ALU.mult))
                        for tap in range(1, 4):
                            VE.after(s)
                            s = VE.mark(dve.scalar_tensor_tensor(dst, r[:, tap:tap + T], pcol("c_cw", 24 * tap + g),
                                                                 dst, ALU.mult, ALU.add))
                        raw_free[g % 4] = s
                        AC.after(s)
                        AC.mark(act.activation(dst, dst, ACT.Silu))
                        return c
                    return evac
                feature_major(ROW["c_in"], 24, KC, x, T, evac_qkv(0))

                def evac_z(t, tile, done):
                    AC.after(done)
                    return AC.mark(act.activation(z[:, t, :], tile, ACT.Silu))
                feature_major(ROW["c_in"] + 12, 8, KC, x, T, evac_z)
                n, w = take(ROW["c_in"] + 16)
                w = w[:, 0:KC * 16].rearrange("p (c m) -> p c m", c=KC)
                b = bank()
                for part in range(2):
                    for c in range(KC):
                        mm = pe.matmul(ps[0:8, b, part * T:(part + 1) * T], w[:, c, 8 * part:8 * part + 8], x(c),
                                       start=(c == 0), stop=(c == KC - 1))
                t = PE.mark(mm)
                release(n, t)
                R = lambda i: (hT, sg)[i // 4][0:8, i % 4, :]
                AC.after(t)
                t0 = AC.mark(act.activation(R(0), ps[0:8, b, 0:T], ACT.Tanh, scale=0.5))
                VE.after(t0, t)
                t0 = VE.mark(dve.tensor_scalar(R(0), R(0), 1.0, 0.5, ALU.add, ALU.mult))
                t1 = VE.mark(dve.tensor_scalar(R(2), ps[0:8, b, T:2 * T], PV[0:8, PCOL["c_dt"]:PCOL["c_dt"] + 1], None,
                                               ALU.add))
                bank_free[b] = [t1]
                VE.after(t1)
                t1 = softplus_cols(R(2), 1.0, R(1), R(3), R(4), 8)
                ea = small[0:8, 0:1]
                t2 = AC.mark(act.activation(ea, PV[0:8, PCOL["c_alog"]:PCOL["c_alog"] + 1], ACT.Exp))
                VE.after(t1, t2)
                t1 = VE.mark(dve.tensor_scalar(R(1), R(1), ea, -1.0, ALU.mult, ALU.mult))
                VE.after(t1)
                one = small[0:8, 1:2]
                VE.mark(dve.memset(R(7), 1.0))
                VE.after(VE.last())
                for c in range(4):
                    cs = slice(c * CH, (c + 1) * CH)
                    t = VE.mark(dve.tensor_tensor_scan(R(2)[:, cs], R(7)[:, cs], R(1)[:, cs], 0.0,
                                                       ALU.mult, ALU.add))
                VE.after(t)
                for c in range(4):
                    cs = slice(c * CH, (c + 1) * CH)
                    t = VE.mark(dve.tensor_scalar(R(4)[:, cs], R(2)[:, cs],
                                                  R(2)[:, (c + 1) * CH - 1:(c + 1) * CH], -1.0,
                                                  ALU.subtract, ALU.mult))
                AC.after(t)
                AC.mark(act.activation(R(3), R(2), ACT.Exp))
                t = AC.mark(act.activation(R(4), R(4), ACT.Exp))
                VE.after(t)
                t = VE.mark(dve.tensor_tensor(R(5), R(0), R(3), ALU.mult))
                PE.after(t)
                b = bank()
                for j, r in enumerate((1, 0, 5, 4)):
                    for half in range(2):
                        mm = pe.transpose(ps[:, b, (2 * j + half) * 8:(2 * j + half + 1) * 8],
                                          R(r)[:, half * P:(half + 1) * P], ident[0:8, 0:8])
                t = PE.mark(mm)
                VE.after(t)
                t = VE.mark(dve.tensor_copy(tcol[:, :, :], ps[:, b, 0:64].rearrange("p (a h) -> p a h", a=8)))
                bank_free[b] = [t]
                tcol_ready = t
                col = lambda j, half, h: tcol[:, 2 * j + half, h:h + 1]

                join()
                s1.close()
                s1 = ExitStack()
                sq = alloc(s1, "c_sq", [4, T])
                rn = alloc(s1, "c_rn", [4, T])
                sq_free, rn_free = [None] * 4, [None] * 4
                for i in range(16):
                    j = i % 4
                    AC.after(sq_free[j])
                    s = AC.mark(act.activation(sq[:, j, :], qkv[:, i, :], ACT.Square))
                    VE.after(rn_free[j])
                    AC.after(rn_free[j])
                    r = rms_rows([(sq[:, j, :], s)], ones, T, 1e-6, rn[:, j, :])
                    sq_free[j] = r
                    VE.after(r)
                    rn_free[j] = VE.mark(dve.scalar_tensor_tensor(qkv[:, i, :], qkv[:, i, :], P ** -0.5 if i < 8 else 1.0,
                                                                  rn[:, j, :], ALU.mult, ALU.mult))
                join()
                s1.close()
                sel = lambda h: ident[0:8, h:h + 1].broadcast_to([8, P])
                for h in range(8):
                    b = bank()
                    pe.matmul(ps[:, b, 0:T], sel(h), R(0), start=True, stop=True)
                    t = PE.mark(pe.matmul(ps[:, b, T:2 * T], sel(h), R(3), start=True, stop=True))
                    VE.after(t)
                    VE.mark(dve.tensor_tensor(kbT[:, h, :], qkv[:, 8 + h, :], ps[:, b, 0:T], ALU.mult))
                    VE.mark(dve.tensor_copy(glast[:, h, :], ps[:, b, T + CH - 1:2 * T:CH]))
                    bank_free[b] = [VE.mark(dve.tensor_tensor(qg[:, h, :], qkv[:, h, :], ps[:, b, T:2 * T], ALU.mult))]
                for h in range(8):
                    b, b2 = bank(), bank()
                    for half in range(2):
                        ts_ = slice(half * P, (half + 1) * P)
                        pe.transpose(ps[:, b, half * P:(half + 1) * P], qkv[:, 8 + h, ts_], ident)
                        mm = pe.transpose(ps[:, b2, half * P:(half + 1) * P], qkv[:, 16 + h, ts_], ident)
                    t = PE.mark(mm)
                    VE.after(t)
                    AC.after(t)
                    for half in range(2):
                        kt = ps[:, b, half * P:(half + 1) * P]
                        vt = ps[:, b2, half * P:(half + 1) * P]
                        a = VE.mark(dve.tensor_scalar(KB[:, h, half, :], kt, col(2, half, h), None, ALU.mult))
                        a = VE.mark(dve.tensor_scalar(Kd[:, h, half, :], kt, col(3, half, h), None, ALU.mult))
                        a2 = AC.mark(act.activation(VB[:, h, half, :], vt, ACT.Copy, scale=col(1, half, h)))
                    bank_free[b], bank_free[b2] = [a], [a2]
                join()

                with ExitStack() as s2:
                    A4 = lambda nm: alloc(s2, nm, [4, P])
                    E, eD = A4("c_E"), A4("c_eD")
                    LT, L = A4("c_LT"), A4("c_L")
                    Pm, PTm = [A4("c_P0"), A4("c_P1")], [A4("c_PT0"), A4("c_PT1")]
                    Tm, Ym = A4("c_T"), A4("c_Yw")
                    B, BT = Pm[0], PTm[0]
                    M1, M2 = E, eD
                    wide = lambda m: m.unsqueeze(1).broadcast_to([P, 4, P])
                    full = lambda b: ps[:, b, :].rearrange("p (u n) -> p u n", u=4)

                    def products(lhs, rhs):
                        b = bank()
                        for u in range(4):
                            mm = pe.matmul(ps[:, b, u * P:(u + 1) * P], lhs(u), rhs(u), start=True, stop=True)
                        return b, PE.mark(mm)

                    def vchain(ins):
                        t = VE.mark(ins)
                        VE.after(t)
                        return t

                    for grp in range(4):
                        unit = lambda u: (2 * grp + u // 2, u % 2)
                        VE.after(VE.last(), PE.last(), AC.last())
                        AC.after(VE.last(), PE.last())
                        for u in range(4):
                            h, half = unit(u)
                            t = VE.mark(dve.tensor_scalar(E[:, u, :], const("upto"), col(0, half, h), None, ALU.mult))
                        PE.after(t, AC.last())
                        b = bank()
                        t = PE.mark(pe.matmul(ps[:, b, :], const("after"), E[:, :, :].rearrange("p u n -> p (u n)"),
                                              start=True, stop=True))
                        AC.after(t)
                        t = AC.mark(act.activation(eD[:, :, :], full(b), ACT.Exp))
                        bank_free[b] = [t]
                        VE.after(t)
                        vchain(dve.tensor_tensor(eD[:, :, :], eD[:, :, :], wide(const("upto")), ALU.mult))
                        tsl = lambda u: slice((u % 2) * P, (u % 2 + 1) * P)
                        hd = lambda u: 2 * grp + u // 2
                        b, t = products(lambda u: qkv[:, 8 + hd(u), tsl(u)], lambda u: qkv[:, hd(u), tsl(u)])
                        VE.after(t)
                        t = VE.mark(dve.tensor_tensor(
                            attnT[:, 2 * grp:2 * grp + 2, :, :].rearrange("p h a n -> p (h a) n"),
                            full(b), eD[:, :, :], ALU.mult))
                        bank_free[b] = [t]
                        b, t = products(lambda u: qkv[:, 8 + hd(u), tsl(u)], lambda u: kbT[:, hd(u), tsl(u)])
                        VE.after(t)
                        t = vchain(dve.tensor_tensor(LT[:, :, :], full(b), eD[:, :, :], ALU.mult))
                        bank_free[b] = [t]
                        t = vchain(dve.tensor_tensor(LT[:, :, :], LT[:, :, :], wide(const("before")), ALU.mult))
                        PE.after(t)
                        b = bank()
                        for u in range(4):
                            mm = pe.transpose(ps[:, b, u * P:(u + 1) * P], LT[:, u, :], ident)
                        t = PE.mark(mm)
                        AC.after(t)
                        t = AC.mark(act.activation(L[:, :, :], full(b), ACT.Copy))
                        bank_free[b] = [t]
                        VE.after(t)
                        p, pt = Pm[0], PTm[0]
                        VE.mark(dve.scalar_tensor_tensor(p[:, :, :], L[:, :, :], -1.0, wide(const("in16")),
                                                         ALU.mult, ALU.mult))
                        vchain(dve.scalar_tensor_tensor(pt[:, :, :], LT[:, :, :], -1.0, wide(const("in16")),
                                                        ALU.mult, ALU.mult))
                        VE.mark(dve.tensor_tensor(Tm[:, :, :], p[:, :, :], wide(ident), ALU.add))
                        t = vchain(dve.tensor_tensor(Ym[:, :, :], pt[:, :, :], wide(ident), ALU.add))
                        PE.after(t)
                        for step in range(3):
                            pn, ptn = Pm[(step + 1) % 2], PTm[(step + 1) % 2]
                            b1, t1 = products(lambda u: pt[:, u, :], lambda u: p[:, u, :])
                            b2, t2 = products(lambda u: p[:, u, :], lambda u: pt[:, u, :])
                            AC.after(t1)
                            a1 = AC.mark(act.activation(pn[:, :, :], full(b1), ACT.Copy))
                            VE.after(t2)
                            a2 = VE.mark(dve.tensor_copy(ptn[:, :, :], full(b2)))
                            bank_free[b1], bank_free[b2] = [a1], [a2]
                            PE.after(a1, a2)
                            b1, t1 = products(lambda u: ptn[:, u, :], lambda u: Tm[:, u, :])
                            b2, t2 = products(lambda u: pn[:, u, :], lambda u: Ym[:, u, :])
                            VE.after(t1, t2)
                            a1 = VE.mark(dve.tensor_tensor(Tm[:, :, :], Tm[:, :, :], full(b1), ALU.add))
                            a2 = VE.mark(dve.tensor_tensor(Ym[:, :, :], Ym[:, :, :], full(b2), ALU.add))
                            bank_free[b1], bank_free[b2] = [a1], [a2]
                            PE.after(a1, a2)
                            p, pt = pn, ptn
                        for m in ("in32", "in64"):
                            lastm = m == "in64"
                            VE.after(PE.last(), VE.last())
                            VE.mark(dve.tensor_tensor(B[:, :, :], L[:, :, :], wide(const(m)), ALU.mult))
                            t = VE.mark(dve.tensor_tensor(BT[:, :, :], LT[:, :, :], wide(const(m)), ALU.mult))
                            PE.after(t)
                            b1, t1 = products(lambda u: B[:, u, :], lambda u: Ym[:, u, :])
                            AC.after(t1)
                            a1 = AC.mark(act.activation(M1[:, :, :], full(b1), ACT.Copy))
                            bank_free[b1] = [a1]
                            if not lastm:
                                b2, t2 = products(lambda u: BT[:, u, :], lambda u: Tm[:, u, :])
                                VE.after(t2)
                                a2 = VE.mark(dve.tensor_copy(M2[:, :, :], full(b2)))
                                bank_free[b2] = [a2]
                                PE.after(a2)
                            PE.after(a1)
                            b1, t1 = products(lambda u: Tm[:, u, :], lambda u: M1[:, u, :])
                            if not lastm:
                                b2, t2 = products(lambda u: Ym[:, u, :], lambda u: M2[:, u, :])
                            VE.after(t1, t2)
                            dst = (Y[:, 2 * grp:2 * grp + 2, :, :].rearrange("p h a n -> p (h a) n") if lastm
                                   else Ym[:, :, :])
                            a1 = VE.mark(dve.tensor_tensor(dst, Ym[:, :, :], full(b1), ALU.subtract))
                            bank_free[b1] = [a1]
                            if not lastm:
                                a1 = VE.mark(dve.tensor_tensor(Tm[:, :, :], Tm[:, :, :], full(b2), ALU.subtract))
                                bank_free[b2] = [a1]
                            PE.after(a1)
                        b, t = products(lambda u: KB[:, hd(u), u % 2, :], lambda u: Y[:, hd(u), u % 2, :])
                        AC.after(t)
                        t = AC.mark(act.activation(nWT[:, 2 * grp:2 * grp + 2, :, :].rearrange("p h a n -> p (h a) n"),
                                                   full(b), ACT.Copy, scale=-1.0))
                        bank_free[b] = [t]
                    join()

                s1 = ExitStack()
                S = alloc(s1, "c_S", [8, P])
                vn = alloc(s1, "c_vn", [8, P])
                for c in range(4):
                    half, p0 = c // 2, CH * (c % 2)
                    r = slice(p0, p0 + CH)
                    for g in range(2):
                        hs = slice(4 * g, 4 * g + 4)
                        b = bank()
                        PE.after(VE.last(), AC.last())
                        for j in range(4):
                            h = 4 * g + j
                            ov = ps[r, b, j * P:(j + 1) * P]
                            mm = pe.matmul(ov, Y[:, h, half, r], VB[:, h, half, :], start=True, stop=(c == 0))
                            if c:
                                mm = pe.matmul(ov, nWT[:, h, half, r], S[:, h, :], start=False, stop=True)
                        t = PE.mark(mm)
                        AC.after(t)
                        a = AC.mark(act.activation(vn[r, hs, :],
                                                   ps[r, b, :].rearrange("p (h n) -> p h n", h=4), ACT.Copy))
                        bank_free[b] = [a]
                        PE.after(a)
                        bo, bs = bank(), bank()
                        for j in range(4):
                            h = 4 * g + j
                            oo = ps[:, bo, j * CH:(j + 1) * CH]
                            if c:
                                pe.matmul(oo, S[:, h, :], qg[:, h, c * CH:(c + 1) * CH], start=True, stop=False)
                            pe.matmul(oo, vn[r, h, :], attnT[r, h, half, r], start=(c == 0), stop=True)
                        for j in range(4):
                            h = 4 * g + j
                            mm = pe.matmul(ps[:, bs, j * P:(j + 1) * P], Kd[r, h, half, :], vn[r, h, :],
                                           start=True, stop=True)
                        t = PE.mark(mm)
                        AC.after(t)
                        bank_free[bo] = [AC.mark(act.activation(
                            o[:, hs, c * CH:(c + 1) * CH],
                            ps[:, bo, 0:4 * CH].rearrange("p (h n) -> p h n", h=4), ACT.Copy))]
                        VE.after(t)
                        for j in range(4):
                            h = 4 * g + j
                            if c == 0:
                                t = VE.mark(dve.tensor_copy(S[:, h, :], ps[:, bs, j * P:(j + 1) * P]))
                            else:
                                t = VE.mark(dve.scalar_tensor_tensor(S[:, h, :], S[:, h, :], glast[:, h, c:c + 1],
                                                                     ps[:, bs, j * P:(j + 1) * P], ALU.mult, ALU.add))
                        bank_free[bs] = [t]
                join()
                s1.close()
                sq = alloc(st, "c_sq2", [4, T])
                rn = alloc(st, "c_rn2", [4, T])
                sq_free, rn_free = [None] * 4, [None] * 4
                for h in range(8):
                    j = h % 4
                    AC.after(sq_free[j])
                    s = AC.mark(act.activation(sq[:, j, :], o[:, h, :], ACT.Square, scale=P ** -0.5))
                    VE.after(rn_free[j])
                    AC.after(rn_free[j])
                    rt = rms_rows([(sq[:, j, :], s)], ones, T, 1e-6, rn[:, j, :])
                    sq_free[j] = rt
                    VE.after(rt)
                    t = VE.mark(dve.scalar_tensor_tensor(o[:, h, :], o[:, h, :], pcol("c_ng"), rn[:, j, :],
                                                         ALU.mult, ALU.mult))
                    rn_free[j] = t
                    VE.after(t)
                    t = VE.mark(dve.tensor_tensor(o[:, h, :], o[:, h, :], z[:, h, :], ALU.mult))
                PE.after(t)
                evac, toks = add_branch(T, 1.0)
                feature_major(ROW["c_out"], 8, KC, lambda c: o[:, c, :], T, evac)
                layer_norm(toks, 0, T, 1e-5, "ln_g11", "ln_b11")
                join()

        def ple(i):
            with ExitStack() as st:
                join()
                pp = alloc(st, f"ple_pp{i}", [8, T])
                th = alloc(st, f"ple_th{i}", [8, T])
                hb = alloc(st, f"ple_hb{i}", [8])
                t0 = VE.mark(dve.tensor_scalar(hb[:, :], pcol(f"ple_b{i}", 0, 8), 0.5, None, ALU.mult))
                AC.after(t0)

                def evac_p(t, tile, done):
                    VE.after(done)
                    return VE.mark(dve.tensor_copy(pp[:, t, :], tile))
                feature_major(ROW[f"ple_p_{i}"], 8, 2, lambda c: PT_[:, i, c, :], T, evac_p, per_slot=8)

                def evac_g(t, tile, done):
                    AC.after(done)
                    return AC.mark(act.activation(th[:, t, :], tile, ACT.Tanh, scale=0.5, bias=hb[:, t:t + 1]))
                feature_major(ROW[f"ple_g_{i}"], 8, KC, lambda c: X[:, c, 0:T], T, evac_g)
                VE.after(VE.last(), AC.last())
                PE.after(AC.last())
                for t in range(8):
                    a = VE.mark(dve.scalar_tensor_tensor(th[:, t, :], th[:, t, :], 1.0, pp[:, t, :], ALU.add, ALU.mult))
                    VE.after(a, PE.last())
                    VE.mark(dve.scalar_tensor_tensor(X[:, t, 0:T], th[:, t, :], 0.5, X[:, t, 0:T], ALU.mult, ALU.add))
                join()

        def adaln():
            with ExitStack() as st:
                join()
                cs = alloc(st, "cond_s", [KC, 2])
                t = AC.mark(act.activation(cs[:, :, :], pcol("cond", 0, 16).rearrange("p (c j) -> p c j", j=2), ACT.Silu))
                PE.after(t)
                for layer in range(2):
                    b = bank()
                    for t_ in range(48):
                        if t_ % 2 == 0:
                            n, w = take(ROW[f"ada_{layer}"] + t_ // 2)
                            w = w.rearrange("p (c m) -> p c m", c=KC)
                        for c in range(KC):
                            mm = pe.matmul(ps[:, b, 2 * t_:2 * t_ + 2], w[:, c, (t_ % 2) * P:(t_ % 2 + 1) * P],
                                           cs[:, c, :], start=(c == 0), stop=(c == KC - 1))
                        if t_ % 2 == 1:
                            m = PE.mark(mm)
                            release(n, m)
                    VE.after(m)
                    t = VE.mark(dve.tensor_tensor(MOD[:, layer, :, :], ps[:, b, 0:96].rearrange("p (t j) -> p t j", j=2),
                                                  pcol(f"ada_b{layer}", 0, 48).unsqueeze(2).broadcast_to([P, 48, 2]),
                                                  ALU.add))
                    bank_free[b] = [t]
                    VE.after(t)
                    for part in (1, 4):
                        m_ = MOD[:, layer, 8 * part:8 * part + 8, :]
                        VE.mark(dve.tensor_scalar(m_, m_, 1.0, None, ALU.add))
                join()

        def modulate(layer, part, n0s, ready):
            VE.after(*ready)
            for j in n0s:
                for c in range(KC):
                    t = VE.mark(dve.tensor_scalar(H[:, c, j * T:(j + 1) * T], X[:, c, j * T:(j + 1) * T],
                                                  MOD[:, layer, 8 * (part + 1) + c, j:j + 1],
                                                  MOD[:, layer, 8 * part + c, j:j + 1], ALU.mult, ALU.add))
            return t

        def head_norm(st, tag):
            sq = alloc(st, f"{tag}_sq", [2, 2 * T])
            rn = alloc(st, f"{tag}_rn", [2, 2 * T])
            turn = [0]
            free = [None, None]

            def norm(dst, tile, done, gain, scale):
                j = turn[0] % 2
                turn[0] += 1
                N = 2 * T
                AC.after(done, free[j])
                s = AC.mark(act.activation(sq[:, j, 0:N], tile, ACT.Square))
                VE.after(free[j])
                r = rms_rows([(sq[:, j, 0:N], s)], const("mean64"), N, 1e-6, rn[:, j, 0:N])
                VE.after(r)
                t = VE.mark(dve.scalar_tensor_tensor(dst, tile, gain, rn[:, j, 0:N], ALU.mult, ALU.mult))
                free[j] = t
                if scale != 1.0:
                    VE.after(t)
                    t = VE.mark(dve.tensor_scalar(dst, dst, scale, None, ALU.mult))
                return t
            return norm

        def even_mixer():
            with ExitStack() as st:
                join()
                qA = alloc(st, "e_qA", [4, 2 * T])
                kA = alloc(st, "e_kA", [2 * T])
                vA = alloc(st, "e_vA", [4, P])
                qB = alloc(st, "e_qB", [4, 2 * T])
                kB = alloc(st, "e_kB", [4, 2 * T])
                vB = alloc(st, "e_vB", [4, 512])
                y = alloc(st, "e_y", [8, 2 * T])
                t = modulate(0, 0, (0, 1), [])
                scaled_residual(0, 2 * T)
                PE.after(t)
                src = lambda c: H[:, c, :]
                with ExitStack() as s2:
                    norm = head_norm(s2, "e")
                    tmp = alloc(s2, "e_tmp", [T])

                    def evac_qA(t, tile, done):
                        return norm(qA[:, t, :], tile, done, pcol("q_gain"), 0.125)
                    feature_major(ROW["l0_in"], 4, KC, src, 2 * T, evac_qA)
                    n, w = take(ROW["l0_in"] + 2)
                    w = w.rearrange("p (c m) -> p c m", c=KC)
                    b = bank()
                    for c in range(KC):
                        mm = pe.matmul(ps[:, b, :], w[:, c, 0:P], src(c), start=(c == 0), stop=(c == KC - 1))
                    bank_free[b] = [norm(kA[:, :], ps[:, b, :], PE.mark(mm), pcol("k_gain"), 1.0)]
                    lhs = lambda c, tt: H[:, c, tt * P:(tt + 1) * P]
                    release(n, token_major(w[:, :, P:2 * P], KC, lhs, 4, P, lambda tt: vA[:, tt, :]))
                    for t in range(4):
                        rope(qA[:, t, 0:T], const("cosA"), const("sinA"), tmp[:, :], VE.last())
                    rope(kA[:, 0:T], const("cosA"), const("sinA"), tmp[:, :], VE.last())

                def evac(dst, scale):
                    def f(t, tile, done):
                        AC.after(done)
                        return AC.mark(act.activation(dst[:, t, :], tile, ACT.Copy, scale=scale))
                    return f
                feature_major(ROW["l0_in"] + 3, 4, KC, src, 2 * T, evac(qB, 0.125))
                feature_major(ROW["l0_in"] + 5, 4, KC, src, 2 * T, evac(kB, 1.0))
                for s_ in range(2):
                    n, w = take(ROW["l0_in"] + 7 + s_)
                    w = w.rearrange("p (c m) -> p c m", c=KC)
                    release(n, token_major(w, KC, lhs, 4, T, lambda tt: vB[:, tt, s_ * T:(s_ + 1) * T]))
                join()
                units, held = [], {}

                def unit512(q, k, v, vcol, h, g, qt, bias):
                    def scores(banks):
                        bk = banks[0]
                        if bias and h == 0 and g == 0:
                            held["n"], held["w"] = take(ROW["rpb"] + qt)
                        r = slice(64 * g, 64 * g + 64)
                        mm = pe.matmul(ps[:, bk, :], q[r, h, qt * P:(qt + 1) * P], k(r), start=True, stop=True)
                        if bias:
                            i = 2 * h + g
                            mm = pe.matmul(ps[:, bk, 0:T], ident, held["w"][:, i * T:(i + 1) * T],
                                           start=False, stop=True, skip_group_check=True)
                        t = PE.mark(mm)
                        if bias and h == 3 and g == 1:
                            release(held["n"], t)
                        return t
                    return scores

                for qt in range(2):
                    for h in range(4):
                        for g in range(2):
                            units.append(dict(
                                scores=unit512(qA, lambda r: kA[r, :], None, None, h, g, qt, False), G=1, halves=(g,),
                                new_o=(g == 0), end_o=(g == 1), sink=None,
                                v=lambda kc, _, g=g: vA[:, kc, 64 * g:64 * g + 64], o=y[:, h, qt * P:(qt + 1) * P]))
                for qt in range(2):
                    for h in range(4):
                        for g in range(2):
                            units.append(dict(
                                scores=unit512(qB, lambda r, h=h: kB[r, h, :], None, None, h, g, qt, True), G=1,
                                halves=(g,), new_o=(g == 0), end_o=(g == 1), sink=None,
                                v=lambda kc, _, g=g, h=h: vB[:, kc, (2 * h + g) * 64:(2 * h + g) * 64 + 64],
                                o=y[:, 4 + h, qt * P:(qt + 1) * P]))
                attention("e", units)
                units = []
                for kind in range(2):
                    for qt in range(2):
                        for h in range(4):
                            def scores(banks, kind=kind, qt=qt, h=h):
                                q = (qA, qB)[kind]
                                for g in range(2):
                                    r = slice(64 * g, 64 * g + 64)
                                    kk = kA[r, T:2 * T] if kind == 0 else kB[r, h, T:2 * T]
                                    mm = pe.matmul(ps[:, banks[g], 0:T], q[r, h, T + qt * P:T + (qt + 1) * P],
                                                   kk, start=True, stop=True)
                                return PE.mark(mm)
                            if kind == 0:
                                v = lambda kc, g: vA[:, 2 + kc, 64 * g:64 * g + 64]
                            else:
                                v = lambda kc, g, h=h: vB[:, 2 + kc, (2 * h + g) * 64:(2 * h + g) * 64 + 64]
                            units.append(dict(scores=scores, G=2, halves=(0, 1), new_o=True, end_o=True, sink=None, v=v,
                                              o=y[:, 4 * kind + h, T + qt * P:T + (qt + 1) * P]))
                attention("f", units)
                add, toks = add_branch(2 * T, lambda c, j: MOD[:, 0, 16 + c, j:j + 1])
                feature_major(ROW["l0_out"], 8, KC, lambda c: y[:, c, :], 2 * T, add)
                layer_norm(toks, 0, 2 * T, 1e-6, "l0_ln1g", "l0_ln1b")
                join()

        def conv_ffn(layer, j):
            t = modulate(layer, 3, (j,), [AC.last()])
            AC.after(t)
            scaled_residual(j * T, T)
            done = ffn(f"l{layer}_ffn", lambda c, n: H[:, c:c + n, j * T:(j + 1) * T], conv=layer)
            toks = ffn_residual(j * T, done, lambda c: MOD[:, layer, 40 + c, j:j + 1])
            layer_norm(toks, j * T, T, 1e-6, f"l{layer}_ln2g", f"l{layer}_ln2b")

        def odd_mixer():
            with ExitStack() as st:
                join()
                q = alloc(st, "m_q", [MLA_H, T])
                k = alloc(st, "m_k", [MLA_H, 2 * T])
                v = alloc(st, "m_v", [4, MLA_H * 64])
                t = modulate(1, 0, (0, 1), [])
                scaled_residual(0, T)
                PE.after(t)
                with ExitStack() as s2:
                    two = lambda buf: buf[:, :, :].rearrange("p (a b) n -> p a (b n)", a=2)
                    cq, cq_sq = x1[:, 0:6, :], Z[:, 0:6, T:2 * T]
                    ckv, ckv_sq, rq = two(sg), two(hT), two(cg)
                    kr = alloc(s2, "m_kr", [2 * T])
                    qr = alloc(s2, "m_qr", [4, T])
                    tmp = alloc(s2, "m_tmp", [T])

                    def evac(dst, sq):
                        def f(t, tile, done):
                            AC.after(done)
                            AC.mark(act.activation(sq[:, t, :], tile, ACT.Square))
                            return AC.mark(act.activation(dst[:, t, :], tile, ACT.Copy))
                        return f

                    def normalise(dst, sq, N, n_tiles, gain, i):
                        b = bank()
                        PE.after(AC.last())
                        for c in range(n_tiles):
                            mm = pe.matmul(ps[:, b, 0:N], ones, sq[:, c, :], start=(c == 0), stop=(c == n_tiles - 1))
                        t = PE.mark(mm)
                        VE.after(t)
                        t = VE.mark(dve.tensor_scalar(rq[:, i, 0:N], ps[:, b, 0:N], 1.0 / (n_tiles * P), 1e-6,
                                                      ALU.mult, ALU.add))
                        bank_free[b] = [t]
                        AC.after(t)
                        t = AC.mark(act.activation(rq[:, i, 0:N], rq[:, i, 0:N], ACT.Ln))
                        AC.after(t)
                        t = AC.mark(act.activation(rq[:, i, 0:N], rq[:, i, 0:N], ACT.Exp, scale=-0.5))
                        VE.after(t)
                        for c in range(n_tiles):
                            t = VE.mark(dve.scalar_tensor_tensor(dst[:, c, :], dst[:, c, :], pcol(gain, c), rq[:, i, 0:N],
                                                                 ALU.mult, ALU.mult))
                        return t
                    feature_major(ROW["l1_in"], 6, KC, lambda c: H[:, c, 0:T], T, evac(cq, cq_sq))
                    t = normalise(cq, cq_sq, T, 6, "cq_gain", 0)
                    AC.after(PE.last())
                    feature_major(ROW["l1_in"] + 3, 2, KC, lambda c: H[:, c, :], 2 * T, evac(ckv, ckv_sq))

                    def evac_kr(t, tile, done):
                        AC.after(done)
                        return AC.mark(act.activation(kr[0:ROPE, :], tile, ACT.Copy))
                    feature_major(ROW["l1_in"] + 4, 1, KC, lambda c: H[:, c, :], 2 * T, evac_kr, per_slot=1, M=ROPE)
                    t = normalise(ckv, ckv_sq, 2 * T, 2, "ckv_gain", 1)
                    b = bank()
                    PE.after(AC.last(), t)
                    t = PE.mark(pe.matmul(ps[0:ROPE, b, 0:T], const("rot")[0:ROPE, 0:ROPE], kr[0:ROPE, 0:T],
                                          start=True, stop=True))
                    VE.after(t)
                    a = VE.mark(dve.tensor_tensor(tmp[0:ROPE, :], ps[0:ROPE, b, 0:T], const("sinM")[0:ROPE, :], ALU.mult))
                    bank_free[b] = [a]
                    c_ = VE.mark(dve.tensor_tensor(kr[0:ROPE, 0:T], kr[0:ROPE, 0:T], const("cosM")[0:ROPE, :], ALU.mult))
                    VE.after(c_)
                    a = VE.mark(dve.tensor_tensor(kr[0:ROPE, 0:T], kr[0:ROPE, 0:T], tmp[0:ROPE, :], ALU.add))
                    VE.after(a)
                    VE.mark(dve.tensor_copy(k[NOPE:NOPE + ROPE, :, :],
                                            kr[0:ROPE, :].unsqueeze(1).broadcast_to([ROPE, MLA_H, 2 * T])))
                    scale = float((NOPE + ROPE) ** -0.5)

                    def split_heads(dst, scale):
                        def f(t, tile, done):
                            AC.after(done)
                            VE.after(done)
                            a = AC.mark(act.activation(dst[0:NOPE, 2 * t, :], tile[0:64, :], ACT.Copy, scale=scale))
                            if scale == 1.0:
                                b_ = VE.mark(dve.tensor_copy(dst[0:NOPE, 2 * t + 1, :], tile[64:128, :]))
                            else:
                                b_ = VE.mark(dve.tensor_scalar(dst[0:NOPE, 2 * t + 1, :], tile[64:128, :], scale, None,
                                                               ALU.mult))
                            return [a, b_]
                        return f
                    VE.after(VE.last())
                    feature_major(ROW["l1_uq"], 8, 6, lambda c: cq[:, c, :], T, split_heads(q, scale))

                    def evac_qr(t, tile, done):
                        AC.after(done)
                        return AC.mark(act.activation(qr[:, t, :], tile, ACT.Copy, scale=scale))
                    feature_major(ROW["l1_uq"] + 4, 4, 6, lambda c: cq[:, c, :], T, evac_qr)
                    VE.after(VE.last())
                    for t_ in range(4):
                        r = rope(qr[:, t_, :], const("cosM"), const("sinM"), tmp[:, :], AC.last())
                        VE.after(r)
                        for j in range(4):
                            VE.mark(dve.tensor_copy(q[NOPE:NOPE + ROPE, 4 * t_ + j, :], qr[32 * j:32 * j + 32, t_, :]))
                    feature_major(ROW["l1_ukv"], 8, 2, lambda c: ckv[:, c, :], 2 * T, split_heads(k, 1.0), per_slot=8)
                    n, w = take(ROW["l1_ukv"] + 1)
                    w = w.rearrange("p (c m) -> p c m", c=2)
                    for s_ in range(2):
                        t = token_major(w[:, :, s_ * 512:(s_ + 1) * 512], 2, lambda c, tt: ckv[:, c, tt * P:(tt + 1) * P],
                                        4, 512, lambda tt: v[:, tt, s_ * 512:(s_ + 1) * 512])
                    release(n, t)
                    join()
                y = x1
                units = []
                for qt in range(2):
                    for h in range(MLA_H):
                        def scores(banks, qt=qt, h=h):
                            return PE.mark(pe.matmul(ps[:, banks[0], :], q[0:96, h, qt * P:(qt + 1) * P], k[0:96, h, :],
                                                     start=True, stop=True))
                        units.append(dict(scores=scores, G=1, halves=(h % 2,), new_o=(h % 2 == 0), end_o=(h % 2 == 1),
                                          sink=None, v=lambda kc, _, h=h: v[:, kc, 64 * h:64 * h + 64],
                                          o=y[:, h // 2, qt * P:(qt + 1) * P]))
                attention("m", units)
                add, toks = add_branch(T, lambda c, j: MOD[:, 1, 16 + c, j:j + 1])
                feature_major(ROW["l1_out"], 8, KC, lambda c: y[:, c, :], T, add)
                layer_norm(toks, 0, T, 1e-6, "l1_ln1g", "l1_ln1b")
                join()

        def swiglu_layer(name, g, b):
            scaled_residual(0, T)
            done = ffn(name, lambda c, n: X[:, c:c + n, 0:T])
            toks = ffn_residual(0, done, 0.5)
            layer_norm(toks, 0, T, 1e-5, g, b)

        x1 = None

        def enter_block_2():
            nonlocal X, Z, H, x1
            join()
            block_1.close()
            x1 = X
            X, Z, H = alloc(top, "X2", [KC, 2 * T]), alloc(top, "Z2", [KC, 2 * T]), alloc(top, "H2", [KC, 2 * T])
            act.dma_start(X[:, :, T:2 * T], cin).then_inc(s_in[4], 16)
            AC.mark(act.activation(X[:, :, 0:T], x1[:, :, :], ACT.Copy))
            adaln()
            for lane in (PE, AC, VE):
                lane.after((s_in[4], 16))

        stages = []
        for i in range(2):
            stages += [lambda i=i: swiglu_layer(f"ffn1_{i}", f"ln_g{i}0", f"ln_b{i}0"),
                       (mixer_ab, mixer_c)[i],
                       lambda i=i: swiglu_layer(f"ffn2_{i}", f"ln_g{i}2", f"ln_b{i}2"),
                       lambda i=i: ple(i)]
        stages += [enter_block_2, even_mixer, lambda: conv_ffn(0, 0), lambda: conv_ffn(0, 1), odd_mixer, lambda: conv_ffn(1, 0)]
        for stage in stages[START:STOP]:
            stage()
        join()

        sp = nc.sync

        def load(n, row, turns=0):
            src = wstream[bass.ds(row + turns * 6, 1), :, :].rearrange("a p n -> p (a n)")
            sp.dma_start(ring[:, n % RING, :], src).then_inc(s_load[n % RING], 16)

        n = 0
        waited = {}
        while n < len(ring_log):
            if n in ffn_at:
                base, row = ffn_at[n]
                for p in range(2):
                    for k in range(3):
                        if n + 3 * p + k >= RING:
                            sp.wait_ge(*ring_log[n + 3 * p + k - RING][1])
                        load(n + 3 * p + k, row + 3 * p + k)
                with nc.Fori(0, (NPAIR - 3) // 2, engines=(ENG.SP,)) as it:
                    for p in range(2):
                        for k in range(3):
                            sp.wait_ge(s_wl[k], it * 4 + (base + 2 * p + 2))
                            load(n + 3 * p + k, row + 6 + 3 * p + k, turns=it)
                p = NPAIR - 1
                for k in range(3):
                    sp.wait_ge(*ring_log[n + 3 * p + k - RING][1])
                    load(n + 3 * p + k, row + 3 * p + k)
                n += 3 * NPAIR
            else:
                if n >= RING:
                    sp.wait_ge(*ring_log[n - RING][1])
                load(n, ring_log[n][0])
                n += 1
        s_out = new_sem("s_out")
        for tok in final:
            if tok is not None:
                sp.wait_ge(*tok)
        sp.dma_start(out, X[:, :, 0:T]).then_inc(s_out, 16)
        sp.wait_ge(s_out, 16)


START, STOP = 0, 99


def _features(w):
    return w.reshape(w.shape[0] // P, P, w.shape[1]).transpose(1, 0, 2)


def _slots(dst, w, width):
    f = _features(w)
    for j in range(0, w.shape[1], width):
        part = f[:, :, j:j + width].reshape(P, -1)
        dst[j // width, :, 0:part.shape[1]] = part


def _ffn_slots(dst, wg, wu, wd):
    for p in range(NPAIR):
        cols = slice(p * 2 * P, (p + 1) * 2 * P)
        dst[3 * p] = _features(wg[:, cols]).reshape(P, -1)
        dst[3 * p + 1] = _features(wu[:, cols]).reshape(P, -1)
        dst[3 * p + 2] = _features(wd[cols, :]).reshape(P, -1)


def _pair_heads(n_rest):
    return np.concatenate([np.arange(h * 64, h * 64 + 64) for h in PAIRED] + [512 + np.arange(n_rest)])


def _alibi():
    q, k = np.arange(T)[:, None], np.arange(T)[None, :]
    inside = (k // CH <= q // CH) & (k // CH >= q // CH - 2)
    slopes = 2.0 ** (-8.0 * np.arange(1, HEADS + 1) / HEADS)
    b = np.where(inside[None], -slopes[:, None, None] * np.abs(q - k)[None], NEG)[PAIRED]
    return b.reshape(HEADS, 2, P, T).transpose(1, 2, 0, 3).reshape(2, P, HEADS * T).astype(np.float32)


def _neighbourhood(rpb):
    q, k = np.arange(T)[:, None], np.arange(T)[None, :]
    start = np.clip(q % 64 - 8, 0, 48)
    inside = (k % 64 >= start) & (k % 64 < start + 16)
    rows, cols = k // 64 - q // 64 + 7, np.where(inside, k % 64 - q % 64 + 15, 31)
    padded = np.concatenate([rpb, np.full(rpb.shape[:2] + (1,), NEG, rpb.dtype)], axis=2)
    b = padded[:, rows, cols]
    return b.reshape(HEADS, 2, P, T).transpose(1, 2, 0, 3).reshape(2, P, HEADS * T)


def _rope_tables(dim, copies):
    pos = np.arange(T)
    rows, cols = (pos // 64).astype(np.float32), (pos % 64).astype(np.float32)
    axis = dim // 2
    inv = (np.float32(10000.0) ** (-np.arange(0, axis, 2, dtype=np.float32) / np.float32(axis))).astype(np.float32)
    ang = np.concatenate([rows[:, None] * inv, cols[:, None] * inv], axis=-1)
    ang = np.tile(np.repeat(ang, 2, axis=1).T, (copies, 1))
    return np.cos(ang), np.sin(ang)


def _consts():
    c = np.zeros((P, N_CCOL), np.float32)

    def put(name, a):
        c[:, CCOL[name]:CCOL[name] + a.shape[1]] = a
    a, b = np.arange(P)[:, None], np.arange(P)[None, :]
    same = lambda n: a // n == b // n
    put("ident", np.eye(P))
    put("mean", np.full((P, P), 1.0 / D))
    put("ones", np.ones((P, P)))
    put("mean64", same(64) / 64.0)
    rot = np.zeros((P, P))
    even = np.arange(0, P, 2)
    rot[even + 1, even], rot[even, even + 1] = -1.0, 1.0
    put("rot", rot)
    for names, dim in ((("cosA", "sinA"), 64), (("cosM", "sinM"), ROPE)):
        for name, table in zip(names, _rope_tables(dim, P // dim)):
            put(name, table)
    put("after", same(CH) & (a > b))
    put("upto", same(CH) & (a <= b))
    put("before", same(CH) & (a < b))
    put("in16", same(16))
    put("in32", same(32) & ~same(16))
    put("in64", same(64) & ~same(32))
    return c


def _layout(x):
    w = np.zeros((N_ROWS, P, SLOT), np.float32)

    def rows(name):
        return w[ROW[name]:ROW[name] + dict(STREAM)[name]]
    for i in range(2):
        _ffn_slots(rows(f"ffn1_{i}"), x["ffn1_wg"][i], x["ffn1_wu"][i], x["ffn1_wd"][i])
        _ffn_slots(rows(f"ffn2_{i}"), x["ffn2_wg"][i], x["ffn2_wu"][i], x["ffn2_wd"][i])
        _slots(rows(f"ple_p_{i}"), x["ple_wp"][i], D)
        _slots(rows(f"ple_g_{i}"), x["ple_wg"][i], 2 * P)
        _slots(rows(f"ada_{i}"), x[f"l{i}_w_ada_2"], 2 * P)
        up = x[f"l{i}_w_up_2"]
        _ffn_slots(rows(f"l{i}_ffn"), up[:, 0:F], up[:, F:2 * F], x[f"l{i}_w_down_2"])
    _slots(rows("ab_in"), x["ab_w_in"][0][:, _pair_heads(1280)], 2 * P)
    rows("alibi")[:] = _alibi()
    _slots(rows("ab_out"), x["ab_w_out"][0][_pair_heads(512)], 2 * P)
    _slots(rows("c_in"), x["c_w_in"][0], 2 * P)
    _slots(rows("c_out"), x["c_w_out"][0], 2 * P)
    _slots(rows("l0_in"), x["l0_w_in_2"][:, _pair_heads(1792)], 2 * P)
    rows("rpb")[:] = _neighbourhood(x["l0_rpb_2"])
    _slots(rows("l0_out"), x["l0_w_out_2"][_pair_heads(512)], 2 * P)
    _slots(rows("l1_in")[0:4], x["l1_w_in_2"][:, 0:CQ + CKV], 2 * P)
    _slots(rows("l1_in")[4:5], x["l1_w_in_2"][:, CQ + CKV:], ROPE)
    uq = x["l1_w_uq_2"].reshape(CQ, MLA_H, NOPE + ROPE)
    _slots(rows("l1_uq")[0:4], uq[:, :, 0:NOPE].reshape(CQ, -1), 2 * P)
    _slots(rows("l1_uq")[4:6], uq[:, :, NOPE:].reshape(CQ, -1), 2 * P)
    ukv = x["l1_w_ukv_2"].reshape(CKV, MLA_H, 128)
    _slots(rows("l1_ukv")[0:1], ukv[:, :, 0:64].reshape(CKV, -1), D)
    _slots(rows("l1_ukv")[1:2], ukv[:, :, 64:].reshape(CKV, -1), D)
    _slots(rows("l1_out"), x["l1_w_out_2"], 2 * P)

    pv = np.zeros((P, N_PCOL), np.float32)

    def put(name, a):
        a = np.asarray(a).reshape(-1, P).T
        pv[:, PCOL[name]:PCOL[name] + a.shape[1]] = a
    for i in range(2):
        for k in range(3):
            put(f"ln_g{i}{k}", x["ln_g"][i, k])
            put(f"ln_b{i}{k}", x["ln_b"][i, k])
        put(f"ple_b{i}", x["ple_bg"][i])
        put(f"ada_b{i}", x[f"l{i}_b_ada_2"])
        for k in (1, 2):
            put(f"l{i}_ln{k}g", x[f"l{i}_ln{k}_g_2"])
            put(f"l{i}_ln{k}b", x[f"l{i}_ln{k}_b_2"])
        put(f"l{i}_cw", x[f"l{i}_conv_w_2"])
        put(f"l{i}_cb", x[f"l{i}_conv_b_2"])
    put("sink", np.repeat(x["a_sinks"][0][PAIRED], P))
    put("b_cw", x["b_conv_w"][0])
    put("b_cb", x["b_conv_b"][0])
    put("b_ba", x["b_ba"][0])
    put("b_bx", x["b_bx"][0])
    put("b_lam", x["b_lam"][0])
    put("c_cw", x["c_conv_w"][0])
    put("c_ng", x["c_norm_g"][0])
    pv[0:8, PCOL["c_alog"]] = x["c_a_log"][0]
    pv[0:8, PCOL["c_dt"]] = x["c_dt_bias"][0]
    both = np.stack([x["c_2"][0], x["c_ctx_2"]], axis=-1)
    pv[:, PCOL["cond"]:PCOL["cond"] + 16] = both.reshape(KC, P, 2).transpose(1, 0, 2).reshape(P, 16)
    put("q_gain", np.tile(x["l0_q_gain_2"], 2))
    put("k_gain", np.tile(x["l0_k_gain_2"], 2))
    put("cq_gain", x["l1_cq_gain_2"])
    put("ckv_gain", x["l1_ckv_gain_2"])

    gates = np.zeros((P, 8, P), np.float32)
    for which, name in enumerate(("b_wa", "b_wx")):
        for blk in range(8):
            r = slice(64 * (blk % 2), 64 * (blk % 2) + 64)
            gates[r, 4 * which + blk // 2, r] = x[name][0, blk]
    return dict(
        wstream=w, params=pv, consts=_consts(), xin=_features(x["x"][0].T), cin=_features(x["ctx_2"][0].T),
        pin=np.stack([_features(x["p"][i, 0].T) for i in range(2)], axis=1), wab=gates)


def kernel(**inputs):
    import concourse.bacc as bacc
    from concourse.bass_utils import run_bass_kernel_spmd

    arrays = {k: np.ascontiguousarray(v) for k, v in _layout({k: np.asarray(v) for k, v in inputs.items()}).items()}
    nc = bacc.Bacc("TRN2", target_bir_lowering=False, num_devices=1)
    args = [nc.dram_tensor(k, v.shape, F32, kind="ExternalInput").ap() for k, v in arrays.items()]
    out = nc.dram_tensor("out", [P, KC, T], F32, kind="ExternalOutput").ap()
    build_program(nc, *args, out)
    got = run_bass_kernel_spmd(nc, [arrays], core_ids=[0]).results[0]["out"]
    return got.transpose(2, 1, 0).reshape(1, T, D)
```

```python
from contextlib import ExitStack

import numpy as np

import concourse.bass as bass
from concourse import mybir

F32 = mybir.dt.float32
F32R = mybir.dt.float32r
ACT = mybir.ActivationFunctionType
ALU = mybir.AluOpType
AX = mybir.AxisListType
ENG = mybir.EngineType

P = 128
D = 1024
KC = D // P
T = 256
F = 2816
NT = F // P
NPAIR = NT // 2
CH = 64
SLOT = 2048
RING = 6
START_FILL = 5
LN_FILL = 2
ALPHA = 4.0 ** 0.25
NEG = -1e30
HEADS = 8
PAIRED = [h for t in range(4) for h in (t, t + 4)]
MLA_H, NOPE, ROPE = 16, 64, 32
CQ, CKV = 768, 256

STREAM = [
    ("ffn1_0", 3 * NPAIR), ("ab_in", 7), ("alibi", 2), ("ab_out", 4), ("ffn2_0", 3 * NPAIR),
    ("ple_p_0", 1), ("ple_g_0", 4),
    ("ffn1_1", 3 * NPAIR), ("c_in", 17), ("c_out", 4), ("ffn2_1", 3 * NPAIR),
    ("ple_p_1", 1), ("ple_g_1", 4),
    ("ada_0", 24), ("ada_1", 24), ("l0_in", 9), ("rpb", 2), ("l0_out", 4), ("l0_ffn", 3 * NPAIR),
    ("l1_in", 5), ("l1_uq", 6), ("l1_ukv", 2), ("l1_out", 4), ("l1_ffn", 3 * NPAIR),
]
ROW = {}
_n = 0
for _name, _count in STREAM:
    ROW[_name] = _n
    _n += _count
N_ROWS = _n

PARAMS = (
    [(f"ln_{v}{i}{k}", KC) for i in range(2) for k in range(3) for v in "gb"]
    + [(f"ple_b{i}", KC) for i in range(2)]
    + [("sink", HEADS), ("b_cw", 16), ("b_cb", 4), ("b_ba", 4), ("b_bx", 4), ("b_lam", 4)]
    + [("c_cw", 96), ("c_alog", 1), ("c_dt", 1), ("c_ng", 1), ("cond", 16), ("ada_b0", 48), ("ada_b1", 48)]
    + [("q_gain", 1), ("k_gain", 1), ("cq_gain", 6), ("ckv_gain", 2)]
    + [(f"l{i}_ln{k}{v}", KC) for i in range(2) for k in (1, 2) for v in "gb"]
    + [(f"l{i}_cw", 3 * NT) for i in range(2)] + [(f"l{i}_cb", NT) for i in range(2)]
)
PCOL = {}
_n = 0
for _name, _count in PARAMS:
    PCOL[_name] = _n
    _n += _count
N_PCOL = _n

CONSTS = [("ident", 128), ("mean", 128), ("ones", 128), ("mean64", 128), ("rot", 128),
          ("cosA", T), ("sinA", T), ("cosM", T), ("sinM", T),
          ("after", 128), ("upto", 128), ("before", 128), ("in16", 128), ("in32", 128), ("in64", 128)]
CCOL = {}
_n = 0
for _name, _count in CONSTS:
    CCOL[_name] = _n
    _n += _count
N_CCOL = _n


class Lane:

    def __init__(self, eng, new_sem, name):
        self.eng, self.new_sem, self.name, self.gen = eng, new_sem, name, 0
        self.seen = {}
        self.fresh()

    def fresh(self):
        self.sem, self.count, self.gen = self.new_sem(f"{self.name}_{self.gen}"), 0, self.gen + 1

    def after(self, *tokens):
        for tok in tokens:
            if tok is not None and self.seen.get(id(tok[0]), 0) < tok[1]:
                self.seen[id(tok[0])] = tok[1]
                self.eng.wait_ge(tok[0], tok[1])

    def mark(self, ins):
        self.count += 1
        ins.then_inc(self.sem, 1)
        return (self.sem, self.count)

    def last(self):
        return (self.sem, self.count) if self.count else None


def build_program(nc, wstream, params, consts, xin, cin, pin, wab, out):
    with ExitStack() as top:
        def new_sem(name):
            return top.enter_context(nc.semaphore(name))

        def alloc(stack, name, shape, dtype=F32):
            return stack.enter_context(nc.sbuf_tensor(name, [P] + list(shape), dtype))

        pe, act, dve = nc.tensor, nc.scalar, nc.vector
        PE, AC, VE = Lane(pe, new_sem, "s_pe"), Lane(act, new_sem, "s_act"), Lane(dve, new_sem, "s_dve")

        final = [None] * 3

        def join():
            ends = [lane.last() for lane in (PE, AC, VE)]
            for i, end in enumerate(ends):
                final[i] = end or final[i]
            for lane in (PE, AC, VE):
                lane.after(*ends)
            for lane in (PE, AC, VE):
                lane.fresh()

        ring = alloc(top, "ring", [RING, SLOT])
        block_1 = ExitStack()
        X = alloc(top, "X", [KC, T])
        PT_ = alloc(top, "PT_", [2, 2, T])
        PV = alloc(top, "PV", [N_PCOL])
        CN = alloc(top, "CN", [N_CCOL])
        MOD = alloc(top, "MOD", [2, 48, 2])
        rstd = alloc(top, "rstd", [2 * T])
        lnv = alloc(top, "lnv", [2 * T])
        hT = alloc(top, "hT", [4, T])
        sg = alloc(top, "sg", [4, T])
        cg = alloc(top, "cg", [4, T])
        ps = top.enter_context(nc.psum_tensor("ps", [P, 8, 512], F32))
        top.enter_context(block_1)
        cond = alloc(block_1, "cond", [KC, 2])
        ada_stage = alloc(block_1, "ada_stage", [4, 2 * P])
        ada_rows = alloc(block_1, "ada_rows", [2, P])
        Z = alloc(block_1, "Z", [KC, T])
        H = alloc(block_1, "H", [KC, T])

        def const(name):
            return CN[:, CCOL[name]:CCOL[name] + dict(CONSTS)[name]]

        def pcol(name, i=0, n=1):
            return PV[:, PCOL[name] + i:PCOL[name] + i + n]

        ident, mean, ones = const("ident"), const("mean"), const("ones")

        s_in = [new_sem(f"s_in{i}") for i in range(6)]
        s_rows = [new_sem(f"s_rows{i}") for i in range(4)]
        first = [(PV[:, :], params), (X[:, :, :], xin), (CN[:, :], consts), (PT_[:, :, :, :], pin)]
        for s, (dst, src) in zip(s_in, first):
            act.dma_start(dst, src).then_inc(s, 16)
        AC.after((s_in[0], 16))
        cond_ready = AC.mark(act.activation(cond[:, :, :], pcol("cond", 0, 16).rearrange("p (c j) -> p c j", j=2),
                                            ACT.Silu))

        def constants_ready():
            for lane in (PE, AC, VE):
                lane.after((s_in[2], 16), (s_in[3], 16))

        s_load = [new_sem(f"s_load{i}") for i in range(RING)]
        s_gu, s_dn = new_sem("s_gu"), new_sem("s_dn")
        s_sg, s_h = new_sem("s_sg"), new_sem("s_h")
        s_hh, s_hl = new_sem("s_hh"), new_sem("s_hl")
        s_wh = [new_sem(f"s_wh{i}") for i in range(3)]
        s_lg, s_lu, s_ld = (new_sem(f"s_l{i}") for i in "gud")
        s_wl = (s_lg, s_lu, s_ld)
        s_id, s_cv = new_sem("s_id"), new_sem("s_cv")
        ring_log = []
        ffn_at = {}

        def loaded(n):
            return (s_load[n % RING], 16 * (n // RING + 1))

        def take(row):
            if ada_open and len(ring_log) - ada_open["n"] >= 2:
                ada_fill((KC - ada_open["c"]) / KC)
            n = len(ring_log)
            ring_log.append([row, None])
            PE.after(loaded(n))
            return n, ring[:, n % RING, :]

        def release(n, tok):
            ring_log[n][1] = tok

        bank_free = [[] for _ in range(8)]
        bank_turn = [0]

        def bank(among=range(8)):
            among = list(among)
            while True:
                b = among[bank_turn[0] % len(among)]
                bank_turn[0] += 1
                if b != ada_open.get("bank"):
                    break
            if b in [d[1] for d in ada_done]:
                ada_copy_out()
            PE.after(*bank_free[b])
            bank_free[b] = []
            return b

        ada_open, ada_done = {}, []
        ada_next = [0]
        ADA_SLOTS = 48

        def ada_fill(slots):
            for _ in range(round(slots * KC)):
                if not ada_open:
                    if ada_next[0] == ADA_SLOTS:
                        return
                    s = ada_next[0]
                    ada_next[0] += 1
                    n, w = take(ROW["ada_0"] + s)
                    PE.after(cond_ready)
                    ada_open.update(s=s, n=n, c=0, w=w.rearrange("p (c m) -> p c m", c=KC), bank=bank())
                a = ada_open
                c = a["c"]
                mm = pe.matmul(ps[0:2, a["bank"], 0:2 * P], cond[:, c, :], a["w"][:, c, :],
                               start=(c == 0), stop=(c == KC - 1), skip_group_check=True)
                a["c"] += 1
                if a["c"] == KC:
                    done = PE.mark(mm)
                    release(a["n"], done)
                    if len(ada_done) == 4:
                        ada_copy_out()
                    ada_done.append((a["s"], a["bank"], done))
                    ada_open.clear()

        def ada_copy_out():
            for s, b, done in ada_done:
                AC.after(done)
                if s >= 4:
                    AC.after((s_rows[s % 4], 32 * (s // 4)))
                t = AC.mark(act.activation(ada_stage[0:2, s % 4, :], ps[0:2, b, 0:2 * P], ACT.Copy))
                bank_free[b] = [t]
                nc.gpsimd.wait_ge(*t)
                for k in range(2):
                    tile = 2 * (s % 24) + k
                    nc.gpsimd.dma_start(ada_rows[2 * tile:2 * tile + 2, s // 24, :],
                                        ada_stage[0:2, s % 4, k * P:(k + 1) * P]).then_inc(s_rows[s % 4], 16)
            ada_done.clear()

        def ada_settle():
            if ada_open:
                ada_fill((KC - ada_open["c"]) / KC)
            ada_copy_out()

        def feature_major(row, n_tiles, kc, rhs, N, evac, per_slot=2, M=P):
            for t in range(n_tiles):
                if t % per_slot == 0:
                    n, w = take(row + t // per_slot)
                    w = w[:, 0:kc * per_slot * M].rearrange("p (c m) -> p c m", c=kc)
                b = bank()
                at = (t % per_slot) * M
                for c in range(kc):
                    mm = pe.matmul(ps[0:M, b, 0:N], w[:, c, at:at + M], rhs(c), start=(c == 0), stop=(c == kc - 1))
                done = PE.mark(mm)
                if t % per_slot == per_slot - 1 or t == n_tiles - 1:
                    release(n, done)
                read = evac(t, ps[0:M, b, 0:N], done)
                bank_free[b] = read if isinstance(read, list) else [read]

        class Split:

            def __init__(self, st, tag, src, ready):
                self.xh, self.xl = alloc(st, tag + "_xh", [KC, T], F32R), alloc(st, tag + "_xl", [KC, T], F32R)
                self.wh, self.wl = alloc(st, tag + "_wh", [3, KC, P], F32R), alloc(st, tag + "_wl", [3, KC, P], F32R)
                self.w_free, self.turn = [None] * 3, 0
                AC.after(*ready)
                VE.after(*ready)
                for c in range(0, KC, 2):
                    t = AC.mark(act.activation(self.xh[:, c:c + 2, :], src(c, 2), ACT.Copy))
                    VE.after(t)
                    self.ready = VE.mark(dve.tensor_tensor(self.xl[:, c:c + 2, :], src(c, 2),
                                                           self.xh[:, c:c + 2, :].bitcast(F32), ALU.subtract))

            def product(self, row, n_tiles, evac):
                split, held = {}, {}

                def split_tile(t):
                    if t % 2 == 0:
                        n, w = take(row + t // 2)
                        held.update(n=n, w=w.rearrange("p (c m) -> p c m", c=KC))
                    w, i = held["w"][:, :, (t % 2) * P:(t % 2 + 1) * P], self.turn % 3
                    self.turn += 1
                    AC.after(loaded(held["n"]), self.w_free[i])
                    VE.after(loaded(held["n"]))
                    a = AC.mark(act.activation(self.wh[:, i, :, :], w, ACT.Copy))
                    VE.after(a)
                    v = VE.mark(dve.tensor_tensor(self.wl[:, i, :, :], w, self.wh[:, i, :, :].bitcast(F32),
                                                  ALU.subtract))
                    if t % 2 == 1 or t == n_tiles - 1:
                        release(held["n"], v)
                    split[t] = (i, v)

                PE.after(self.ready)
                split_tile(0)
                split_tile(1)
                for t in range(n_tiles):
                    i, ready = split[t]
                    b = bank()
                    PE.after(ready)
                    for c in range(KC):
                        for k, (w, x) in enumerate(((self.wh, self.xh), (self.wl, self.xh), (self.wh, self.xl))):
                            mm = pe.matmul(ps[:, b, 0:T], w[:, i, c, :], x[:, c, :], start=(c == 0 and k == 0),
                                           stop=(c == KC - 1 and k == 2))
                    done = self.w_free[i] = PE.mark(mm)
                    if t + 2 < n_tiles:
                        split_tile(t + 2)
                    read = evac(t, ps[:, b, 0:T], done)
                    bank_free[b] = read if isinstance(read, list) else [read]

        def token_major(w, kc, lhs, n_tt, cols, dst):
            for tt in range(n_tt):
                b = bank()
                for c in range(kc):
                    mm = pe.matmul(ps[:, b, 0:cols], lhs(c, tt), w[:, c, :], start=(c == 0), stop=(c == kc - 1))
                done = PE.mark(mm)
                AC.after(done)
                bank_free[b] = [AC.mark(act.activation(dst(tt), ps[:, b, 0:cols], ACT.Copy))]
            return done

        def layer_norm(z_ready, n0, N, eps, g, b):
            z = Z[:, :, n0:n0 + N]
            mb = bank()
            for c in range(KC):
                PE.after(z_ready[c])
                mm = pe.matmul(ps[:, mb, 0:N], mean, z[:, c, :], start=(c == 0), stop=(c == KC - 1))
            got_mean = PE.mark(mm)
            ada_fill(3 / 8)
            vb = bank()
            VE.after(got_mean)
            squares = []
            for q in range(4):
                zq = z[:, 2 * q:2 * q + 2, :]
                centred = VE.mark(dve.tensor_tensor(zq, zq, ps[:, mb, 0:N].unsqueeze(1).broadcast_to([P, 2, N]),
                                                    ALU.subtract))
                AC.after(centred)
                squares.append(AC.mark(act.activation(H[:, 2 * q:2 * q + 2, n0:n0 + N], zq, ACT.Square)))
            bank_free[mb] = [centred]
            for c in range(KC):
                PE.after(squares[c // 2])
                mm = pe.matmul(ps[:, vb, 0:N], mean, H[:, c, n0:n0 + N], start=(c == 0), stop=(c == KC - 1))
            got_var = PE.mark(mm)
            ada_fill(LN_FILL)
            AC.after(got_var)
            VE.after(got_var)
            VE.after(AC.last())
            act.preload_act_table_set("natural_log_exp_and_others")
            t = VE.mark(dve.tensor_scalar(rstd[:, 0:N], ps[:, vb, 0:N], eps, None, ALU.add))
            bank_free[vb] = [t]
            AC.after(t)
            t = AC.mark(act.activation(lnv[:, 0:N], rstd[:, 0:N], ACT.Ln))
            AC.after(t)
            t = AC.mark(act.activation(rstd[:, 0:N], lnv[:, 0:N], ACT.Exp, scale=-0.5))
            VE.after(t)
            done = []
            for q in range(4):
                zq = z[:, 2 * q:2 * q + 2, :]
                t = VE.mark(dve.tensor_tensor(zq, zq, rstd[:, 0:N].unsqueeze(1).broadcast_to([P, 2, N]), ALU.mult))
                AC.after(t)
                for c in (2 * q, 2 * q + 1):
                    done.append(AC.mark(act.activation(X[:, c, n0:n0 + N], z[:, c, :], ACT.Identity,
                                                       scale=pcol(g, c), bias=pcol(b, c))))
            ada_copy_out()
            return done

        def scaled_residual(n0, N):
            return AC.mark(act.activation(Z[:, :, n0:n0 + N], X[:, :, n0:n0 + N], ACT.Copy, scale=ALPHA))

        ffn_count = [0]

        def ffn(name, src, residual, conv=None):
            with ExitStack() as st:
                return ffn_split(name, src, residual, conv, st)

        def ffn_split(name, src, residual, conv, st):
            ada_settle()
            join()
            base = NT * ffn_count[0]
            ffn_count[0] += 1
            n0 = len(ring_log)
            ffn_at[n0] = (base, ROW[name])
            for p in range(NPAIR):
                for k in range(3):
                    ring_log.append([ROW[name] + 3 * p + k, (s_wl[k], base + 2 * p + 2)])

            tag = f"f{ffn_count[0]}"
            xh, xl = alloc(st, tag + "_xh", [KC, T], F32R), alloc(st, tag + "_xl", [KC, T], F32R)
            wh, wl = alloc(st, tag + "_wh", [2, 3, KC, P], F32R), alloc(st, tag + "_wl", [2, 3, KC, P], F32R)
            hh, hl = alloc(st, tag + "_hh", [2, T], F32R), alloc(st, tag + "_hl", [2, T], F32R)
            for c in range(0, KC, 2):
                t = AC.mark(act.activation(xh[:, c:c + 2, :], src(c, 2), ACT.Copy))
                VE.after(t)
                x_split = VE.mark(dve.tensor_tensor(xl[:, c:c + 2, :], src(c, 2), xh[:, c:c + 2, :].bitcast(F32),
                                                    ALU.subtract))
            PE.after(x_split)

            def slot(n, k, j):
                w = ring[:, (n + k) % RING, :]
                if k == 2:
                    return w.rearrange("p (j c m) -> p j c m", j=2, m=P)[:, j, :, :]
                return w.rearrange("p (c m) -> p c m", c=KC)[:, :, j * P:(j + 1) * P]

            def split_weights(ks, n, j, t, s, free=None, turns=0):
                for k in ks:
                    w = slot(n, k, j)
                    if j == 0:
                        for eng in (act, dve):
                            eng.wait_ge(s_load[(n + k) % RING], turns * 16 + 16 * ((n + k) // RING + 1))
                    if free is not None and k != 1:
                        act.wait_ge(*free)
                    act.activation(wh[:, s, k, :, :], w, ACT.Copy).then_inc(s_wh[k], 1)
                    dve.wait_ge(s_wh[k], t + 1)
                    dve.tensor_tensor(wl[:, s, k, :, :], w, wh[:, s, k, :, :].bitcast(F32),
                                      ALU.subtract).then_inc(s_wl[k], 1)

            def three(out, w_hi, w_lo, x_hi, x_lo, start):
                pe.matmul(out, w_hi, x_hi, start=start, stop=False, skip_group_check=True)
                pe.matmul(out, w_lo, x_hi, start=False, stop=False, skip_group_check=True)
                return pe.matmul(out, w_hi, x_lo, start=False, stop=True, skip_group_check=True)

            def gate_up(t, s, bk):
                pe.wait_ge(s_lg, t + 1)
                for k in range(2):
                    if k == 1:
                        pe.wait_ge(s_lu, t + 1)
                    for c in range(KC):
                        mm = three(ps[:, bk, k * T:(k + 1) * T], wh[:, s, k, c, :], wl[:, s, k, c, :],
                                   xh[:, c, :], xl[:, c, :], start=(c == 0))
                mm.then_inc(s_gu, 1)

            def down(t, s, first=False):
                pe.wait_ge(s_ld, t + 1)
                pe.wait_ge(s_hl, t + 1)
                for o in range(KC):
                    mm = three(ps[:, o // 2, (o % 2) * T:(o % 2 + 1) * T], wh[:, s, 2, o, :], wl[:, s, 2, o, :],
                               hh[:, s, :], hl[:, s, :], start=(first and o % 2 == 0))
                mm.then_inc(s_dn, 1)

            def hidden(t, k, bk, conv_at):
                gate, up = ps[:, bk, 0:T], ps[:, bk, T:2 * T]
                act.wait_ge(s_gu, t + 1)
                if conv is None:
                    act.activation(sg[:, k, :], gate, ACT.Silu).then_inc(s_sg, 1)
                else:
                    w = [PV[:, bass.ds(conv_at + PCOL[f"l{conv}_cw"] + NT * tap, 1)] for tap in range(3)]
                    bias = PV[:, bass.ds(conv_at + PCOL[f"l{conv}_cb"], 1)]
                    cb = conv_at + base_cv
                    act.activation(cg[:, k, :], gate, ACT.Identity, scale=w[1], bias=bias).then_inc(s_id, 1)
                    dve.wait_ge(s_id, cb + 1)
                    dve.scalar_tensor_tensor(cg[:, k, 1:T], gate[:, 0:T - 1], w[0], cg[:, k, 1:T],
                                             ALU.mult, ALU.add).then_inc(s_cv, 1)
                    dve.wait_ge(s_cv, cb * 2 + 1)
                    dve.scalar_tensor_tensor(cg[:, k, 0:T - 1], gate[:, 1:T], w[2], cg[:, k, 0:T - 1],
                                             ALU.mult, ALU.add).then_inc(s_cv, 1)
                    act.wait_ge(s_cv, cb * 2 + 2)
                    act.activation(sg[:, k, :], cg[:, k, :], ACT.Silu).then_inc(s_sg, 1)
                dve.wait_ge(s_sg, t + 1)
                dve.tensor_tensor(hT[:, k, :], sg[:, k, :], up, ALU.mult).then_inc(s_h, 1)
                act.wait_ge(s_h, t + 1)
                act.activation(hh[:, k % 2, :], hT[:, k, :], ACT.Copy).then_inc(s_hh, 1)
                dve.wait_ge(s_hh, t + 1)
                dve.tensor_tensor(hl[:, k % 2, :], hT[:, k, :], hh[:, k % 2, :].bitcast(F32),
                                  ALU.subtract).then_inc(s_hl, 1)

            base_cv = conv_count[0]
            if conv is not None:
                conv_count[0] += NT
            split_weights((0, 1, 2), n0, 0, base, 0)
            split_weights((0, 1), n0, 1, base + 1, 1)
            gate_up(base, 0, 4)
            hidden(base, 0, 4, 0)
            residual()
            split_weights((2,), n0, 1, base + 1, 1)
            n1 = n0 + 3
            split_weights((0, 1), n1, 0, base + 2, 0, free=(s_gu, base + 1))
            gate_up(base + 1, 1, 5)
            hidden(base + 1, 1, 5, 1)
            down(base, 0, first=True)
            split_weights((2,), n1, 0, base + 2, 0, free=(s_dn, base + 1))

            def tile(t, i, n_next, j_next, conv_at, turns):
                if n_next is not None:
                    split_weights((0, 1), n_next, j_next, t + 1, (i + 1) % 2, free=(s_gu, t), turns=turns)
                gate_up(t, i % 2, 4 + (2 + i) % 4)
                hidden(t, (2 + i) % 4, 4 + (2 + i) % 4, conv_at)
                down(t - 1, (i + 1) % 2)
                if n_next is not None:
                    split_weights((2,), n_next, j_next, t + 1, (i + 1) % 2, free=(s_dn, t), turns=turns)

            turns_of_4 = (NT - 6) // 4
            with nc.Fori(0, turns_of_4, engines=(ENG.PE, ENG.Activation, ENG.DVE)) as it:
                for i in range(4):
                    t = it * 4 + (base + 2 + i)
                    tile(t, i, n1 + 3 * ((i + 1) // 2), (i + 1) % 2, it * 4 + (2 + i), it)
            for i in range(4):
                k = 4 * turns_of_4 + i
                nxt = n1 + 3 * ((k + 1) // 2) if i < 3 else None
                tile(base + 2 + k, i, nxt, (k + 1) % 2, 2 + k, 0)
            down(base + NT - 1, (NT - 1) % 2)
            PE.seen.clear()
            AC.seen.clear()
            VE.seen.clear()
            constants_ready()
            return (s_dn, base + NT)

        conv_count = [0]

        def ffn_residual(n0, done, coef):
            zin = AC.last()
            VE.after(done, zin)
            toks = []
            for c in range(KC):
                y = ps[:, c // 2, (c % 2) * T:(c % 2 + 1) * T]
                k = coef if isinstance(coef, float) else coef(c)
                z = Z[:, c, n0:n0 + T]
                toks.append(VE.mark(dve.scalar_tensor_tensor(z, y, k, z, ALU.mult, ALU.add)))
            for b in range(4):
                bank_free[b] = [toks[2 * b + 1]]
            return toks

        def add_branch(N, coef):
            toks = []

            def evac(t, tile, done):
                VE.after(done)
                for n0 in range(0, N, T):
                    k = coef if isinstance(coef, float) else coef(t, n0 // T)
                    z = Z[:, t, n0:n0 + T]
                    tok = VE.mark(dve.scalar_tensor_tensor(z, tile[:, n0:n0 + T], k, z, ALU.mult, ALU.add))
                toks.append(tok)
                return tok
            return evac, toks

        def attention(tag, units, beside=()):
            ada_settle()
            st = ExitStack()
            n = len(units)
            parts = [buf[:, 2 * i:2 * i + 2, :].rearrange("p a n -> p (a n)") for buf in (hT, sg, cg) for i in range(2)]
            pb, pt = parts[0:3], parts[3:6]
            small = alloc(st, f"{tag}_s", [3, 8])
            G = units[0]["G"]
            K = 512 // G
            s_sets = [(0, 1), (2, 3)] if G == 2 else [(0,), (1,), (2,), (3,)]
            t_banks, o_banks = (4, 5), (6, 7)
            tok = [dict() for _ in units]
            o_turn = [0]

            def scores(i):
                banks = s_sets[i % len(s_sets)]
                PE.after(*bank_free[banks[0]])
                tok[i]["s"] = units[i]["scores"](banks)

            def row_max(i):
                u, banks = units[i], s_sets[i % len(s_sets)]
                s = ps[:, banks[0]:banks[0] + G, 0:K]
                nm = small[:, i % 3, 0:G]
                if i >= 3:
                    VE.after(tok[i - 3]["exp"])
                VE.after(tok[i]["s"])
                t = VE.mark(dve.tensor_reduce(nm, s, AX.X, ALU.max, negate=True))
                if u["sink"] is not None:
                    VE.after(t)
                    t = VE.mark(dve.tensor_tensor(nm, nm, u["nsink"], ALU.min))
                tok[i]["max"] = t

            def exponentials(i):
                u, banks = units[i], s_sets[i % len(s_sets)]
                nm, den, es = (small[:, i % 3, 2 * j:2 * j + G] for j in (0, 1, 3))
                AC.after(tok[i]["max"])
                if i >= 3:
                    AC.after(tok[i - 3]["tr"], tok[i - 3]["norm"])
                for g in range(G):
                    e = AC.mark(act.activation(pb[i % 3][:, g * K:(g + 1) * K], ps[:, banks[g], 0:K], ACT.Exp,
                                               bias=nm[:, g:g + 1], accum_out=den[:, g:g + 1]))
                bank_free[banks[0]] = [e]
                if u["sink"] is not None:
                    for g in range(G):
                        e = AC.mark(act.activation(es[:, g:g + 1], u["sink"][g], ACT.Exp, bias=nm[:, g:g + 1]))
                tok[i]["exp"] = e

            def normalise(i):
                u = units[i]
                den, rd, es = (small[:, i % 3, 2 * j:2 * j + G] for j in (1, 2, 3))
                VE.after(tok[i]["exp"])
                if u["sink"] is not None:
                    t = VE.mark(dve.tensor_tensor(den, den, es, ALU.add))
                    VE.after(t)
                t = VE.mark(dve.reciprocal(rd, den))
                VE.after(t)
                for g in range(G):
                    pg = pb[i % 3][:, g * K:(g + 1) * K]
                    t = VE.mark(dve.tensor_scalar(pg, pg, rd[:, g:g + 1], None, ALU.mult))
                tok[i]["norm"] = t

            def transposes(i):
                b = t_banks[i % 2]
                PE.after(*bank_free[b])
                PE.after(tok[i]["norm"])
                for k in range(4):
                    mm = pe.transpose(ps[:, b, k * P:(k + 1) * P], pb[i % 3][:, k * P:(k + 1) * P], ident)
                tok[i]["tr"] = PE.mark(mm)
                AC.after(tok[i]["tr"])
                if i >= 3:
                    AC.after(tok[i - 3]["pv"])
                tok[i]["pt"] = AC.mark(act.activation(pt[i % 3], ps[:, b, :], ACT.Copy))
                bank_free[b] = [tok[i]["pt"]]

            def values(i):
                u = units[i]
                b = o_banks[o_turn[0] % 2]
                if u["new_o"]:
                    PE.after(*bank_free[b])
                PE.after(tok[i]["pt"])
                for g in range(G):
                    half, blocks = u["halves"][g], 4 // G
                    for k in range(blocks):
                        blk = g * blocks + k
                        mm = pe.matmul(ps[64 * half:64 * half + 64, b, 0:P], u["v"](k, g),
                                       pt[i % 3][:, blk * P:(blk + 1) * P], start=(k == 0), stop=(k == blocks - 1),
                                       skip_group_check=True)
                tok[i]["pv"] = PE.mark(mm)
                if u["end_o"]:
                    VE.after(tok[i]["pv"])
                    bank_free[b] = [VE.mark(dve.tensor_copy(u["o"], ps[:, b, 0:P]))]
                    o_turn[0] += 1

            steps = ((scores, 0), (transposes, 2), (normalise, 1), (row_max, 0), (exponentials, 0), (values, 3))
            for i in range(n + 3):
                for step, lag in steps:
                    if 0 <= i - lag < n:
                        step(i - lag)
                if i < len(beside):
                    beside[i]()
            join()
            st.close()

        def rms_rows(terms, matrix, N, eps, dst, extra=0.0):
            b = bank()
            for k, (tile, tk) in enumerate(terms):
                PE.after(tk)
                mm = pe.matmul(ps[:, b, 0:N], matrix, tile, start=(k == 0), stop=(k == len(terms) - 1))
            t = PE.mark(mm)
            VE.after(t)
            VE.after(AC.last())
            t = VE.mark(dve.tensor_scalar(dst, ps[:, b, 0:N], eps, None, ALU.add))
            bank_free[b] = [t]
            AC.after(t)
            t = AC.mark(act.activation(dst, dst, ACT.Ln))
            AC.after(t)
            return AC.mark(act.activation(dst, dst, ACT.Exp, scale=-0.5))

        def rms_batch(src, sq, rn, scale, apply):
            flat = lambda buf, k: buf[:, 2 * k:2 * k + 2, :].rearrange("p a n -> p (a n)")
            sums = []
            for k in range(4):
                t = AC.mark(act.activation(flat(sq, k), flat(src, k), ACT.Square, scale=scale))
                b = bank()
                PE.after(t)
                t = PE.mark(pe.matmul(ps[:, b, :], ones, flat(sq, k), start=True, stop=True))
                VE.after(t)
                t = VE.mark(dve.tensor_scalar(flat(rn, k), ps[:, b, :], 1e-6, None, ALU.add))
                bank_free[b] = [t]
                sums.append(t)
                ada_fill(3 / 8)
            for k in range(4):
                AC.after(sums[k])
                t = AC.mark(act.activation(flat(rn, k), flat(rn, k), ACT.Ln))
            ada_fill(1)
            AC.after(t)
            for k in range(4):
                t = AC.mark(act.activation(flat(rn, k), flat(rn, k), ACT.Exp, scale=-0.5))
                VE.after(t)
                t = apply(k, flat(rn, k))
            return t

        def rope(q, cos, sin, tmp, ready):
            b = bank()
            PE.after(ready)
            t = PE.mark(pe.matmul(ps[:, b, 0:T], const("rot"), q, start=True, stop=True))
            VE.after(t)
            VE.after(VE.last())
            a = VE.mark(dve.tensor_tensor(tmp, ps[:, b, 0:T], sin, ALU.mult))
            bank_free[b] = [a]
            c = VE.mark(dve.tensor_tensor(q, q, cos, ALU.mult))
            VE.after(c)
            return VE.mark(dve.tensor_tensor(q, q, tmp, ALU.add))

        def mixer_ab():
            with ExitStack() as st:
                join()
                x = lambda c: X[:, c, 0:T]
                q = alloc(st, "ab_q", [4, T])
                k = alloc(st, "ab_k", [T])
                v = alloc(st, "ab_v", [2, P])
                y = alloc(st, "ab_y", [8, T])
                bx = alloc(st, "ab_bx", [4, T + 3])
                xb = alloc(st, "ab_xb", [4, T])
                bg = alloc(st, "ab_bg", [4, T])
                tr = alloc(st, "ab_tr", [4, T])
                ti = alloc(st, "ab_ti", [4, T])
                wab_sb = alloc(st, "ab_w", [8, P])
                cols = alloc(st, "ab_cols", [40])
                scaled_residual(0, T)
                act.dma_start(wab_sb[:, :, :], wab).then_inc(s_in[5], 16)
                pads = VE.mark(dve.memset(bx[:, :, 0:3], 0.0))

                def evac_q(t, tile, done):
                    AC.after(done)
                    return AC.mark(act.activation(q[:, t, :], tile, ACT.Copy, scale=0.125))

                sp_ = ExitStack()
                parts = Split(sp_, "ab", lambda c, n: X[:, c:c + n, 0:T], [])
                parts.product(ROW["ab_in"], 4, evac_q)
                n, w = take(ROW["ab_in"] + 2)
                w = w.rearrange("p (c m) -> p c m", c=KC)
                b = bank()
                for c in range(KC):
                    mm = pe.matmul(ps[:, b, 0:T], w[:, c, 0:P], x(c), start=(c == 0), stop=(c == KC - 1))
                t = PE.mark(mm)
                AC.after(t)
                bank_free[b] = [AC.mark(act.activation(k[:, :], ps[:, b, 0:T], ACT.Copy))]
                t = token_major(w[:, :, P:2 * P], KC, lambda c, tt: X[:, c, tt * P:(tt + 1) * P], 2, P,
                                lambda tt: v[:, tt, :])
                release(n, t)

                def evac_b(dst, off):
                    def evac(t, tile, done):
                        VE.after(done)
                        return VE.mark(dve.tensor_copy(dst[:, t, off:off + T], tile))
                    return evac
                parts.product(ROW["ab_in"] + 3, 4, evac_b(bx, 3))
                parts.product(ROW["ab_in"] + 5, 4, evac_b(bg, 0))

                nsink = cols[:, 0:8]
                t = VE.mark(dve.tensor_scalar(nsink, pcol("sink", 0, 8), -1.0, None, ALU.mult))
                VE.after(t)
                units, held = [], {}
                for qt in range(2):
                    for h in range(4):
                        def scores(banks, qt=qt, h=h):
                            if h == 0:
                                held["n"], held["w"] = take(ROW["alibi"] + qt)
                            for g in range(2):
                                r = slice(64 * g, 64 * g + 64)
                                o = ps[:, banks[g], 0:T]
                                pe.matmul(o, q[r, h, qt * P:(qt + 1) * P], k[r, :], start=True, stop=False)
                                mm = pe.matmul(o, ident, held["w"][:, (2 * h + g) * T:(2 * h + g + 1) * T],
                                               start=False, stop=True)
                            t = PE.mark(mm)
                            if h == 3:
                                release(held["n"], t)
                            return t
                        units.append(dict(
                            scores=scores, G=2, halves=(0, 1), new_o=True, end_o=True,
                            sink=[pcol("sink", 2 * h + g) for g in range(2)], nsink=nsink[:, 2 * h:2 * h + 2],
                            v=lambda kc, g: v[:, kc, 64 * g:64 * g + 64], o=y[:, h, qt * P:(qt + 1) * P]))
                join()
                sp_.close()
                hba, hbx, sp, e1, c4 = (cols[:, 8 + 4 * j:12 + 4 * j] for j in range(5))
                ready = {}

                def convolve(t_):
                    for tap in range(4):
                        xs, wt = bx[:, t_, tap:tap + T], pcol("b_cw", tap * 4 + t_)
                        if tap == 0:
                            s = VE.mark(dve.tensor_scalar(xb[:, t_, :], xs, wt, pcol("b_cb", t_), ALU.mult, ALU.add))
                        else:
                            VE.after(s)
                            s = VE.mark(dve.scalar_tensor_tensor(xb[:, t_, :], xs, wt, xb[:, t_, :],
                                                                 ALU.mult, ALU.add))
                    ready["conv"] = s

                def gate_columns():
                    VE.mark(dve.tensor_scalar(hba, pcol("b_ba", 0, 4), 0.5, None, ALU.mult))
                    VE.mark(dve.tensor_scalar(hbx, pcol("b_bx", 0, 4), 0.5, None, ALU.mult))
                    VE.after(softplus_cols(pcol("b_lam", 0, 4), -1.0, sp, e1, cols[:, 28:32], P))
                    ready["c4"] = VE.mark(dve.tensor_scalar(c4, sp, -4.0, None, ALU.mult))

                z_ = y[:, 4:8, :]

                def gelu_square():
                    ready["g"] = AC.mark(act.activation(z_, bg[:, :, :], ACT.Square))

                def gelu_cubic():
                    VE.after(ready["g"])
                    g1 = VE.mark(dve.tensor_scalar(z_, z_, 0.044715, 1.0, ALU.mult, ALU.add))
                    VE.after(g1)
                    ready["g"] = VE.mark(dve.tensor_tensor(z_, z_, bg[:, :, :], ALU.mult))

                def gelu_tanh():
                    AC.after(ready["g"])
                    ready["g"] = AC.mark(act.activation(z_, z_, ACT.Tanh, scale=float(np.sqrt(2 / np.pi))))

                def gelu_last():
                    VE.after(ready["g"])
                    VE.mark(dve.scalar_tensor_tensor(bg[:, :, :], z_, 1.0, bg[:, :, :], ALU.add, ALU.mult))

                def columns_and_square():
                    gate_columns()
                    gelu_square()
                attention("ab", units, [columns_and_square, lambda: convolve(0), lambda: convolve(1), gelu_cubic,
                                        lambda: convolve(2), gelu_tanh, lambda: convolve(3), gelu_last])

                PE.after(ready["c4"], ready["conv"], (s_in[5], 16))
                AC.after(ready["c4"])
                for w_i, (dst, hb) in enumerate(((tr, hba), (ti, hbx))):
                    for t_ in range(4):
                        b = bank()
                        m = PE.mark(pe.matmul(ps[:, b, 0:T], wab_sb[:, 4 * w_i + t_, :], xb[:, t_, :],
                                              start=True, stop=True))
                        AC.after(m)
                        bank_free[b] = [AC.mark(act.activation(dst[:, t_, :], ps[:, b, 0:T], ACT.Tanh,
                                                               bias=hb[:, t_:t_ + 1], scale=0.5))]
                la, a_, m1 = alloc(st, "ab_la", [4, T]), alloc(st, "ab_a", [4, T]), alloc(st, "ab_m1", [4, T])
                VE.after(AC.last())
                for t_ in range(4):
                    t = VE.mark(dve.tensor_scalar(la[:, t_, :], tr[:, t_, :], 1.0, c4[:, t_:t_ + 1], ALU.add, ALU.mult))
                AC.after(t)
                AC.mark(act.activation(a_[:, :, :], la[:, :, :], ACT.Exp))
                t = AC.mark(act.activation(tr[:, :, :], la[:, :, :], ACT.Tanh))
                VE.after(t)
                t = VE.mark(dve.tensor_scalar(m1[:, :, :], tr[:, :, :], -1.0, 1.0, ALU.mult, ALU.add))
                VE.after(t)
                t = VE.mark(dve.reciprocal(la[:, :, :], m1[:, :, :]))
                VE.after(t)
                t = VE.mark(dve.scalar_tensor_tensor(m1[:, :, :], tr[:, :, :], -2.0, la[:, :, :], ALU.mult, ALU.mult))
                AC.after(t)
                t = AC.mark(act.activation(la[:, :, :], m1[:, :, :], ACT.Sqrt))
                VE.after(t)
                t = VE.mark(dve.scalar_tensor_tensor(m1[:, :, :], ti[:, :, :], 1.0, xb[:, :, :], ALU.add, ALU.mult))
                VE.after(t)
                t = VE.mark(dve.scalar_tensor_tensor(m1[:, :, :], m1[:, :, :], 0.5, la[:, :, :], ALU.mult, ALU.mult))
                VE.after(t)
                for t_ in range(4):
                    t = VE.mark(dve.tensor_tensor_scan(tr[:, t_, :], a_[:, t_, :], m1[:, t_, :], 0.0,
                                                       ALU.mult, ALU.add))
                VE.after(t)
                g1 = VE.mark(dve.scalar_tensor_tensor(y[:, 4:8, :], bg[:, :, :], 0.5, tr[:, :, :], ALU.mult, ALU.mult))
                evac, toks = add_branch(T, 1.0)
                Split(st, "ab2", lambda c, n: y[:, c:c + n, :], [g1]).product(ROW["ab_out"], 8, evac)
                layer_norm(toks, 0, T, 1e-5, "ln_g01", "ln_b01")
                join()

        def softplus_cols(src, sign, dst, tmp, tmp2, rows):
            t = VE.mark(dve.tensor_scalar(dst, src, sign, None, ALU.mult))
            VE.after(t)
            t = VE.mark(dve.tensor_scalar(tmp, dst, -1.0, None, ALU.mult))
            VE.after(t)
            t = VE.mark(dve.tensor_tensor(tmp, tmp, dst, ALU.min))
            AC.after(t)
            t = AC.mark(act.activation(tmp2, tmp, ACT.Exp))
            VE.after(t)
            t = VE.mark(dve.tensor_scalar(tmp2, tmp2, 1.0, None, ALU.add))
            AC.after(t)
            t = AC.mark(act.activation(tmp, tmp2, ACT.Ln))
            VE.after(t)
            t = VE.mark(dve.tensor_scalar(dst, dst, 0.0, None, ALU.max))
            VE.after(t)
            return VE.mark(dve.tensor_tensor(dst, dst, tmp, ALU.add))

        def mixer_c():
            with ExitStack() as st:
                join()
                x = lambda c: X[:, c, 0:T]
                qkv = alloc(st, "c_qkv", [24, T])
                z = alloc(st, "c_z", [8, T])
                kbT = H
                o = qkv[:, 16:24, :]
                tcol = alloc(st, "c_tcol", [8, 8])
                glast = alloc(st, "c_gl", [8, 4])
                small = alloc(st, "c_small", [8])
                s1 = ExitStack()
                raw = alloc(s1, "c_raw", [4, T + 3])
                parts = Split(s1, "c", lambda c, n: X[:, c:c + n, 0:T], [])
                scaled_residual(0, T)
                pad = VE.mark(dve.memset(raw[:, :, 0:3], 0.0))
                AC.after(pad)
                raw_free = [None] * 4

                silus = []

                def silu():
                    dst, ready = silus.pop(0)
                    AC.after(ready)
                    AC.mark(act.activation(dst, dst, ACT.Silu))

                def evac_qkv(base):
                    def evac(t, tile, done):
                        g = base + t
                        AC.after(done, raw_free[g % 4])
                        r = raw[:, g % 4, :]
                        c = AC.mark(act.activation(r[:, 3:T + 3], tile, ACT.Copy))
                        VE.after(c)
                        dst = qkv[:, g, :]
                        s = VE.mark(dve.tensor_scalar(dst, r[:, 0:T], pcol("c_cw", g), None, ALU.mult))
                        for tap in range(1, 4):
                            VE.after(s)
                            s = VE.mark(dve.scalar_tensor_tensor(dst, r[:, tap:tap + T], pcol("c_cw", 24 * tap + g),
                                                                 dst, ALU.mult, ALU.add))
                        raw_free[g % 4] = s
                        silus.append((dst, s))
                        if g:
                            silu()
                        return c
                    return evac
                parts.product(ROW["c_in"], 24, evac_qkv(0))
                silu()

                def evac_z(t, tile, done):
                    AC.after(done)
                    return AC.mark(act.activation(z[:, t, :], tile, ACT.Silu))
                parts.product(ROW["c_in"] + 12, 8, evac_z)
                n, w = take(ROW["c_in"] + 16)
                w = w[:, 0:KC * 16].rearrange("p (c m) -> p c m", c=KC)
                b = bank()
                for part in range(2):
                    for c in range(KC):
                        mm = pe.matmul(ps[0:8, b, part * T:(part + 1) * T], w[:, c, 8 * part:8 * part + 8], x(c),
                                       start=(c == 0), stop=(c == KC - 1))
                t = PE.mark(mm)
                release(n, t)
                R = lambda i: (hT, sg)[i // 4][0:8, i % 4, :]
                AC.after(t)
                t0 = AC.mark(act.activation(R(0), ps[0:8, b, 0:T], ACT.Tanh, scale=0.5))
                VE.after(t0, t)
                t0 = VE.mark(dve.tensor_scalar(R(0), R(0), 1.0, 0.5, ALU.add, ALU.mult))
                t1 = VE.mark(dve.tensor_scalar(R(2), ps[0:8, b, T:2 * T], PV[0:8, PCOL["c_dt"]:PCOL["c_dt"] + 1], None,
                                               ALU.add))
                bank_free[b] = [t1]
                VE.after(t1)
                t1 = softplus_cols(R(2), 1.0, R(1), R(3), R(4), 8)
                ea = small[0:8, 0:1]
                t2 = AC.mark(act.activation(ea, PV[0:8, PCOL["c_alog"]:PCOL["c_alog"] + 1], ACT.Exp))
                VE.after(t1, t2)
                t1 = VE.mark(dve.tensor_scalar(R(1), R(1), ea, -1.0, ALU.mult, ALU.mult))
                VE.after(t1)
                one = small[0:8, 1:2]
                VE.mark(dve.memset(R(7), 1.0))
                VE.after(VE.last())
                for c in range(4):
                    cs = slice(c * CH, (c + 1) * CH)
                    t = VE.mark(dve.tensor_tensor_scan(R(2)[:, cs], R(7)[:, cs], R(1)[:, cs], 0.0,
                                                       ALU.mult, ALU.add))
                VE.after(t)
                for c in range(4):
                    cs = slice(c * CH, (c + 1) * CH)
                    t = VE.mark(dve.tensor_scalar(R(4)[:, cs], R(2)[:, cs],
                                                  R(2)[:, (c + 1) * CH - 1:(c + 1) * CH], -1.0,
                                                  ALU.subtract, ALU.mult))
                AC.after(t)
                AC.mark(act.activation(R(3), R(2), ACT.Exp))
                t = AC.mark(act.activation(R(4), R(4), ACT.Exp))
                VE.after(t)
                t = VE.mark(dve.tensor_tensor(R(5), R(0), R(3), ALU.mult))
                ada_fill(3)
                PE.after(t)
                b = bank()
                for j, r in enumerate((1, 0, 5, 4)):
                    for half in range(2):
                        mm = pe.transpose(ps[:, b, (2 * j + half) * 8:(2 * j + half + 1) * 8],
                                          R(r)[:, half * P:(half + 1) * P], ident[0:8, 0:8])
                t = PE.mark(mm)
                VE.after(t)
                t = VE.mark(dve.tensor_copy(tcol[:, :, :], ps[:, b, 0:64].rearrange("p (a h) -> p a h", a=8)))
                bank_free[b] = [t]
                tcol_ready = t
                col = lambda j, half, h: tcol[:, 2 * j + half, h:h + 1]

                join()
                s1.close()
                heads = ExitStack()
                Kd = alloc(heads, "c_kd", [8, 2, P])
                KB = alloc(heads, "c_kb", [8, 2, P])
                VB = alloc(heads, "c_vb", [8, 2, P])
                attnT = alloc(heads, "c_at", [8, 2, P])
                Y = alloc(heads, "c_Y", [8, 2, P])
                nWT = KB
                qg = alloc(heads, "c_qg", [8, T])
                s1 = ExitStack()
                sq, rn = alloc(s1, "c_sq", [8, T]), alloc(s1, "c_rn", [8, T])
                for first, scale in ((0, P ** -0.5), (8, 1.0)):
                    def unit_length(k, r, first=first, scale=scale):
                        pair = qkv[:, first + 2 * k:first + 2 * k + 2, :].rearrange("p a n -> p (a n)")
                        return VE.mark(dve.scalar_tensor_tensor(pair, pair, scale, r, ALU.mult, ALU.mult))
                    t = rms_batch(qkv[:, first:first + 8, :], sq, rn, 1.0, unit_length)
                    AC.after(t)
                join()
                s1.close()
                sel = lambda h: ident[0:8, h:h + 1].broadcast_to([8, P])
                for h in range(8):
                    b = bank()
                    pe.matmul(ps[:, b, 0:T], sel(h), R(0), start=True, stop=True)
                    t = PE.mark(pe.matmul(ps[:, b, T:2 * T], sel(h), R(3), start=True, stop=True))
                    VE.after(t)
                    VE.mark(dve.tensor_tensor(kbT[:, h, :], qkv[:, 8 + h, :], ps[:, b, 0:T], ALU.mult))
                    VE.mark(dve.tensor_copy(glast[:, h, :], ps[:, b, T + CH - 1:2 * T:CH]))
                    bank_free[b] = [VE.mark(dve.tensor_tensor(qg[:, h, :], qkv[:, h, :], ps[:, b, T:2 * T], ALU.mult))]
                for h in range(8):
                    b, b2 = bank(), bank()
                    for half in range(2):
                        ts_ = slice(half * P, (half + 1) * P)
                        pe.transpose(ps[:, b, half * P:(half + 1) * P], qkv[:, 8 + h, ts_], ident)
                        mm = pe.transpose(ps[:, b2, half * P:(half + 1) * P], qkv[:, 16 + h, ts_], ident)
                    t = PE.mark(mm)
                    VE.after(t)
                    AC.after(t)
                    for half in range(2):
                        kt = ps[:, b, half * P:(half + 1) * P]
                        vt = ps[:, b2, half * P:(half + 1) * P]
                        a = VE.mark(dve.tensor_scalar(KB[:, h, half, :], kt, col(2, half, h), None, ALU.mult))
                        a = VE.mark(dve.tensor_scalar(Kd[:, h, half, :], kt, col(3, half, h), None, ALU.mult))
                        a2 = AC.mark(act.activation(VB[:, h, half, :], vt, ACT.Copy, scale=col(1, half, h)))
                    bank_free[b], bank_free[b2] = [a], [a2]
                join()
                FILL = 2 / 8

                with ExitStack() as s2:
                    A4 = lambda nm: alloc(s2, nm, [4, P])
                    E, eD = A4("c_E"), A4("c_eD")
                    LT, L = A4("c_LT"), A4("c_L")
                    Pm, PTm = [A4("c_P0"), A4("c_P1")], [A4("c_PT0"), A4("c_PT1")]
                    Tm, Ym = (cg[:, 2 * i:2 * i + 2, :].rearrange("p a (b n) -> p (a b) n", b=2) for i in range(2))
                    B, BT = Pm[0], PTm[0]
                    M1, M2 = E, eD
                    wide = lambda m: m.unsqueeze(1).broadcast_to([P, 4, P])
                    full = lambda b: ps[:, b, :].rearrange("p (u n) -> p u n", u=4)

                    def products(lhs, rhs):
                        b = bank()
                        for u in range(4):
                            mm = pe.matmul(ps[:, b, u * P:(u + 1) * P], lhs(u), rhs(u), start=True, stop=True)
                        return b, PE.mark(mm)

                    def vchain(ins):
                        t = VE.mark(ins)
                        VE.after(t)
                        return t

                    for grp in range(4):
                        unit = lambda u: (2 * grp + u // 2, u % 2)
                        VE.after(VE.last(), PE.last(), AC.last())
                        AC.after(VE.last(), PE.last())
                        for u in range(4):
                            h, half = unit(u)
                            t = VE.mark(dve.tensor_scalar(E[:, u, :], const("upto"), col(0, half, h), None, ALU.mult))
                        PE.after(t, AC.last())
                        ada_fill(FILL)
                        b = bank()
                        t = PE.mark(pe.matmul(ps[:, b, :], const("after"), E[:, :, :].rearrange("p u n -> p (u n)"),
                                              start=True, stop=True))
                        AC.after(t)
                        t = AC.mark(act.activation(eD[:, :, :], full(b), ACT.Exp))
                        bank_free[b] = [t]
                        VE.after(t)
                        vchain(dve.tensor_tensor(eD[:, :, :], eD[:, :, :], wide(const("upto")), ALU.mult))
                        tsl = lambda u: slice((u % 2) * P, (u % 2 + 1) * P)
                        hd = lambda u: 2 * grp + u // 2
                        b, t = products(lambda u: qkv[:, 8 + hd(u), tsl(u)], lambda u: qkv[:, hd(u), tsl(u)])
                        VE.after(t)
                        t = VE.mark(dve.tensor_tensor(
                            attnT[:, 2 * grp:2 * grp + 2, :, :].rearrange("p h a n -> p (h a) n"),
                            full(b), eD[:, :, :], ALU.mult))
                        bank_free[b] = [t]
                        b, t = products(lambda u: qkv[:, 8 + hd(u), tsl(u)], lambda u: kbT[:, hd(u), tsl(u)])
                        VE.after(t)
                        t = vchain(dve.tensor_tensor(LT[:, :, :], full(b), eD[:, :, :], ALU.mult))
                        bank_free[b] = [t]
                        t = vchain(dve.tensor_tensor(LT[:, :, :], LT[:, :, :], wide(const("before")), ALU.mult))
                        ada_fill(FILL)
                        PE.after(t)
                        b = bank()
                        for u in range(4):
                            mm = pe.transpose(ps[:, b, u * P:(u + 1) * P], LT[:, u, :], ident)
                        t = PE.mark(mm)
                        AC.after(t)
                        t = AC.mark(act.activation(L[:, :, :], full(b), ACT.Copy))
                        bank_free[b] = [t]
                        VE.after(t)
                        p, pt = Pm[0], PTm[0]
                        VE.mark(dve.scalar_tensor_tensor(p[:, :, :], L[:, :, :], -1.0, wide(const("in16")),
                                                         ALU.mult, ALU.mult))
                        vchain(dve.scalar_tensor_tensor(pt[:, :, :], LT[:, :, :], -1.0, wide(const("in16")),
                                                        ALU.mult, ALU.mult))
                        VE.mark(dve.tensor_tensor(Tm[:, :, :], p[:, :, :], wide(ident), ALU.add))
                        t = vchain(dve.tensor_tensor(Ym[:, :, :], pt[:, :, :], wide(ident), ALU.add))
                        ada_fill(FILL)
                        PE.after(t)
                        for step in range(3):
                            pn, ptn = Pm[(step + 1) % 2], PTm[(step + 1) % 2]
                            b1, t1 = products(lambda u: pt[:, u, :], lambda u: p[:, u, :])
                            b2, t2 = products(lambda u: p[:, u, :], lambda u: pt[:, u, :])
                            AC.after(t1)
                            a1 = AC.mark(act.activation(pn[:, :, :], full(b1), ACT.Copy))
                            VE.after(t2)
                            a2 = VE.mark(dve.tensor_copy(ptn[:, :, :], full(b2)))
                            bank_free[b1], bank_free[b2] = [a1], [a2]
                            ada_fill(FILL)
                            PE.after(a1, a2)
                            b1, t1 = products(lambda u: ptn[:, u, :], lambda u: Tm[:, u, :])
                            b2, t2 = products(lambda u: pn[:, u, :], lambda u: Ym[:, u, :])
                            VE.after(t1, t2)
                            a1 = VE.mark(dve.tensor_tensor(Tm[:, :, :], Tm[:, :, :], full(b1), ALU.add))
                            a2 = VE.mark(dve.tensor_tensor(Ym[:, :, :], Ym[:, :, :], full(b2), ALU.add))
                            bank_free[b1], bank_free[b2] = [a1], [a2]
                            ada_fill(FILL)
                            PE.after(a1, a2)
                            p, pt = pn, ptn
                        for m in ("in32", "in64"):
                            lastm = m == "in64"
                            VE.after(PE.last(), VE.last())
                            VE.mark(dve.tensor_tensor(B[:, :, :], L[:, :, :], wide(const(m)), ALU.mult))
                            t = VE.mark(dve.tensor_tensor(BT[:, :, :], LT[:, :, :], wide(const(m)), ALU.mult))
                            ada_fill(FILL)
                            PE.after(t)
                            b1, t1 = products(lambda u: B[:, u, :], lambda u: Ym[:, u, :])
                            AC.after(t1)
                            a1 = AC.mark(act.activation(M1[:, :, :], full(b1), ACT.Copy))
                            bank_free[b1] = [a1]
                            if not lastm:
                                b2, t2 = products(lambda u: BT[:, u, :], lambda u: Tm[:, u, :])
                                VE.after(t2)
                                a2 = VE.mark(dve.tensor_copy(M2[:, :, :], full(b2)))
                                bank_free[b2] = [a2]
                                PE.after(a2)
                            ada_fill(FILL)
                            PE.after(a1)
                            b1, t1 = products(lambda u: Tm[:, u, :], lambda u: M1[:, u, :])
                            if not lastm:
                                b2, t2 = products(lambda u: Ym[:, u, :], lambda u: M2[:, u, :])
                            VE.after(t1, t2)
                            dst = (Y[:, 2 * grp:2 * grp + 2, :, :].rearrange("p h a n -> p (h a) n") if lastm
                                   else Ym[:, :, :])
                            a1 = VE.mark(dve.tensor_tensor(dst, Ym[:, :, :], full(b1), ALU.subtract))
                            bank_free[b1] = [a1]
                            if not lastm:
                                a1 = VE.mark(dve.tensor_tensor(Tm[:, :, :], Tm[:, :, :], full(b2), ALU.subtract))
                                bank_free[b2] = [a1]
                            ada_fill(FILL)
                            PE.after(a1)
                        b, t = products(lambda u: KB[:, hd(u), u % 2, :], lambda u: Y[:, hd(u), u % 2, :])
                        AC.after(t)
                        t = AC.mark(act.activation(nWT[:, 2 * grp:2 * grp + 2, :, :].rearrange("p h a n -> p (h a) n"),
                                                   full(b), ACT.Copy, scale=-1.0))
                        bank_free[b] = [t]
                    join()

                s1 = ExitStack()
                S = alloc(s1, "c_S", [8, P])
                vn = alloc(s1, "c_vn", [8, P])
                for c in range(4):
                    half, p0 = c // 2, CH * (c % 2)
                    r = slice(p0, p0 + CH)
                    for g in range(2):
                        hs = slice(4 * g, 4 * g + 4)
                        b = bank()
                        PE.after(VE.last(), AC.last())
                        for j in range(4):
                            h = 4 * g + j
                            ov = ps[r, b, j * P:(j + 1) * P]
                            mm = pe.matmul(ov, Y[:, h, half, r], VB[:, h, half, :], start=True, stop=(c == 0))
                            if c:
                                mm = pe.matmul(ov, nWT[:, h, half, r], S[:, h, :], start=False, stop=True)
                        t = PE.mark(mm)
                        AC.after(t)
                        a = AC.mark(act.activation(vn[r, hs, :],
                                                   ps[r, b, :].rearrange("p (h n) -> p h n", h=4), ACT.Copy))
                        bank_free[b] = [a]
                        ada_fill(FILL)
                        PE.after(a)
                        bo, bs = bank(), bank()
                        for j in range(4):
                            h = 4 * g + j
                            oo = ps[:, bo, j * CH:(j + 1) * CH]
                            if c:
                                pe.matmul(oo, S[:, h, :], qg[:, h, c * CH:(c + 1) * CH], start=True, stop=False)
                            pe.matmul(oo, vn[r, h, :], attnT[r, h, half, r], start=(c == 0), stop=True)
                        for j in range(4):
                            h = 4 * g + j
                            mm = pe.matmul(ps[:, bs, j * P:(j + 1) * P], Kd[r, h, half, :], vn[r, h, :],
                                           start=True, stop=True)
                        t = PE.mark(mm)
                        AC.after(t)
                        bank_free[bo] = [AC.mark(act.activation(
                            o[:, hs, c * CH:(c + 1) * CH],
                            ps[:, bo, 0:4 * CH].rearrange("p (h n) -> p h n", h=4), ACT.Copy))]
                        VE.after(t)
                        for j in range(4):
                            h = 4 * g + j
                            if c == 0:
                                t = VE.mark(dve.tensor_copy(S[:, h, :], ps[:, bs, j * P:(j + 1) * P]))
                            else:
                                t = VE.mark(dve.scalar_tensor_tensor(S[:, h, :], S[:, h, :], glast[:, h, c:c + 1],
                                                                     ps[:, bs, j * P:(j + 1) * P], ALU.mult, ALU.add))
                        bank_free[bs] = [t]
                        ada_fill(FILL)
                join()
                s1.close()
                heads.close()
                sq, rn = alloc(st, "c_sq2", [8, T]), alloc(st, "c_rn2", [8, T])

                def gated(k, r):
                    pair = o[:, 2 * k:2 * k + 2, :].rearrange("p a n -> p (a n)")
                    t = VE.mark(dve.scalar_tensor_tensor(pair, pair, pcol("c_ng"), r, ALU.mult, ALU.mult))
                    VE.after(t)
                    return VE.mark(dve.tensor_tensor(pair, pair, z[:, 2 * k:2 * k + 2, :].rearrange("p a n -> p (a n)"),
                                                     ALU.mult))
                t = rms_batch(o, sq, rn, P ** -0.5, gated)
                evac, toks = add_branch(T, 1.0)
                Split(st, "c2", lambda c, n: o[:, c:c + n, :], [t]).product(ROW["c_out"], 8, evac)
                layer_norm(toks, 0, T, 1e-5, "ln_g11", "ln_b11")
                join()

        def ple(i):
            with ExitStack() as st:
                join()
                pp = alloc(st, f"ple_pp{i}", [8, T])
                th = alloc(st, f"ple_th{i}", [8, T])
                hb = alloc(st, f"ple_hb{i}", [8])
                t0 = VE.mark(dve.tensor_scalar(hb[:, :], pcol(f"ple_b{i}", 0, 8), 0.5, None, ALU.mult))
                AC.after(t0)

                def evac_p(t, tile, done):
                    VE.after(done)
                    return VE.mark(dve.tensor_copy(pp[:, t, :], tile))
                feature_major(ROW[f"ple_p_{i}"], 8, 2, lambda c: PT_[:, i, c, :], T, evac_p, per_slot=8)

                def evac_g(t, tile, done):
                    AC.after(done)
                    return AC.mark(act.activation(th[:, t, :], tile, ACT.Tanh, scale=0.5, bias=hb[:, t:t + 1]))
                Split(st, f"ple{i}", lambda c, n: X[:, c:c + n, 0:T], []).product(ROW[f"ple_g_{i}"], 8, evac_g)
                VE.after(VE.last(), AC.last())
                PE.after(AC.last())
                for t in range(8):
                    a = VE.mark(dve.scalar_tensor_tensor(th[:, t, :], th[:, t, :], 1.0, pp[:, t, :], ALU.add, ALU.mult))
                    VE.after(a, PE.last())
                    VE.mark(dve.scalar_tensor_tensor(X[:, t, 0:T], th[:, t, :], 0.5, X[:, t, 0:T], ALU.mult, ALU.add))
                join()

        def adaln():
            ada_fill(ADA_SLOTS)
            ada_settle()
            for layer in range(2):
                PE.after(*[(s, 32 * ADA_SLOTS // 4) for s in s_rows])
                b = bank()
                m = PE.mark(pe.transpose(ps[:, b, 0:96], ada_rows[0:96, layer, :], ident[0:96, 0:96]))
                VE.after(m)
                t = VE.mark(dve.tensor_tensor(MOD[:, layer, :, :], ps[:, b, 0:96].rearrange("p (t j) -> p t j", j=2),
                                              pcol(f"ada_b{layer}", 0, 48).unsqueeze(2).broadcast_to([P, 48, 2]),
                                              ALU.add))
                bank_free[b] = [t]
                VE.after(t)
                for part in (1, 4):
                    m_ = MOD[:, layer, 8 * part:8 * part + 8, :]
                    VE.mark(dve.tensor_scalar(m_, m_, 1.0, None, ALU.add))
            join()

        def modulate(layer, part, n0s, ready):
            VE.after(*ready)
            for j in n0s:
                for c in range(KC):
                    t = VE.mark(dve.tensor_scalar(H[:, c, j * T:(j + 1) * T], X[:, c, j * T:(j + 1) * T],
                                                  MOD[:, layer, 8 * (part + 1) + c, j:j + 1],
                                                  MOD[:, layer, 8 * part + c, j:j + 1], ALU.mult, ALU.add))
            return t

        def head_norm(st, tag):
            sq = alloc(st, f"{tag}_sq", [2, 2 * T])
            rn = alloc(st, f"{tag}_rn", [2, 2 * T])
            turn = [0]
            free = [None, None]

            def norm(dst, tile, done, gain, scale):
                j = turn[0] % 2
                turn[0] += 1
                N = 2 * T
                AC.after(done, free[j])
                s = AC.mark(act.activation(sq[:, j, 0:N], tile, ACT.Square))
                VE.after(free[j])
                r = rms_rows([(sq[:, j, 0:N], s)], const("mean64"), N, 1e-6, rn[:, j, 0:N])
                VE.after(r)
                t = VE.mark(dve.scalar_tensor_tensor(dst, tile, gain, rn[:, j, 0:N], ALU.mult, ALU.mult))
                free[j] = t
                if scale != 1.0:
                    VE.after(t)
                    t = VE.mark(dve.tensor_scalar(dst, dst, scale, None, ALU.mult))
                return t
            return norm

        def even_mixer():
            with ExitStack() as st:
                join()
                qA = alloc(st, "e_qA", [4, 2 * T])
                kA = alloc(st, "e_kA", [2 * T])
                vA = alloc(st, "e_vA", [4, P])
                qB = alloc(st, "e_qB", [4, 2 * T])
                kB = alloc(st, "e_kB", [4, 2 * T])
                vB = alloc(st, "e_vB", [4, 512])
                y = alloc(st, "e_y", [8, 2 * T])
                t = modulate(0, 0, (0, 1), [])
                scaled_residual(0, 2 * T)
                PE.after(t)
                src = lambda c: H[:, c, :]
                with ExitStack() as s2:
                    norm = head_norm(s2, "e")
                    tmp = alloc(s2, "e_tmp", [T])

                    def evac_qA(t, tile, done):
                        return norm(qA[:, t, :], tile, done, pcol("q_gain"), 0.125)
                    feature_major(ROW["l0_in"], 4, KC, src, 2 * T, evac_qA)
                    n, w = take(ROW["l0_in"] + 2)
                    w = w.rearrange("p (c m) -> p c m", c=KC)
                    b = bank()
                    for c in range(KC):
                        mm = pe.matmul(ps[:, b, :], w[:, c, 0:P], src(c), start=(c == 0), stop=(c == KC - 1))
                    bank_free[b] = [norm(kA[:, :], ps[:, b, :], PE.mark(mm), pcol("k_gain"), 1.0)]
                    lhs = lambda c, tt: H[:, c, tt * P:(tt + 1) * P]
                    release(n, token_major(w[:, :, P:2 * P], KC, lhs, 4, P, lambda tt: vA[:, tt, :]))
                    for t in range(4):
                        rope(qA[:, t, 0:T], const("cosA"), const("sinA"), tmp[:, :], VE.last())
                    rope(kA[:, 0:T], const("cosA"), const("sinA"), tmp[:, :], VE.last())

                def evac(dst, scale):
                    def f(t, tile, done):
                        AC.after(done)
                        return AC.mark(act.activation(dst[:, t, :], tile, ACT.Copy, scale=scale))
                    return f
                feature_major(ROW["l0_in"] + 3, 4, KC, src, 2 * T, evac(qB, 0.125))
                feature_major(ROW["l0_in"] + 5, 4, KC, src, 2 * T, evac(kB, 1.0))
                for s_ in range(2):
                    n, w = take(ROW["l0_in"] + 7 + s_)
                    w = w.rearrange("p (c m) -> p c m", c=KC)
                    release(n, token_major(w, KC, lhs, 4, T, lambda tt: vB[:, tt, s_ * T:(s_ + 1) * T]))
                join()
                units, held = [], {}

                def unit512(q, k, v, vcol, h, g, qt, bias):
                    def scores(banks):
                        bk = banks[0]
                        if bias and h == 0 and g == 0:
                            held["n"], held["w"] = take(ROW["rpb"] + qt)
                        r = slice(64 * g, 64 * g + 64)
                        mm = pe.matmul(ps[:, bk, :], q[r, h, qt * P:(qt + 1) * P], k(r), start=True, stop=True)
                        if bias:
                            i = 2 * h + g
                            mm = pe.matmul(ps[:, bk, 0:T], ident, held["w"][:, i * T:(i + 1) * T],
                                           start=False, stop=True, skip_group_check=True)
                        t = PE.mark(mm)
                        if bias and h == 3 and g == 1:
                            release(held["n"], t)
                        return t
                    return scores

                for qt in range(2):
                    for h in range(4):
                        for g in range(2):
                            units.append(dict(
                                scores=unit512(qA, lambda r: kA[r, :], None, None, h, g, qt, False), G=1, halves=(g,),
                                new_o=(g == 0), end_o=(g == 1), sink=None,
                                v=lambda kc, _, g=g: vA[:, kc, 64 * g:64 * g + 64], o=y[:, h, qt * P:(qt + 1) * P]))
                for qt in range(2):
                    for h in range(4):
                        for g in range(2):
                            units.append(dict(
                                scores=unit512(qB, lambda r, h=h: kB[r, h, :], None, None, h, g, qt, True), G=1,
                                halves=(g,), new_o=(g == 0), end_o=(g == 1), sink=None,
                                v=lambda kc, _, g=g, h=h: vB[:, kc, (2 * h + g) * 64:(2 * h + g) * 64 + 64],
                                o=y[:, 4 + h, qt * P:(qt + 1) * P]))
                attention("e", units)
                units = []
                for kind in range(2):
                    for qt in range(2):
                        for h in range(4):
                            def scores(banks, kind=kind, qt=qt, h=h):
                                q = (qA, qB)[kind]
                                for g in range(2):
                                    r = slice(64 * g, 64 * g + 64)
                                    kk = kA[r, T:2 * T] if kind == 0 else kB[r, h, T:2 * T]
                                    mm = pe.matmul(ps[:, banks[g], 0:T], q[r, h, T + qt * P:T + (qt + 1) * P],
                                                   kk, start=True, stop=True)
                                return PE.mark(mm)
                            if kind == 0:
                                v = lambda kc, g: vA[:, 2 + kc, 64 * g:64 * g + 64]
                            else:
                                v = lambda kc, g, h=h: vB[:, 2 + kc, (2 * h + g) * 64:(2 * h + g) * 64 + 64]
                            units.append(dict(scores=scores, G=2, halves=(0, 1), new_o=True, end_o=True, sink=None, v=v,
                                              o=y[:, 4 * kind + h, T + qt * P:T + (qt + 1) * P]))
                attention("f", units)
                add, toks = add_branch(2 * T, lambda c, j: MOD[:, 0, 16 + c, j:j + 1])
                feature_major(ROW["l0_out"], 8, KC, lambda c: y[:, c, :], 2 * T, add)
                layer_norm(toks, 0, 2 * T, 1e-6, "l0_ln1g", "l0_ln1b")
                join()

        def conv_ffn(layer, parts):
            AC.after(modulate(layer, 3, parts, [AC.last()]))
            for j in parts:
                done = ffn(f"l{layer}_ffn", lambda c, n: H[:, c:c + n, j * T:(j + 1) * T],
                           lambda: scaled_residual(j * T, T), conv=layer)
                toks = ffn_residual(j * T, done, lambda c: MOD[:, layer, 40 + c, j:j + 1])
            layer_norm(toks, 0, T * len(parts), 1e-6, f"l{layer}_ln2g", f"l{layer}_ln2b")

        def odd_mixer():
            with ExitStack() as st:
                join()
                q = alloc(st, "m_q", [MLA_H, T])
                k = alloc(st, "m_k", [MLA_H, 2 * T])
                v = alloc(st, "m_v", [4, MLA_H * 64])
                t = modulate(1, 0, (0, 1), [])
                scaled_residual(0, T)
                PE.after(t)
                with ExitStack() as s2:
                    two = lambda buf: buf[:, :, :].rearrange("p (a b) n -> p a (b n)", a=2)
                    cq, cq_sq = x1[:, 0:6, :], Z[:, 0:6, T:2 * T]
                    ckv, ckv_sq, rq = two(sg), two(hT), two(cg)
                    kr = alloc(s2, "m_kr", [2 * T])
                    qr = alloc(s2, "m_qr", [4, T])
                    tmp = alloc(s2, "m_tmp", [T])

                    def evac(dst, sq):
                        def f(t, tile, done):
                            AC.after(done)
                            AC.mark(act.activation(sq[:, t, :], tile, ACT.Square))
                            return AC.mark(act.activation(dst[:, t, :], tile, ACT.Copy))
                        return f

                    def normalise(dst, sq, N, n_tiles, gain, i):
                        b = bank()
                        PE.after(AC.last())
                        for c in range(n_tiles):
                            mm = pe.matmul(ps[:, b, 0:N], ones, sq[:, c, :], start=(c == 0), stop=(c == n_tiles - 1))
                        t = PE.mark(mm)
                        VE.after(t)
                        t = VE.mark(dve.tensor_scalar(rq[:, i, 0:N], ps[:, b, 0:N], 1.0 / (n_tiles * P), 1e-6,
                                                      ALU.mult, ALU.add))
                        bank_free[b] = [t]
                        AC.after(t)
                        t = AC.mark(act.activation(rq[:, i, 0:N], rq[:, i, 0:N], ACT.Ln))
                        AC.after(t)
                        t = AC.mark(act.activation(rq[:, i, 0:N], rq[:, i, 0:N], ACT.Exp, scale=-0.5))
                        VE.after(t)
                        for c in range(n_tiles):
                            t = VE.mark(dve.scalar_tensor_tensor(dst[:, c, :], dst[:, c, :], pcol(gain, c), rq[:, i, 0:N],
                                                                 ALU.mult, ALU.mult))
                        return t
                    feature_major(ROW["l1_in"], 6, KC, lambda c: H[:, c, 0:T], T, evac(cq, cq_sq))
                    t = normalise(cq, cq_sq, T, 6, "cq_gain", 0)
                    AC.after(PE.last())
                    feature_major(ROW["l1_in"] + 3, 2, KC, lambda c: H[:, c, :], 2 * T, evac(ckv, ckv_sq))

                    def evac_kr(t, tile, done):
                        AC.after(done)
                        return AC.mark(act.activation(kr[0:ROPE, :], tile, ACT.Copy))
                    feature_major(ROW["l1_in"] + 4, 1, KC, lambda c: H[:, c, :], 2 * T, evac_kr, per_slot=1, M=ROPE)
                    t = normalise(ckv, ckv_sq, 2 * T, 2, "ckv_gain", 1)
                    b = bank()
                    PE.after(AC.last(), t)
                    t = PE.mark(pe.matmul(ps[0:ROPE, b, 0:T], const("rot")[0:ROPE, 0:ROPE], kr[0:ROPE, 0:T],
                                          start=True, stop=True))
                    VE.after(t)
                    a = VE.mark(dve.tensor_tensor(tmp[0:ROPE, :], ps[0:ROPE, b, 0:T], const("sinM")[0:ROPE, :], ALU.mult))
                    bank_free[b] = [a]
                    c_ = VE.mark(dve.tensor_tensor(kr[0:ROPE, 0:T], kr[0:ROPE, 0:T], const("cosM")[0:ROPE, :], ALU.mult))
                    VE.after(c_)
                    a = VE.mark(dve.tensor_tensor(kr[0:ROPE, 0:T], kr[0:ROPE, 0:T], tmp[0:ROPE, :], ALU.add))
                    VE.after(a)
                    VE.mark(dve.tensor_copy(k[NOPE:NOPE + ROPE, :, :],
                                            kr[0:ROPE, :].unsqueeze(1).broadcast_to([ROPE, MLA_H, 2 * T])))
                    scale = float((NOPE + ROPE) ** -0.5)

                    def split_heads(dst, scale):
                        def f(t, tile, done):
                            AC.after(done)
                            VE.after(done)
                            a = AC.mark(act.activation(dst[0:NOPE, 2 * t, :], tile[0:64, :], ACT.Copy, scale=scale))
                            if scale == 1.0:
                                b_ = VE.mark(dve.tensor_copy(dst[0:NOPE, 2 * t + 1, :], tile[64:128, :]))
                            else:
                                b_ = VE.mark(dve.tensor_scalar(dst[0:NOPE, 2 * t + 1, :], tile[64:128, :], scale, None,
                                                               ALU.mult))
                            return [a, b_]
                        return f
                    VE.after(VE.last())
                    feature_major(ROW["l1_uq"], 8, 6, lambda c: cq[:, c, :], T, split_heads(q, scale))

                    def evac_qr(t, tile, done):
                        AC.after(done)
                        return AC.mark(act.activation(qr[:, t, :], tile, ACT.Copy, scale=scale))
                    feature_major(ROW["l1_uq"] + 4, 4, 6, lambda c: cq[:, c, :], T, evac_qr)
                    VE.after(VE.last())
                    for t_ in range(4):
                        r = rope(qr[:, t_, :], const("cosM"), const("sinM"), tmp[:, :], AC.last())
                        VE.after(r)
                        for j in range(4):
                            VE.mark(dve.tensor_copy(q[NOPE:NOPE + ROPE, 4 * t_ + j, :], qr[32 * j:32 * j + 32, t_, :]))
                    feature_major(ROW["l1_ukv"], 8, 2, lambda c: ckv[:, c, :], 2 * T, split_heads(k, 1.0), per_slot=8)
                    n, w = take(ROW["l1_ukv"] + 1)
                    w = w.rearrange("p (c m) -> p c m", c=2)
                    for s_ in range(2):
                        t = token_major(w[:, :, s_ * 512:(s_ + 1) * 512], 2, lambda c, tt: ckv[:, c, tt * P:(tt + 1) * P],
                                        4, 512, lambda tt: v[:, tt, s_ * 512:(s_ + 1) * 512])
                    release(n, t)
                    join()
                y = x1
                units = []
                for qt in range(2):
                    for h in range(MLA_H):
                        def scores(banks, qt=qt, h=h):
                            return PE.mark(pe.matmul(ps[:, banks[0], :], q[0:96, h, qt * P:(qt + 1) * P], k[0:96, h, :],
                                                     start=True, stop=True))
                        units.append(dict(scores=scores, G=1, halves=(h % 2,), new_o=(h % 2 == 0), end_o=(h % 2 == 1),
                                          sink=None, v=lambda kc, _, h=h: v[:, kc, 64 * h:64 * h + 64],
                                          o=y[:, h // 2, qt * P:(qt + 1) * P]))
                attention("m", units)
                add, toks = add_branch(T, lambda c, j: MOD[:, 1, 16 + c, j:j + 1])
                feature_major(ROW["l1_out"], 8, KC, lambda c: y[:, c, :], T, add)
                layer_norm(toks, 0, T, 1e-6, "l1_ln1g", "l1_ln1b")
                join()

        def swiglu_layer(name, g, b):
            done = ffn(name, lambda c, n: X[:, c:c + n, 0:T], lambda: scaled_residual(0, T))
            toks = ffn_residual(0, done, 0.5)
            layer_norm(toks, 0, T, 1e-5, g, b)

        x1 = None

        def enter_block_2():
            nonlocal X, Z, H, x1
            join()
            adaln()
            block_1.close()
            x1 = X
            X, Z, H = alloc(top, "X2", [KC, 2 * T]), alloc(top, "Z2", [KC, 2 * T]), alloc(top, "H2", [KC, 2 * T])
            act.dma_start(X[:, :, T:2 * T], cin).then_inc(s_in[4], 16)
            AC.mark(act.activation(X[:, :, 0:T], x1[:, :, :], ACT.Copy))
            for lane in (PE, AC, VE):
                lane.after((s_in[4], 16))

        stages = []
        for i in range(2):
            stages += [lambda i=i: swiglu_layer(f"ffn1_{i}", f"ln_g{i}0", f"ln_b{i}0"),
                       (mixer_ab, mixer_c)[i],
                       lambda i=i: swiglu_layer(f"ffn2_{i}", f"ln_g{i}2", f"ln_b{i}2"),
                       lambda i=i: ple(i)]
        stages += [enter_block_2, even_mixer, lambda: conv_ffn(0, (0, 1)), odd_mixer, lambda: conv_ffn(1, (0,))]
        ada_fill(START_FILL)
        ada_copy_out()
        for lane in (AC, VE):
            lane.after((s_in[0], 16), (s_in[1], 16))
        PE.after((s_in[1], 16))
        for stage in stages:
            stage()
        join()

        sp = nc.sync

        def load(n, row, turns=0):
            src = wstream[bass.ds(row + turns * 6, 1), :, :].rearrange("a p n -> p (a n)")
            sp.dma_start(ring[:, n % RING, :], src).then_inc(s_load[n % RING], 16)

        n = 0
        waited = {}
        while n < len(ring_log):
            if n in ffn_at:
                base, row = ffn_at[n]
                for p in range(2):
                    for k in range(3):
                        if n + 3 * p + k >= RING:
                            sp.wait_ge(*ring_log[n + 3 * p + k - RING][1])
                        load(n + 3 * p + k, row + 3 * p + k)
                with nc.Fori(0, (NPAIR - 3) // 2, engines=(ENG.SP,)) as it:
                    for p in range(2):
                        for k in range(3):
                            sp.wait_ge(s_wl[k], it * 4 + (base + 2 * p + 2))
                            load(n + 3 * p + k, row + 6 + 3 * p + k, turns=it)
                p = NPAIR - 1
                for k in range(3):
                    sp.wait_ge(*ring_log[n + 3 * p + k - RING][1])
                    load(n + 3 * p + k, row + 3 * p + k)
                n += 3 * NPAIR
            else:
                if n >= RING:
                    sp.wait_ge(*ring_log[n - RING][1])
                load(n, ring_log[n][0])
                n += 1
        s_out = new_sem("s_out")
        for tok in final:
            if tok is not None:
                sp.wait_ge(*tok)
        sp.dma_start(out, X[:, :, 0:T]).then_inc(s_out, 16)
        sp.wait_ge(s_out, 16)


def _features(w):
    return w.reshape(w.shape[0] // P, P, w.shape[1]).transpose(1, 0, 2)


def _slots(dst, w, width):
    f = _features(w)
    for j in range(0, w.shape[1], width):
        part = f[:, :, j:j + width].reshape(P, -1)
        dst[j // width, :, 0:part.shape[1]] = part


def _ffn_slots(dst, wg, wu, wd):
    for p in range(NPAIR):
        cols = slice(p * 2 * P, (p + 1) * 2 * P)
        dst[3 * p] = _features(wg[:, cols]).reshape(P, -1)
        dst[3 * p + 1] = _features(wu[:, cols]).reshape(P, -1)
        dst[3 * p + 2] = _features(wd[cols, :]).reshape(P, -1)


def _pair_heads(n_rest):
    return np.concatenate([np.arange(h * 64, h * 64 + 64) for h in PAIRED] + [512 + np.arange(n_rest)])


def _alibi():
    q, k = np.arange(T)[:, None], np.arange(T)[None, :]
    inside = (k // CH <= q // CH) & (k // CH >= q // CH - 2)
    slopes = 2.0 ** (-8.0 * np.arange(1, HEADS + 1) / HEADS)
    b = np.where(inside[None], -slopes[:, None, None] * np.abs(q - k)[None], NEG)[PAIRED]
    return b.reshape(HEADS, 2, P, T).transpose(1, 2, 0, 3).reshape(2, P, HEADS * T).astype(np.float32)


def _neighbourhood(rpb):
    q, k = np.arange(T)[:, None], np.arange(T)[None, :]
    start = np.clip(q % 64 - 8, 0, 48)
    inside = (k % 64 >= start) & (k % 64 < start + 16)
    rows, cols = k // 64 - q // 64 + 7, np.where(inside, k % 64 - q % 64 + 15, 31)
    padded = np.concatenate([rpb, np.full(rpb.shape[:2] + (1,), NEG, rpb.dtype)], axis=2)
    b = padded[:, rows, cols]
    return b.reshape(HEADS, 2, P, T).transpose(1, 2, 0, 3).reshape(2, P, HEADS * T)


def _rope_tables(dim, copies):
    pos = np.arange(T)
    rows, cols = (pos // 64).astype(np.float32), (pos % 64).astype(np.float32)
    axis = dim // 2
    inv = (np.float32(10000.0) ** (-np.arange(0, axis, 2, dtype=np.float32) / np.float32(axis))).astype(np.float32)
    ang = np.concatenate([rows[:, None] * inv, cols[:, None] * inv], axis=-1)
    ang = np.tile(np.repeat(ang, 2, axis=1).T, (copies, 1))
    return np.cos(ang), np.sin(ang)


def _consts():
    c = np.zeros((P, N_CCOL), np.float32)

    def put(name, a):
        c[:, CCOL[name]:CCOL[name] + a.shape[1]] = a
    a, b = np.arange(P)[:, None], np.arange(P)[None, :]
    same = lambda n: a // n == b // n
    put("ident", np.eye(P))
    put("mean", np.full((P, P), 1.0 / D))
    put("ones", np.ones((P, P)))
    put("mean64", same(64) / 64.0)
    rot = np.zeros((P, P))
    even = np.arange(0, P, 2)
    rot[even + 1, even], rot[even, even + 1] = -1.0, 1.0
    put("rot", rot)
    for names, dim in ((("cosA", "sinA"), 64), (("cosM", "sinM"), ROPE)):
        for name, table in zip(names, _rope_tables(dim, P // dim)):
            put(name, table)
    put("after", same(CH) & (a > b))
    put("upto", same(CH) & (a <= b))
    put("before", same(CH) & (a < b))
    put("in16", same(16))
    put("in32", same(32) & ~same(16))
    put("in64", same(64) & ~same(32))
    return c


def _layout(x):
    w = np.zeros((N_ROWS, P, SLOT), np.float32)

    def rows(name):
        return w[ROW[name]:ROW[name] + dict(STREAM)[name]]
    for i in range(2):
        _ffn_slots(rows(f"ffn1_{i}"), x["ffn1_wg"][i], x["ffn1_wu"][i], x["ffn1_wd"][i])
        _ffn_slots(rows(f"ffn2_{i}"), x["ffn2_wg"][i], x["ffn2_wu"][i], x["ffn2_wd"][i])
        _slots(rows(f"ple_p_{i}"), x["ple_wp"][i], D)
        _slots(rows(f"ple_g_{i}"), x["ple_wg"][i], 2 * P)
        _slots(rows(f"ada_{i}"), x[f"l{i}_w_ada_2"], 2 * P)
        up = x[f"l{i}_w_up_2"]
        _ffn_slots(rows(f"l{i}_ffn"), up[:, 0:F], up[:, F:2 * F], x[f"l{i}_w_down_2"])
    _slots(rows("ab_in"), x["ab_w_in"][0][:, _pair_heads(1280)], 2 * P)
    rows("alibi")[:] = _alibi()
    _slots(rows("ab_out"), x["ab_w_out"][0][_pair_heads(512)], 2 * P)
    _slots(rows("c_in"), x["c_w_in"][0], 2 * P)
    _slots(rows("c_out"), x["c_w_out"][0], 2 * P)
    _slots(rows("l0_in"), x["l0_w_in_2"][:, _pair_heads(1792)], 2 * P)
    rows("rpb")[:] = _neighbourhood(x["l0_rpb_2"])
    _slots(rows("l0_out"), x["l0_w_out_2"][_pair_heads(512)], 2 * P)
    _slots(rows("l1_in")[0:4], x["l1_w_in_2"][:, 0:CQ + CKV], 2 * P)
    _slots(rows("l1_in")[4:5], x["l1_w_in_2"][:, CQ + CKV:], ROPE)
    uq = x["l1_w_uq_2"].reshape(CQ, MLA_H, NOPE + ROPE)
    _slots(rows("l1_uq")[0:4], uq[:, :, 0:NOPE].reshape(CQ, -1), 2 * P)
    _slots(rows("l1_uq")[4:6], uq[:, :, NOPE:].reshape(CQ, -1), 2 * P)
    ukv = x["l1_w_ukv_2"].reshape(CKV, MLA_H, 128)
    _slots(rows("l1_ukv")[0:1], ukv[:, :, 0:64].reshape(CKV, -1), D)
    _slots(rows("l1_ukv")[1:2], ukv[:, :, 64:].reshape(CKV, -1), D)
    _slots(rows("l1_out"), x["l1_w_out_2"], 2 * P)

    pv = np.zeros((P, N_PCOL), np.float32)

    def put(name, a):
        a = np.asarray(a).reshape(-1, P).T
        pv[:, PCOL[name]:PCOL[name] + a.shape[1]] = a
    for i in range(2):
        for k in range(3):
            put(f"ln_g{i}{k}", x["ln_g"][i, k])
            put(f"ln_b{i}{k}", x["ln_b"][i, k])
        put(f"ple_b{i}", x["ple_bg"][i])
        put(f"ada_b{i}", x[f"l{i}_b_ada_2"])
        for k in (1, 2):
            put(f"l{i}_ln{k}g", x[f"l{i}_ln{k}_g_2"])
            put(f"l{i}_ln{k}b", x[f"l{i}_ln{k}_b_2"])
        put(f"l{i}_cw", x[f"l{i}_conv_w_2"])
        put(f"l{i}_cb", x[f"l{i}_conv_b_2"])
    put("sink", np.repeat(x["a_sinks"][0][PAIRED], P))
    put("b_cw", x["b_conv_w"][0])
    put("b_cb", x["b_conv_b"][0])
    put("b_ba", x["b_ba"][0])
    put("b_bx", x["b_bx"][0])
    put("b_lam", x["b_lam"][0])
    put("c_cw", x["c_conv_w"][0])
    put("c_ng", x["c_norm_g"][0])
    pv[0:8, PCOL["c_alog"]] = x["c_a_log"][0]
    pv[0:8, PCOL["c_dt"]] = x["c_dt_bias"][0]
    both = np.stack([x["c_2"][0], x["c_ctx_2"]], axis=-1)
    pv[:, PCOL["cond"]:PCOL["cond"] + 16] = both.reshape(KC, P, 2).transpose(1, 0, 2).reshape(P, 16)
    put("q_gain", np.tile(x["l0_q_gain_2"], 2))
    put("k_gain", np.tile(x["l0_k_gain_2"], 2))
    put("cq_gain", x["l1_cq_gain_2"])
    put("ckv_gain", x["l1_ckv_gain_2"])

    gates = np.zeros((P, 8, P), np.float32)
    for which, name in enumerate(("b_wa", "b_wx")):
        for blk in range(8):
            r = slice(64 * (blk % 2), 64 * (blk % 2) + 64)
            gates[r, 4 * which + blk // 2, r] = x[name][0, blk]
    return dict(
        wstream=w, params=pv, consts=_consts(), xin=_features(x["x"][0].T), cin=_features(x["ctx_2"][0].T),
        pin=np.stack([_features(x["p"][i, 0].T) for i in range(2)], axis=1), wab=gates)


def kernel(**inputs):
    import concourse.bacc as bacc
    from concourse.bass_utils import run_bass_kernel_spmd

    arrays = {k: np.ascontiguousarray(v) for k, v in _layout({k: np.asarray(v) for k, v in inputs.items()}).items()}
    nc = bacc.Bacc("TRN2", target_bir_lowering=False, num_devices=1)
    args = [nc.dram_tensor(k, v.shape, F32, kind="ExternalInput").ap() for k, v in arrays.items()]
    out = nc.dram_tensor("out", [P, KC, T], F32, kind="ExternalOutput").ap()
    build_program(nc, *args, out)
    got = run_bass_kernel_spmd(nc, [arrays], core_ids=[0]).results[0]["out"]
    return got.transpose(2, 1, 0).reshape(1, T, D)
```
